# Optimizing a Trainium2 kernel written in Bass

```python
import math
import jax, jax.numpy as jnp
from jax import lax
import numpy as np

D_MODEL = 1024
BATCH = 1
SEQ = 512
DEPTH = 1

HEAD_DIM = 64
NSA_HEADS = 8
NSA_KV_HEADS = 2
NSA_GROUP = NSA_HEADS // NSA_KV_HEADS
SB_HEADS = 8
CMP_LEN = 32
CMP_STRIDE = 16
CMP_HIDDEN = 256
SEL_LEN = 64
SEL_TOPK = 4
WINDOW = 512
Q_BLOCK = 128
N_BUCKETS = 32
MAX_DISTANCE = 128
D_FF = 4 * D_MODEL
EPS = 1e-6
NEG = -1e30
FORCE_BONUS = 1e4

NSA_Q_W = NSA_HEADS * HEAD_DIM
NSA_KV_W = NSA_KV_HEADS * HEAD_DIM
SB_W = SB_HEADS * HEAD_DIM
SPLITS = (NSA_Q_W, 6 * NSA_KV_W, 3 * NSA_HEADS, 3 * SB_W, 2 * D_MODEL)
IN_COLS = sum(SPLITS)

kernel_name = 'hybrid_nsa_stickbreaking_block'

def rmsnorm(x, g):
    xf = x.astype(jnp.float32)
    y = xf * lax.rsqrt(jnp.mean(xf * xf, axis=-1, keepdims=True) + EPS)
    return y * g.astype(jnp.float32)

def t5_bucket(dist):
    n = jnp.maximum(dist, 0)
    max_exact = N_BUCKETS // 2
    nf = jnp.maximum(n, 1).astype(jnp.float32)
    large = max_exact + (jnp.log(nf / max_exact) / math.log(MAX_DISTANCE / max_exact)
                         * (N_BUCKETS - max_exact)).astype(jnp.int32)
    return jnp.where(n < max_exact, n, jnp.minimum(large, N_BUCKETS - 1))

def compress_blocks(kv, pe, w1, b1, w2):
    b, t, g, dh = kv.shape
    n_cmp = (t - CMP_LEN) // CMP_STRIDE + 1
    idx = np.arange(n_cmp)[:, None] * CMP_STRIDE + np.arange(CMP_LEN)[None, :]
    blocks = kv[:, idx] + pe[None, None, :, None, :]
    flat = blocks.transpose(0, 1, 3, 2, 4).reshape(b, n_cmp, g, CMP_LEN * dh)
    hid = jax.nn.gelu(flat @ w1 + b1)
    return hid @ w2

def nsa_attention(q, kv, gate_logits, rel_bias, cmp_k, cmp_v):
    b, t = q.shape[:2]
    g, hg, dh = NSA_KV_HEADS, NSA_GROUP, HEAD_DIM
    scale = dh ** -0.5
    qg = q.reshape(b, t, g, hg, dh)
    k_c, v_c, k_s, v_s, k_w, v_w = (kv[:, :, i] for i in range(6))
    tbl = rel_bias.reshape(N_BUCKETS, g, hg)
    pos = jnp.arange(t)

    kc = compress_blocks(k_c, *cmp_k)
    vc = compress_blocks(v_c, *cmp_v)
    n_cmp = kc.shape[1]
    c_start = np.arange(n_cmp) * CMP_STRIDE
    dist_c = pos[:, None] - jnp.asarray(c_start + CMP_LEN - 1)[None, :]
    valid_c = dist_c >= 0
    bias_c = jnp.moveaxis(tbl[t5_bucket(dist_c)], (2, 3), (0, 1))
    s_c = (jnp.einsum('btgjd,bcgd->bgjtc', qg, kc) * scale + bias_c).astype(jnp.float32)
    p_c = jax.nn.softmax(jnp.where(valid_c, s_c, NEG), axis=-1) * valid_c
    o_cmp = jnp.einsum('bgjtc,bcgd->btgjd', p_c, vc)

    n_sel = t // SEL_LEN
    s_start = np.arange(n_sel) * SEL_LEN
    overlap = ((c_start[:, None] < s_start[None, :] + SEL_LEN)
               & (c_start[:, None] + CMP_LEN > s_start[None, :])).astype(np.float32)
    imp = jnp.einsum('bgjtc,cn->bgtn', p_c, jnp.asarray(overlap))
    blk = jnp.arange(n_sel)[None, :]
    sel_ok = jnp.asarray(s_start)[None, :] <= pos[:, None]
    forced = (blk == (pos // SEL_LEN)[:, None]) | (blk == 0)
    score = jnp.where(forced, imp + FORCE_BONUS, jnp.where(sel_ok, imp, -FORCE_BONUS))
    _, sel_idx = lax.top_k(score, SEL_TOPK)

    ks_blk = k_s.reshape(b, n_sel, SEL_LEN, g, dh).transpose(0, 3, 1, 2, 4)
    vs_blk = v_s.reshape(b, n_sel, SEL_LEN, g, dh).transpose(0, 3, 1, 2, 4)
    gather = jax.vmap(jax.vmap(lambda arr, i: arr[i]))
    kw_pad = jnp.pad(k_w, ((0, 0), (WINDOW, 0), (0, 0), (0, 0)))
    vw_pad = jnp.pad(v_w, ((0, 0), (WINDOW, 0), (0, 0), (0, 0)))
    g_idx = jnp.arange(g)[None, :, None, None, None]
    offs = jnp.arange(SEL_LEN)

    def block(s0):
        tq = s0 + jnp.arange(Q_BLOCK)
        qb = lax.dynamic_slice_in_dim(qg, s0, Q_BLOCK, axis=1)
        ib = lax.dynamic_slice_in_dim(sel_idx, s0, Q_BLOCK, axis=2)
        kb = gather(ks_blk, ib)
        vb = gather(vs_blk, ib)
        kpos = ib[..., None] * SEL_LEN + offs
        dist_s = tq[:, None, None] - kpos
        valid_s = (dist_s >= 0)[:, :, None]
        bias_s = jnp.moveaxis(tbl[t5_bucket(dist_s), g_idx], -1, 2)
        s_s = (jnp.einsum('bqgjd,bgqkld->bgjqkl', qb, kb) * scale + bias_s).astype(jnp.float32)
        s_s = jnp.where(valid_s, s_s, NEG).reshape(b, g, hg, Q_BLOCK, SEL_TOPK * SEL_LEN)
        p_s = jax.nn.softmax(s_s, axis=-1)
        o_s = jnp.einsum('bgjqn,bgqnd->bqgjd', p_s,
                         vb.reshape(b, g, Q_BLOCK, SEL_TOPK * SEL_LEN, dh))
        kwb = lax.dynamic_slice_in_dim(kw_pad, s0, WINDOW + Q_BLOCK, axis=1)
        vwb = lax.dynamic_slice_in_dim(vw_pad, s0, WINDOW + Q_BLOCK, axis=1)
        kpos_w = s0 - WINDOW + jnp.arange(WINDOW + Q_BLOCK)
        dist_w = tq[:, None] - kpos_w[None, :]
        valid_w = (dist_w >= 0) & (dist_w < WINDOW) & (kpos_w >= 0)[None, :]
        bias_w = jnp.moveaxis(tbl[t5_bucket(dist_w)], (2, 3), (0, 1))
        s_w = (jnp.einsum('bqgjd,bkgd->bgjqk', qb, kwb) * scale + bias_w).astype(jnp.float32)
        p_w = jax.nn.softmax(jnp.where(valid_w, s_w, NEG), axis=-1)
        o_w = jnp.einsum('bgjqk,bkgd->bqgjd', p_w, vwb)
        return o_s, o_w

    o_sel, o_win = lax.map(block, jnp.arange(t // Q_BLOCK) * Q_BLOCK)
    o_sel = jnp.moveaxis(o_sel, 0, 1).reshape(b, t, g, hg, dh)
    o_win = jnp.moveaxis(o_win, 0, 1).reshape(b, t, g, hg, dh)
    gts = jax.nn.sigmoid(gate_logits).reshape(b, t, g, hg, 3)
    o = gts[..., 0:1] * o_cmp + gts[..., 1:2] * o_sel + gts[..., 2:3] * o_win
    return o.reshape(b, t, NSA_HEADS * dh)

def stick_breaking_attention(q, k, v):
    b, t, h, dh = q.shape
    scale = dh ** -0.5
    kpos = jnp.arange(t)

    def block(s0):
        qb = lax.dynamic_slice_in_dim(q, s0, Q_BLOCK, axis=1)
        z = jnp.einsum('bqhd,bkhd->bhqk', qb, k).astype(jnp.float32) * scale
        tq = s0 + jnp.arange(Q_BLOCK)
        causal = kpos[None, :] < tq[:, None]
        log_beta = jax.nn.log_sigmoid(z)
        log_keep = jnp.where(causal, log_beta - z, 0.0)
        later = lax.cumsum(log_keep, axis=3, reverse=True) - log_keep
        a = jnp.where(causal, jnp.exp(log_beta + later), 0.0)
        return jnp.einsum('bhqk,bkhd->bqhd', a, v)

    o = lax.map(block, jnp.arange(t // Q_BLOCK) * Q_BLOCK)
    return jnp.moveaxis(o, 0, 1).reshape(b, t, h * dh)

def setup_inputs(seed: int = 0) -> dict:
    key = jax.random.key(seed)
    ks = jax.random.split(key, 20)

    def nrm(k, shape, scale):
        return jax.random.normal(k, shape, jnp.float32) * scale

    flat_in = CMP_LEN * HEAD_DIM
    return {
        'x': nrm(ks[0], (BATCH, SEQ, D_MODEL), 1.0),
        'norm_attn': 1.0 + nrm(ks[1], (DEPTH, D_MODEL), 0.1),
        'w_in': nrm(ks[2], (DEPTH, D_MODEL, IN_COLS), D_MODEL ** -0.5),
        'rel_bias': nrm(ks[3], (N_BUCKETS, NSA_HEADS), 0.5),
        'cmp_k_pe': nrm(ks[4], (DEPTH, CMP_LEN, HEAD_DIM), 0.1),
        'cmp_k_w1': nrm(ks[5], (DEPTH, flat_in, CMP_HIDDEN), flat_in ** -0.5),
        'cmp_k_b1': nrm(ks[6], (DEPTH, CMP_HIDDEN), 0.02),
        'cmp_k_w2': nrm(ks[7], (DEPTH, CMP_HIDDEN, HEAD_DIM), CMP_HIDDEN ** -0.5),
        'cmp_v_pe': nrm(ks[8], (DEPTH, CMP_LEN, HEAD_DIM), 0.1),
        'cmp_v_w1': nrm(ks[9], (DEPTH, flat_in, CMP_HIDDEN), flat_in ** -0.5),
        'cmp_v_b1': nrm(ks[10], (DEPTH, CMP_HIDDEN), 0.02),
        'cmp_v_w2': nrm(ks[11], (DEPTH, CMP_HIDDEN, HEAD_DIM), CMP_HIDDEN ** -0.5),
        'w_up_nsa': nrm(ks[12], (DEPTH, NSA_Q_W, D_MODEL), NSA_Q_W ** -0.5),
        'w_up_sb': nrm(ks[13], (DEPTH, SB_W, D_MODEL), SB_W ** -0.5),
        'w_out': nrm(ks[14], (DEPTH, D_MODEL, D_MODEL), D_MODEL ** -0.5),
        'norm_mlp': 1.0 + nrm(ks[15], (DEPTH, D_MODEL), 0.1),
        'w_ff1': nrm(ks[16], (DEPTH, D_MODEL, D_FF), D_MODEL ** -0.5),
        'w_ff2': nrm(ks[17], (DEPTH, D_FF, D_MODEL), D_FF ** -0.5),
        'norm_final': 1.0 + nrm(ks[18], (D_MODEL,), 0.1),
    }

def reference(x, norm_attn, w_in, rel_bias, cmp_k_pe, cmp_k_w1, cmp_k_b1, cmp_k_w2,
              cmp_v_pe, cmp_v_w1, cmp_v_b1, cmp_v_w2, w_up_nsa, w_up_sb, w_out,
              norm_mlp, w_ff1, w_ff2, norm_final):
    b, t, _ = x.shape
    split_at = np.cumsum(SPLITS)[:-1].tolist()
    for layer in range(DEPTH):
        h = rmsnorm(x, norm_attn[layer])
        proj = h @ w_in[layer]
        q_n, kv_n, g_n, qkv_s, g_m = jnp.split(proj, split_at, axis=-1)
        o_nsa = nsa_attention(
            q_n.reshape(b, t, NSA_HEADS, HEAD_DIM),
            kv_n.reshape(b, t, 6, NSA_KV_HEADS, HEAD_DIM),
            g_n.reshape(b, t, NSA_HEADS, 3),
            rel_bias,
            (cmp_k_pe[layer], cmp_k_w1[layer], cmp_k_b1[layer], cmp_k_w2[layer]),
            (cmp_v_pe[layer], cmp_v_w1[layer], cmp_v_b1[layer], cmp_v_w2[layer]))
        qkv = qkv_s.reshape(b, t, 3, SB_HEADS, HEAD_DIM)
        o_sb = stick_breaking_attention(qkv[:, :, 0], qkv[:, :, 1], qkv[:, :, 2])
        merge = jax.nn.sigmoid(g_m.reshape(b, t, 2, D_MODEL))
        mixed = merge[:, :, 0] * (o_nsa @ w_up_nsa[layer]) + merge[:, :, 1] * (o_sb @ w_up_sb[layer])
        x = x + mixed @ w_out[layer]
        h = rmsnorm(x, norm_mlp[layer])
        x = x + jnp.square(jax.nn.relu(h @ w_ff1[layer])) @ w_ff2[layer]
    return rmsnorm(x, norm_final)


_drawn_inputs = setup_inputs


def setup_inputs(seed=0):
    import zlib

    import numpy as np

    out = dict(_drawn_inputs(seed))
    spreads = {}
    factors = {'cmp_k_pe': 24.838, 'cmp_k_b1': 64.0, 'cmp_v_pe': 3.828, 'cmp_v_b1': 8.0}
    for name, (base, spread) in spreads.items():
        noise = np.random.default_rng([zlib.crc32(name.encode()), seed]).standard_normal(out[name].shape)
        drawn = base * np.exp(spread * noise) if base else spread * noise
        out[name] = __import__('jax').numpy.asarray(drawn.astype(out[name].dtype))
    for name, factor in factors.items():
        out[name] = (out[name] * factor).astype(out[name].dtype)
    return out
```

```python
import math
from contextlib import ExitStack

import numpy as np

import concourse.bass as bass
from concourse import mybir

F32 = mybir.dt.float32
F32R = mybir.dt.float32r
BF16 = mybir.dt.bfloat16
U32 = mybir.dt.uint32
ALU = mybir.AluOpType
ACT = mybir.ActivationFunctionType
AX = mybir.AxisListType

P = 128
T = 512
D = 1024
KT = D // P
RT = T // P
DH = 64
H = 8
G = 2
HG = H // G
PAIRS = 4
CL, CS = 32, 16
NC = (T - CL) // CS + 1
CM = 256
CI = CL * DH // P
NB = T // 64
TOPK = 4
BUCKETS = 32
FT = 4 * D // P
QF = 4
EPS = 1e-6
BIG = 1e30
FORCE = 1e4

P_CK, P_CV, P_V, P_KS, P_KW, P_QN = 0, 1, 2, 4, 5, 6
P_SV, P_SQK, P_GM = 10, 14, 22
P_UP = P_GM + 16
P_OUT = P_UP + 8
P_FF = P_OUT + 8
FF_ORDER = [(1, 0), (1, 1), (2, 0), (1, 2), (2, 1), (1, 3), (2, 2), (2, 3)]
NPANEL = P_FF + 8 * len(FF_ORDER)
RING = 4

GM_IN_ATT = 12
GM_SB = 4
UNITS = PAIRS * 2 * G * RT
CH_SB = GM_SB * 24 // H
CH_NS = (GM_IN_ATT - GM_SB) * 24 // UNITS


def bank_plan():
    order = [("vec0", 6), ("vec1", 7), (("pan", 0), 0), (("pan", 1), 1), ("rms", 5), ("rcol", 4),
             ("dt", 6), (("v", 0), 2), (("v", 1), 3), ("gn", 7), (("pan", 4), 0), (("pan", 5), 1),
             (("hid", 0), 5), (("pan", 6), 0), (("hid", 1), 6), (("pan", 7), 1), ("hidT", 4),
             (("pan", 8), 0), ("kcvc", 7), (("pan", 9), 1)]
    sv = [(("sv", i), 2 + i % 2) for i in range(4)]
    cs = [[(("cs", r, g), 4 + g) for g in range(G)] for r in range(RT)]
    ct = [(("ct", r), 6 + r % 2) for r in range(RT)]
    order += [sv[0], sv[1], *cs[0], sv[2], sv[3], *cs[1]]
    for i in range(8):
        order.append((("pan", P_SQK + i), i % 2))
        if i in (0, 2, 4, 6):
            order.append(ct[i // 2])
        if i in (1, 3):
            order += cs[2 + i // 2]
    order += [(("z", h, i), 3 * (h % 2) + i) for h in range(H) for i in range(3)]
    order += [(("osb", p), 6) for p in range(PAIRS)]
    order += [(("gm", i), 7) for i in range(GM_IN_ATT)]
    order += [(("s", u), u % 3) for u in range(UNITS)]
    order += [(("t", u), 3 + u % 2) for u in range(UNITS)]
    order += [(("ons", p), 5) for p in range(PAIRS)]
    order += [(("gm", i), 7) for i in range(GM_IN_ATT, 16)]
    for n in range(KT):
        order += [(("up0", n), 2 * (n % 2)), (("up1", n), 2 * (n % 2) + 1)]
    order += [(("out", n), 4 + n % 2) for n in range(KT)]
    order += [("rms2", 6)]
    for s, (which, q) in enumerate(FF_ORDER):
        order += [(("ff", s, n), n % 4 if which == 1 else 4 + n % 2) for n in range(8)]
    order += [("rms3", 7)]
    seen, use = {}, {}
    for name, b in order:
        assert name not in use, name
        use[name] = (b, seen.get(b, 0))
        seen[b] = seen.get(b, 0) + 1
    return use


USE = bank_plan()


def panel_product(p):
    if P_V <= p < P_V + 2:
        return "v", 1
    if P_SV <= p < P_SV + 4:
        return "sv", (p - P_SV) // 2 * 2 + 1
    if p < P_GM:
        return "pan", p
    if p < P_UP:
        return "gm", p - P_GM
    if p < P_OUT:
        return "up1", p - P_UP
    if p < P_FF:
        return "out", p - P_OUT
    return "ff", (p - P_FF) // 8, (p - P_FF) % 8


def unit(u):
    run, r = divmod(u, RT)
    p, bg = divmod(run, 2 * G)
    return p, bg // G, bg % G, r, run


def block_kernel(nc, xT, panels, w_gn, norms, rel_bias, pe, w1, b1, w2, onehot, cst, outT):
    with ExitStack() as ctx:
        top = [nc.sbuf_base + (-nc.sbuf_base) % 64]
        fence = ctx.enter_context(nc.sbuf_tensor("arena", [P, (nc.sbuf_usable_end - top[0] - 256) // 4], F32))
        limit = nc.sbuf_usable_end

        def place(name, shape, dt=F32, at=None):
            size = int(np.prod(shape[1:])) * (2 if dt == BF16 else 4)
            size += (-size) % 64
            start = top[0] if at is None else at
            if at is None:
                top[0] += size
            assert start + size <= limit, (name, start + size - limit)
            return nc.alloc_sbuf_tensor_at(name, shape, dt, offset=start)

        def sem(name):
            return ctx.enter_context(nc.semaphore(name))

        wraw = [place(f"wraw{i}", [P, 8, P]) for i in range(RING)]
        whi = place("whi", [P, RING, 8, P], F32R)
        wlo = place("wlo", [P, RING, 8, P], F32R)
        rstd_b = place("rstd_b", [P, T])
        tmp = place("tmp", [P, 2, T])
        ones = place("ones", [P, P])
        nrm = place("nrm", [P, 3, KT])
        epsc = place("epsc", [P, 1])
        onec = place("onec", [P, 1])
        after_kept = top[0]
        hh = place("hh", [P, KT, T], F32R)
        hl = place("hl", [P, KT, T], F32R)
        at_q = top[0]
        qn_h = place("qn_h", [P, PAIRS, T], F32R)
        qn_l = place("qn_l", [P, PAIRS, T], F32R)
        kn_h = place("kn_h", [P, 2, T], F32R)
        kn_l = place("kn_l", [P, 2, T], F32R)
        at_sbq = top[0]
        sq_h = place("sq_h", [P, PAIRS, T], F32R)
        sq_l = place("sq_l", [P, PAIRS, T], F32R)
        at_sbk = top[0]
        sk_h = place("sk_h", [P, PAIRS, T], F32R)
        sk_l = place("sk_l", [P, PAIRS, T], F32R)
        at_sbv = top[0]
        sv = place("sv", [P, RT, H * DH])
        nv = place("nv", [P, RT, 2, P])
        at_g = top[0]
        hank = place("hank", [P, H, T])
        at_gm = top[0]
        gm = place("gm", [P, GM_IN_ATT, T])
        small = top[0]
        ident = place("ident", [P, P])
        tables = place("tables", [P, 2 * NB + 1 + NB])
        scoreadd = tables[:, 0:2 * NB].rearrange("p (r n) -> p r n", r=2)
        rowvalid = tables[:, 2 * NB:2 * NB + 1]
        iota8 = tables[:, 2 * NB + 1:]
        negtri = place("negtri", [P, P], F32R)
        negones = place("negones", [P, P], F32R)
        ident_bf = place("ident_bf", [P, P], BF16)
        diag_bf = place("diag_bf", [P, P], BF16)
        blk_bf = place("blk_bf", [2 * NB, G, T], BF16)
        rcol = place("rcol", [P, RT])
        gate = place("gate", [P, RT, H, 3])
        dmat = place("dmat", [P, H, 56])
        kc_h = place("kc_h", [P, 32], F32R)
        kc_l = place("kc_l", [P, 32], F32R)
        vc = place("vc", [P, G, DH])
        maskT = place("maskT", [2 * NB, 2, P], BF16)
        nmin = place("nmin", [P, 4])
        rsum = place("rsum", [P, 4])
        rec = place("rec", [P, 4])
        at_pct = top[0]
        pct = place("pct", [P, G, T])
        ckv = place("ckv", [P, 2, T], at=at_pct)
        xs = place("xs", [P, KT, T], at=at_gm)
        x2 = [place(f"x2{i}", [P, G, T], at=at_gm + 4096 * i) for i in range(2)]
        bm = [place(f"bm{i}", [P, CI, G * NC], at=at_gm + 8192 + 4096 * i) for i in range(2)]
        oneh = place("oneh", [BUCKETS + 1, 2 * T], at=at_gm + 16384)
        vec = place("vec", [H, 2 * T], at=at_gm + 20480)
        hid = place("hid", [G * NC, 2, CM], at=at_gm + 16384)
        hidTk = place("hidTk", [P, 2, G, 32], at=at_gm + 18432)
        hidTv = place("hidTv", [P, 2, G, 4, 32], at=at_gm + 18944)
        kc32 = place("kc32", [P, 32], at=at_gm + 20992)
        c_t = place("c_t", [P, H, NC], at=at_gm + 8192)
        c_p = place("c_p", [P, 2, H, 32], at=at_gm + 9216)
        c_g = place("c_g", [P, 2, H, 32], at=at_gm + 11264)
        c_m = place("c_m", [P, 4, H], at=at_gm + 13312)
        c_s = place("c_s", [P, G, 40], at=at_gm + 13440)
        c_i = place("c_i", [P, G, NB], at=at_gm + 13760)
        c_8 = place("c_8", [P, G, NB], at=at_gm + 13824)
        c_x = place("c_x", [P, G, NB], U32, at=at_gm + 13888)
        c_f = place("c_f", [P, G, NB], at=at_gm + 13952)
        c_e = place("c_e", [P, G, NB, TOPK], at=at_gm + 14016)
        c_k = place("c_k", [P, G, NB], at=at_gm + 14272)
        w1s = [place("w1k", [P, CI, CM], at=at_g), place("w1v", [P, CI, CM], at=at_sbk)]
        sqt = place("sqt", [P, 2, T], at=at_sbq)
        sqs = place("sqs", [P, T], at=at_sbq + 4096)
        dts = place("dts", [55, H, P], at=at_sbq + 6144)
        relx = place("relx", [BUCKETS + 1, H], at=at_sbq + 10240)
        pes = place("pes", [P, 2, CI], at=at_sbq + 10304)
        b1s = place("b1s", [1, 2, CM], at=at_sbq + 10496)
        w2k = place("w2k", [P, 2, 2, DH], at=at_sbq + 12544)
        w2v = place("w2v", [P, 2, DH], at=at_sbq + 13568)
        cstb = place("cstb", [P, 2 * P + 2 * T], at=at_sbv)
        gns = place("gns", [P, KT, 3 * H], at=at_sbv + 5632)
        gn_h = place("gn_h", [P, KT, 3 * H], F32R, at=at_sbv + 6400)
        gn_l = place("gn_l", [P, KT, 3 * H], F32R, at=at_sbv + 7168)
        KOFF = [0, T, 2 * T, T + 3 * P]
        KLEN = [T - P * k for k in range(RT)]
        SBW = 2 * T + 2 * P
        behind_gm = at_gm + 2048 * GM_SB
        ew = [place(f"ew{i}", [P, SBW], at=at_g + 5120 * i) for i in range(2)]
        sp_h = [place(f"sp_h{i}", [P, SBW], F32R, at=(at_g + 10240, behind_gm)[i]) for i in range(2)]
        sp_l = [place(f"sp_l{i}", [P, SBW], F32R, at=behind_gm + 5120 * (i + 1)) for i in range(2)]
        ns = [place(f"ns{i}", [P, T], at=at_sbk + 2048 * i) for i in range(4)]
        pt = [place(f"pt{i}", [P, RT, T], at=at_sbk + 8192 + 8192 * i) for i in range(2)]
        gm2 = place("gm2", [P, 16 - GM_IN_ATT, T], at=at_g)
        mx = [place(f"mx{i}", [P, T], at=at_sbk + 16384 + 2048 * i) for i in range(4)]
        x_res = place("x_res", [P, KT, T], at=at_sbk)
        h2h = place("h2h", [P, KT, T], F32R, at=at_q)
        h2l = place("h2l", [P, KT, T], F32R, at=at_q + 16384)
        r_h = [place(f"r_h{i}", [P, 8, T], F32R, at=at_sbv + 32768 * i) for i in range(2)]
        r_l = [place(f"r_l{i}", [P, 8, T], F32R, at=at_sbv + 16384 + 32768 * i) for i in range(2)]
        fin_sq = place("fin_sq", [P, 2, T], at=after_kept)
        fin_ss = place("fin_ss", [P, T], at=after_kept + 4096)

        bank = [ctx.enter_context(nc.psum_tensor(f"bank{i}", [P, T], F32)) for i in range(8)]
        full = [sem(f"bank{i}_full") for i in range(8)]
        free = [sem(f"bank{i}_free") for i in range(8)]

        def claim(eng, name):
            b, n = USE[name]
            if n:
                eng.wait_ge(free[b], n)
            return bank[b]

        def filled(ins, name):
            ins.then_inc(full[USE[name][0]], 1)

        def result(eng, name):
            b, n = USE[name]
            eng.wait_ge(full[b], n + 1)
            return bank[b]

        def emptied(ins, name):
            ins.then_inc(free[USE[name][0]], 1)

        def stored(eng, name):
            b, n = USE[name]
            eng.wait_ge(free[b], n + 1)

        x_in = [sem(f"x_in{i}") for i in range(4)]
        small_in, cst_in, gn_in, cmp_in = sem("norms_in"), sem("constants_in"), sem("gate_weights_in"), sem("cmp_weights_in")
        vec_out, dt_in, x2_in = sem("bias_out"), sem("bias_rows_in"), [sem("cmp_k_tokens_in"), sem("cmp_v_tokens_in")]
        hank_in, xres_in, out_sem = sem("bias_in"), sem("residual_in"), sem("out_written")
        w_in = [sem(f"panel_in{i}") for i in range(RING)]
        w_hi, w_lo = sem("panel_hi"), sem("panel_lo")
        set_done, cast_done = sem("memsets"), sem("const_casts")
        h_hi, h_lo, sq_done, sqs_done = sem("h_hi"), sem("h_lo"), sem("sq_done"), sem("sqsum_done")
        rst, gn_split, gate_st = sem("rstd_ready"), sem("gate_weights_split"), sem("branch_gate_steps")
        t_hi, t_lo = sem("tmp_hi"), sem("tmp_lo")
        bm_done, kc_cp, kc_split = sem("block_matrices"), sem("kc_copied"), sem("kc_split")
        c_min, c_sub, c_exp, c_pready, c_link = sem("cmp_min"), sem("cmp_less_min"), sem("cmp_exp"), sem("cmp_probs"), sem("cmp_links")
        zc, ze, zl, zs = sem("z_clamped"), sem("z_exp"), sem("z_log"), sem("softplus")
        zh, zlo, c_acc, pv_sb = sem("softplus_hi"), sem("softplus_lo"), sem("stick_sums"), sem("stick_pv_first_half")
        o_hi = sem("mixer_out_hi")
        s_exp, s_rec, s_nrm, s_pv = sem("scores_exp"), sem("sum_reciprocal"), sem("probs_ready"), sem("sparse_pv")
        sig_done, mxs, m_hi, m_lo = sem("gates"), sem("mixed"), sem("mixed_hi"), sem("mixed_lo")
        x_sq, x_ss, h2hi, h2lo, rs2 = sem("x_squared"), sem("x_sqsum"), sem("h2_hi"), sem("h2_lo"), sem("rstd2_ready")
        r_pos, r_sc, r_hi, r_lo = sem("relu"), sem("relu_squared"), sem("r_hi"), sem("r_lo")
        y_sq, y_ss, rs3, y_fin = sem("y_squared"), sem("y_sqsum"), sem("rstd3_ready"), sem("y_final")

        vf = nc.dram_tensor("bias_by_distance", [H, 2 * T], F32, kind="Internal").ap()

        def gate_tile(i):
            return gm[:, i, :] if i < GM_IN_ATT else gm2[:, i - GM_IN_ATT, :]

        SB_A = [(0, 0, T), (1, T, 2 * T), (2, 2 * T, SBW)]

        def stick_pv_done(eng, h):
            if h % 2:
                result(eng, ("osb", h // 2))
            else:
                eng.wait_ge(pv_sb, h // 2 + 1)

        def sparse_pv_done(eng, run):
            p, bg = divmod(run, 2 * G)
            if bg == 2 * G - 1:
                result(eng, ("ons", p))
            else:
                eng.wait_ge(s_pv, (2 * G - 1) * p + bg + 1)

        block = ctx.enter_context(nc.Block())

        @block.sync
        def _(sp):
            def panel(p):
                if p >= RING:
                    sp.wait_ge(w_lo, p - RING + 1)
                sp.dma_start(wraw[p % RING][:], panels[p].rearrange("p (k m) -> p k m", k=8)).then_inc(w_in[p % RING], 16)

            for i in range(4):
                sp.dma_start(xs[:, 2 * i:2 * i + 2, :], xT[:, 2 * i:2 * i + 2, :]).then_inc(x_in[i], 16)
            for p in range(RING):
                panel(p)
            for i in range(2):
                sp.dma_start(w1s[i][:], w1[i]).then_inc(cmp_in, 16)
            for p in range(RING, NPANEL):
                panel(p)
                if p == P_GM + GM_SB + 3:
                    stick_pv_done(sp, H - 1)
                    sp.dma_start(hank[:], bass.AP(vf.tensor, 3 * P, [[1, P], [2 * T, H], [1, T]])).then_inc(hank_in, 16)
                if p == P_UP + 2:
                    sparse_pv_done(sp, 4 * PAIRS - 1)
                    sp.dma_start(x_res[:], xT).then_inc(xres_in, 16)
            for n in range(KT):
                sp.wait_ge(y_fin, n + 1)
                sp.dma_start(outT[:, n, :], x_res[:, n, :]).then_inc(out_sem, 16)
            sp.wait_ge(out_sem, 16 * KT)

        @block.gpsimd
        def _(pool):
            for p in range(NPANEL):
                s = p % RING
                pool.wait_ge(w_hi, p + 1)
                nc.gpsimd.tensor_tensor(wlo[:, s], wraw[s][:], whi[:, s].bitcast(F32), ALU.subtract).then_inc(w_lo, 1)

        @block.scalar
        def _(act):
            A = nc.scalar.activation
            act.dma_start(nrm[:], norms).then_inc(small_in, 16)
            act.dma_start(relx[0:BUCKETS, :], rel_bias).then_inc(cst_in, 16)
            act.dma_start(oneh[:], onehot).then_inc(cst_in, 16)
            act.dma_start(cstb[:], cst[:, 0:2 * P + 2 * T]).then_inc(cst_in, 16)
            act.dma_start(ident[:], cst[:, 2 * P + 2 * T:3 * P + 2 * T]).then_inc(cst_in, 16)
            act.dma_start(tables[:], cst[:, 3 * P + 2 * T:]).then_inc(cst_in, 16)
            act.dma_start(gns[:], w_gn).then_inc(gn_in, 16)
            act.dma_start(pes[:], pe).then_inc(cmp_in, 16)
            act.dma_start(b1s[:], b1).then_inc(cmp_in, 16)
            act.dma_start(w2k[:, :, 0, :], w2[0]).then_inc(cmp_in, 16)
            act.dma_start(w2k[:, :, 1, :], w2[0]).then_inc(cmp_in, 16)
            act.dma_start(w2v[:], w2[1]).then_inc(cmp_in, 16)

            def split(p):
                s = p % RING
                act.wait_ge(w_in[s], 16 * (p // RING + 1))
                if p >= RING:
                    result(act, panel_product(p - RING))
                A(whi[:, s], wraw[s][:], ACT.Copy).then_inc(w_hi, 1)

            act.wait_ge(small_in, 16)
            for k in range(KT):
                act.wait_ge(x_in[k // 2], 16)
                A(hh[:, k], xs[:, k], ACT.Copy, scale=nrm[:, 0, k:k + 1]).then_inc(h_hi, 1)
                if k >= 2:
                    act.wait_ge(sqs_done, k - 1)
                A(sqt[:, k % 2], xs[:, k], ACT.Square).then_inc(sq_done, 1)
                if k in (2, 4, 6):
                    split(k // 2 - 1)
            stored(act, "vec0")
            stored(act, "vec1")
            act.dma_start(vf, vec[:]).then_inc(vec_out, 16)
            act.wait_ge(vec_out, 16)
            act.dma_start(dts[:], bass.AP(vf.tensor, 0, [[16, 55], [2 * T, H], [1, P]])).then_inc(dt_in, 16)
            ps = result(act, "rms")
            act.wait_ge(set_done, 4)
            emptied(A(rstd_b[:], ps[:], ACT.Ln, bias=epsc[:], scale=1.0 / D), "rms")
            stored(act, "rms")
            A(rstd_b[:], rstd_b[:], ACT.Exp, scale=-0.5).then_inc(rst, 1)
            act.wait_ge(gn_in, 16)
            A(gn_h[:], gns[:], ACT.Copy).then_inc(gn_split, 1)
            split(3)

            nt = [0]

            def round_tmp(p, dst):
                stored(act, ("pan", p))
                A(dst, tmp[:, nt[0] % 2], ACT.Copy).then_inc(t_hi, 1)
                nt[0] += 1

            def cmp_exp(r):
                act.wait_ge(c_sub, r + 1)
                A(c_p[:, r % 2, :, 0:NC], c_t[:], ACT.Exp, scale=-1.0).then_inc(c_exp, 1)

            for i in range(2):
                split(4 + i)
                stored(act, ("pan", i))
                for g in range(G):
                    src = ckv[64 * g:64 * g + 64, i, :]
                    act.dma_start(x2[i][0:64, g, :], src).then_inc(x2_in[i], 16)
                    act.dma_start(x2[i][64:128, g, 0:T - 1], src[:, 1:T]).then_inc(x2_in[i], 16)
            stored(act, "gn")
            A(gate[:], gate[:], ACT.Exp, scale=-1.0).then_inc(gate_st, 1)
            split(6)
            split(7)
            split(8)
            round_tmp(P_KS, kn_h[:, 1])
            split(9)
            round_tmp(P_KW, kn_h[:, 0])
            for j in range(PAIRS):
                split(P_QN + j + RING)
                round_tmp(P_QN + j, qn_h[:, j])
                if j in (0, 1):
                    ps = result(act, ("hid", j))
                    emptied(A(hid[:, j], ps[0:G * NC, 0:CM], ACT.Gelu_apprx_tanh), ("hid", j))
            act.wait_ge(kc_cp, 2)
            A(kc_h[:], kc32[:], ACT.Copy).then_inc(kc_split, 1)
            split(14)
            split(15)
            cmp_exp(0)
            split(16)
            split(17)
            cmp_exp(1)
            for i in range(8):
                p, qk = divmod(i, 2)
                split(P_SQK + i + RING)
                round_tmp(P_SQK + i, (sk_h if qk else sq_h)[:, p])
                if i in (1, 3):
                    cmp_exp(2 + i // 2)

            def stick_weights(h):
                act.wait_ge(c_acc, h + 1)
                act.wait_ge(zlo, h + 1)
                for i, lo, hi in SB_A:
                    emptied(A(ew[h % 2][:, lo:hi], bank[3 * (h % 2) + i][:, 0:hi - lo], ACT.Exp), ("z", h, i))

            def stick_out_high(p):
                A(sq_h[:, p], result(act, ("osb", p))[:], ACT.Copy).then_inc(o_hi, 1)

            for h in range(H):
                w = ew[h % 2]
                if h % 2 == 1 and h >= 3:
                    stick_out_high((h - 3) // 2)
                act.wait_ge(zc, 3 * h + 3)
                A(w[:], w[:], ACT.Exp).then_inc(ze, 1)
                act.wait_ge(ze, h + 1)
                A(w[:], w[:], ACT.Ln, bias=onec[:], scale=1.0).then_inc(zl, 1)
                if h:
                    stick_weights(h - 1)
                act.wait_ge(zs, 3 * h + 3)
                A(sp_h[h % 2][:], w[:], ACT.Copy).then_inc(zh, 1)
                if h % 2 == 1:
                    split(P_GM + h // 2 + RING)
            stick_weights(H - 1)
            stick_out_high(PAIRS - 1)

            for i in range(UNITS + 5):
                if i < UNITS:
                    n = P * (unit(i)[3] + 1)
                    stored(act, ("s", i))
                    if i >= 4:
                        act.wait_ge(s_rec, i - 3)
                    A(ns[i % 4][:, 0:n], ns[i % 4][:, 0:n], ACT.Exp, scale=-1.0, bias=nmin[:, i % 4:i % 4 + 1],
                      accum_out=rsum[:, i % 4:i % 4 + 1]).then_inc(s_exp, 1)
                if i % 8 == 1 and i > 8:
                    split(P_GM + GM_SB + (i - 9) // 8 + RING)
                u = i - 3
                if 0 <= u < UNITS:
                    r, run = unit(u)[3:]
                    ps = result(act, ("t", u))
                    if run >= 2 and r == 0:
                        sparse_pv_done(act, run - 2)
                    emptied(A(pt[run % 2][:, 0:r + 1, P * r:P * r + P],
                              ps[:, 0:P * (r + 1)].rearrange("p (k t) -> p k t", k=r + 1), ACT.Copy), ("t", u))
                if i >= 16 and i % 16 == 4:
                    p = i // 16 - 1
                    A(qn_h[:, p], result(act, ("ons", p))[:], ACT.Copy).then_inc(o_hi, 1)
            for i in range(16):
                j = i // 2 + 8 * (i % 2)
                if i >= 8 and i % 2 == 0:
                    split(P_GM + GM_IN_ATT + (i - 8) // 2 + RING)
                stored(act, ("gm", j))
                A(gate_tile(j), gate_tile(j), ACT.Sigmoid).then_inc(sig_done, 1)
            for n in range(KT):
                split(P_UP + n + RING)
                act.wait_ge(mxs, n + 1)
                A(hh[:, n], mx[2 * (n % 2)][:], ACT.Copy).then_inc(m_hi, 1)
            for n in range(KT):
                split(P_OUT + n + RING)
                stored(act, ("out", n))
                if n >= 2:
                    act.wait_ge(x_ss, n - 1)
                A(tmp[:, n % 2], x_res[:, n], ACT.Square).then_inc(x_sq, 1)
                A(h2h[:, n], x_res[:, n], ACT.Copy, scale=nrm[:, 1, n:n + 1]).then_inc(h2hi, 1)
            ps = result(act, "rms2")
            emptied(A(rstd_b[:], ps[:], ACT.Ln, bias=epsc[:], scale=1.0 / D), "rms2")
            stored(act, "rms2")
            A(rstd_b[:], rstd_b[:], ACT.Exp, scale=-1.0).then_inc(rs2, 1)
            nr = 0
            for s, (which, q) in enumerate(FF_ORDER):
                for n in range(8):
                    p = P_FF + 8 * s + n + RING
                    if p < NPANEL:
                        split(p)
                    if which == 1:
                        act.wait_ge(r_sc, nr + 1)
                        if q >= 2 and n == 0:
                            result(act, ("ff", FF_ORDER.index((2, q - 2)), 7))
                        A(r_h[q % 2][:, n], tmp[:, nr % 2], ACT.Copy).then_inc(r_hi, 1)
                        nr += 1
                    elif q == QF - 1:
                        stored(act, ("ff", s, n))
                        if n >= 2:
                            act.wait_ge(y_ss, n - 1)
                        A(fin_sq[:, n % 2], x_res[:, n], ACT.Square).then_inc(y_sq, 1)
            ps = result(act, "rms3")
            act.wait_ge(r_lo, FT)
            emptied(A(tmp[:, 0], ps[:], ACT.Ln, bias=epsc[:], scale=1.0 / D), "rms3")
            stored(act, "rms3")
            A(tmp[:, 0], tmp[:, 0], ACT.Exp, scale=-0.5).then_inc(rs3, 1)

        @block.vector
        def _(dve):
            V = nc.vector
            for i, (t, v) in enumerate(((ones, 1.0), (epsc, EPS), (onec, 1.0))):
                V.memset(t[:], v).then_inc(set_done, 1)
            V.memset(relx[BUCKETS:BUCKETS + 1, :], BIG).then_inc(set_done, 1)
            dve.wait_ge(cst_in, 16 * 5)
            V.tensor_copy(negtri[:], cstb[:, 0:P]).then_inc(cast_done, 1)
            V.tensor_scalar(negones[:], ident[:], 0.0, -1.0, ALU.mult, ALU.add).then_inc(cast_done, 1)
            V.tensor_copy(diag_bf[:], cstb[:, P:2 * P]).then_inc(cast_done, 1)
            V.tensor_copy(ident_bf[:], ident[:]).then_inc(cast_done, 1)
            V.tensor_copy(blk_bf[:], cstb[0:2 * NB, 2 * P:2 * P + 2 * T].rearrange("p (g t) -> p g t", g=G)).then_inc(cast_done, 1)
            for i in range(2):
                ps = result(dve, f"vec{i}")
                emptied(V.tensor_copy(vec[:, T * i:T * i + T], ps[0:H, :]), f"vec{i}")
            dve.wait_ge(small_in, 16)
            for k in range(KT):
                dve.wait_ge(h_hi, k + 1)
                V.scalar_tensor_tensor(out=hl[:, k], in0=xs[:, k], scalar=nrm[:, 0, k:k + 1], in1=hh[:, k].bitcast(F32),
                                       op0=ALU.mult, op1=ALU.subtract).then_inc(h_lo, 1)
                dve.wait_ge(sq_done, k + 1)
                if k == 0:
                    V.tensor_copy(sqs[:], sqt[:, 0]).then_inc(sqs_done, 1)
                else:
                    dve.wait_ge(sqs_done, k)
                    V.tensor_tensor(sqs[:], sqs[:], sqt[:, k % 2], ALU.add).then_inc(sqs_done, 1)
            dve.wait_ge(gn_split, 1)
            V.tensor_tensor(gn_l[:], gns[:], gn_h[:].bitcast(F32), ALU.subtract).then_inc(gn_split, 1)
            dve.wait_ge(rst, 1)

            for i in range(2):
                ps = result(dve, ("pan", i))
                emptied(V.tensor_tensor(ckv[:, i], ps[:], rstd_b[:], ALU.mult), ("pan", i))
            ps = result(dve, "rcol")
            ins = V.tensor_copy(rcol[:], ps[:].rearrange("p (r t) -> p r t", r=RT)[:, :, 0])
            emptied(ins, "rcol")
            ps = result(dve, "dt")
            emptied(V.tensor_copy(dmat[:, :, 0:55], ps[:, 0:H * 56].rearrange("p (h m) -> p h m", h=H)[:, :, 0:55]), "dt")
            stored(dve, "rcol")

            def values(name, i, dst, width):
                ps = result(dve, name)
                for a in range(2):
                    r = 2 * i + a
                    ins = V.tensor_scalar(dst[r], ps[:, width * a:width * a + width], rcol[:, r:r + 1], None, ALU.mult)
                emptied(ins, name)

            for i in range(2):
                values(("v", i), i, [nv[:, r].rearrange("p a b -> p (a b)") for r in range(RT)], 2 * P)
            ps = result(dve, "gn")
            for r in range(RT):
                ins = V.tensor_scalar(gate[:, r].rearrange("p h b -> p (h b)"), ps[:, 32 * r:32 * r + 24], rcol[:, r:r + 1],
                                      -80.0, ALU.mult, ALU.max)
            emptied(ins, "gn")
            dve.wait_ge(gate_st, 1)
            V.tensor_scalar(gate[:], gate[:], 1.0, None, ALU.add).then_inc(gate_st, 1)
            dve.wait_ge(gate_st, 2)
            V.reciprocal(gate[:], gate[:]).then_inc(gate_st, 1)
            dve.wait_ge(cmp_in, 16 * 7)
            V.memset(hidTk[:], 0.0).then_inc(bm_done, 1)
            V.memset(hidTv[:], 0.0).then_inc(bm_done, 1)
            for i in range(2):
                dve.wait_ge(x2_in[i], 16 * 4)
                for g in range(G):
                    src = x2[i][:, g, :]
                    row = src.ap[0]
                    view = bass.AP(src.tensor, src.offset, [list(row), [2, CI], [CS, NC]])
                    V.tensor_tensor(bm[i][:, :, NC * g:NC * g + NC], view,
                                    pes[:, i, :].unsqueeze(2).to_broadcast([P, CI, NC]), ALU.add).then_inc(bm_done, 1)

            nt = [0]

            def evac(name, scale, lo, hi):
                i = nt[0]
                nt[0] += 1
                ps = result(dve, name)
                if i >= 2:
                    dve.wait_ge(t_lo, i - 1)
                ins = V.scalar_tensor_tensor(out=tmp[:, i % 2], in0=ps[:], scalar=scale, in1=rstd_b[:],
                                             op0=ALU.mult, op1=ALU.mult)
                emptied(ins, name)
                dve.wait_ge(t_hi, i + 1)
                V.tensor_tensor(lo, tmp[:, i % 2], hi.bitcast(F32), ALU.subtract).then_inc(t_lo, 1)

            evac(("pan", P_KS), 1.0, kn_l[:, 1], kn_h[:, 1])
            evac(("pan", P_KW), 1.0, kn_l[:, 0], kn_h[:, 0])
            evac(("pan", 6), -DH ** -0.5, qn_l[:, 0], qn_h[:, 0])
            evac(("pan", 7), -DH ** -0.5, qn_l[:, 1], qn_h[:, 1])
            ps = result(dve, "hidT")
            hk, hv = (ps[:, 124 * i:124 * i + 124].rearrange("p (m g c) -> p m g c", m=2, g=G) for i in range(2))
            V.tensor_copy(hidTk[:, :, :, 0:NC], hk)
            for m in range(2):
                for g in range(G):
                    ins = V.tensor_copy(hidTv[:, m, g, :, 0:NC], hv[:, m, g, :].unsqueeze(1).to_broadcast([P, 4, NC]))
            emptied(ins, "hidT")
            evac(("pan", 8), -DH ** -0.5, qn_l[:, 2], qn_h[:, 2])
            ps = result(dve, "kcvc")
            V.tensor_copy(kc32[0:64, :], ps[0:64, 0:32]).then_inc(kc_cp, 1)
            V.tensor_copy(kc32[64:128, :], ps[64:128, 32:64]).then_inc(kc_cp, 1)
            emptied(V.tensor_copy(vc[:], ps[:, 64:192].rearrange("p (g d) -> p g d", g=G)), "kcvc")
            evac(("pan", 9), -DH ** -0.5, qn_l[:, 3], qn_h[:, 3])
            dve.wait_ge(kc_split, 1)
            V.tensor_tensor(kc_l[:], kc32[:], kc_h[:].bitcast(F32), ALU.subtract).then_inc(kc_split, 1)

            def cmp_scores(r):
                dview = dmat[:, :, 30 + 8 * r - NC + 1:30 + 8 * r + 1][:, :, ::-1]
                if r:
                    dve.wait_ge(c_exp, r)
                for g in range(G):
                    hs = slice(HG * g, HG * g + HG)
                    ps = result(dve, ("cs", r, g))[:, 0:HG * 32].rearrange("p (h c) -> p h c", h=HG)
                    emptied(V.tensor_tensor(c_t[:, hs], ps[:, :, 0:NC], dview[:, hs], ALU.add), ("cs", r, g))
                for g in range(G):
                    stored(dve, ("cs", r, g))
                V.tensor_reduce(c_m[:, 0, :], c_t[:], AX.X, ALU.min).then_inc(c_min, 1)
                dve.wait_ge(c_min, r + 1)
                V.tensor_tensor(c_t[:], c_t[:], c_m[:, 0, :].unsqueeze(2).to_broadcast([P, H, NC]), ALU.subtract).then_inc(c_sub, 1)

            sel = [0]

            def step(ins):
                sel[0] += 1
                ins.then_inc(c_link, 1)
                dve.wait_ge(c_link, sel[0])

            def cmp_probs(r):
                dve.wait_ge(c_exp, r + 1)
                pr, pg = c_p[:, r % 2], c_g[:, r % 2]
                step(V.tensor_reduce(c_m[:, 1, :], pr[:, :, 0:NC], AX.X, ALU.add))
                step(V.reciprocal(c_m[:, 2, :], c_m[:, 1, :]))
                if r == 0:
                    step(V.tensor_scalar(c_m[:, 2, :], c_m[:, 2, :], rowvalid, None, ALU.mult))
                step(V.tensor_tensor(pr[:, :, 0:NC], pr[:, :, 0:NC], c_m[:, 2, :].unsqueeze(2).to_broadcast([P, H, NC]), ALU.mult))
                if r >= 2:
                    ct_read(r - 2)
                V.tensor_tensor(pg[:, :, 0:NC], pr[:, :, 0:NC], gate[:, r, :, 0].unsqueeze(2).to_broadcast([P, H, NC]), ALU.mult).then_inc(c_pready, 1)
                if r < 2:
                    return
                step(V.tensor_reduce(c_s[:, :, 1:1 + NC], pr.rearrange("p (g j) c -> p g c j", g=G)[:, :, 0:NC, :], AX.X, ALU.add))
                row = c_s[:].ap[0]
                win = bass.AP(c_s[:].tensor, c_s[:].offset, [list(row), [40, G], [4, NB], [1, 5]])
                step(V.tensor_reduce(c_i[:], win, AX.X, ALU.add))
                step(V.tensor_tensor(c_i[:], c_i[:], scoreadd[:, r - 2, :].unsqueeze(1).to_broadcast([P, G, NB]), ALU.add))
                for g in range(G):
                    step(V.max(c_8[:, g, :], c_i[:, g, :]))
                for g in range(G):
                    step(V.max_index(c_x[:, g, :], c_8[:, g, :], c_i[:, g, :]))
                step(V.tensor_copy(c_f[:], c_x[:]))
                for g in range(G):
                    step(V.tensor_tensor(c_e[:, g], iota8.unsqueeze(2).to_broadcast([P, NB, TOPK]),
                                         c_f[:, g, 0:TOPK].unsqueeze(1).to_broadcast([P, NB, TOPK]), ALU.is_equal))
                step(V.tensor_reduce(c_k[:], c_e[:], AX.X, ALU.max))
                V.tensor_scalar(c_k[:], c_k[:], -BIG, BIG, ALU.mult, ALU.add).then_inc(c_pready, 1)

            def ct_read(r):
                ps = result(dve, ("ct", r))
                ins = V.tensor_copy(pct[:, :, P * r:P * r + P], ps[:, 0:2 * P].rearrange("p (g t) -> p g t", g=G))
                if r >= 2:
                    ins = V.tensor_copy(maskT[:, r - 2, :], ps[0:2 * NB, 2 * P:3 * P])
                emptied(ins, ("ct", r))

            for t in (c_p, c_g, c_s):
                step(V.memset(t[:], 0.0))
            svd = [sv[:, r] for r in range(RT)]

            def sb_values(i):
                values(("sv", i), i % 2, [sv[:, r, 2 * P * (i // 2):2 * P * (i // 2) + 2 * P] for r in range(RT)], 2 * P)

            sb_values(0)
            sb_values(1)
            cmp_scores(0)
            sb_values(2)
            sb_values(3)
            cmp_probs(0)
            cmp_scores(1)
            for i in range(8):
                p, qk = divmod(i, 2)
                d_h, d_l = (sk_h, sk_l) if qk else (sq_h, sq_l)
                evac(("pan", P_SQK + i), 1.0 if qk else DH ** -0.5, d_l[:, p], d_h[:, p])
                if i == 1:
                    cmp_probs(1)
                    cmp_scores(2)
                if i == 3:
                    cmp_probs(2)
                    cmp_scores(3)
                if i == 5:
                    cmp_probs(3)
            for r in (2, 3):
                ct_read(r)

            def gate_logit(i):
                if i == GM_SB:
                    stick_pv_done(dve, H - 1)
                emptied(V.tensor_tensor(gate_tile(i), result(dve, ("gm", i))[:], rstd_b[:], ALU.mult), ("gm", i))

            def o_low(name, hi, lo, n):
                ps = result(dve, name)
                dve.wait_ge(o_hi, n + 1)
                emptied(V.tensor_tensor(lo, ps[:], hi.bitcast(F32), ALU.subtract), name)

            for h in range(H):
                w, b = ew[h % 2], 3 * (h % 2)
                if h >= 2:
                    stick_pv_done(dve, h - 2)
                for i, lo, hi in SB_A:
                    result(dve, ("z", h, i))
                    V.tensor_scalar(w[:, lo:hi], bank[b + i][:, 0:hi - lo], 40.0, None, ALU.min).then_inc(zc, 1)
                if h % 2 == 1 and h >= 3:
                    o_low(("osb", (h - 3) // 2), sq_h[:, (h - 3) // 2], sq_l[:, (h - 3) // 2], (h - 3) // 2)
                if h % 2 == 0 and h:
                    gate_logit(h // 2 - 1)
                dve.wait_ge(zl, h + 1)
                for i, lo, hi in SB_A:
                    V.tensor_tensor(w[:, lo:hi], bank[b + i][:, 0:hi - lo], w[:, lo:hi], ALU.max).then_inc(zs, 1)
                dve.wait_ge(zh, h + 1)
                V.tensor_tensor(sp_l[h % 2][:], w[:], sp_h[h % 2][:].bitcast(F32), ALU.subtract).then_inc(zlo, 1)
            gate_logit(GM_SB - 1)
            o_low(("osb", PAIRS - 1), sq_h[:, PAIRS - 1], sq_l[:, PAIRS - 1], PAIRS - 1)

            for i in range(UNITS + 5):
                if i < UNITS:
                    p, br, g, r, run = unit(i)
                    n = P * (r + 1)
                    ps = result(dve, ("s", i))
                    if i == 0:
                        dve.wait_ge(hank_in, 16)
                    if i >= 4:
                        result(dve, ("t", i - 4))
                    emptied(V.tensor_tensor_reduce(ns[i % 4][:, 0:n], ps[:, 0:n], hank[:, g * HG + p, 0:n][:, ::-1], 1.0, 3.0e38,
                                                   ALU.add, ALU.min, nmin[:, i % 4:i % 4 + 1]), ("s", i))
                u = i - 1
                if 0 <= u < UNITS:
                    p, br, g, r, run = unit(u)
                    n = P * (r + 1)
                    dve.wait_ge(s_exp, u + 1)
                    V.reciprocal(rec[:, u % 4:u % 4 + 1], rsum[:, u % 4:u % 4 + 1]).then_inc(s_rec, 1)
                    dve.wait_ge(s_rec, u + 1)
                    V.tensor_scalar(ns[u % 4][:, 0:n], ns[u % 4][:, 0:n], rec[:, u % 4:u % 4 + 1],
                                    gate[:, r, g * HG + p, 2 - br:3 - br], ALU.mult, ALU.mult).then_inc(s_nrm, 1)
                if i % 8 == 7 and i // 8 < UNITS // 8:
                    gate_logit(GM_SB + i // 8)
                if i >= 16 and i % 16 == 4:
                    p = i // 16 - 1
                    o_low(("ons", p), qn_h[:, p], qn_l[:, p], PAIRS + p)
            for i in range(GM_IN_ATT, 16):
                gate_logit(i)
            for n in range(KT):
                a, b = mx[2 * (n % 2)], mx[2 * (n % 2) + 1]
                dve.wait_ge(sig_done, 2 * n + 2)
                if n >= 2:
                    dve.wait_ge(m_lo, n - 1)
                for i, t in ((0, a), (1, b)):
                    ps = result(dve, (f"up{i}", n))
                    ins = V.tensor_tensor(t[:], ps[:], gate_tile(n + 8 * i), ALU.mult)
                    emptied(ins, (f"up{i}", n))
                stored(dve, ("up0", n))
                stored(dve, ("up1", n))
                V.tensor_tensor(a[:], a[:], b[:], ALU.add).then_inc(mxs, 1)
                dve.wait_ge(m_hi, n + 1)
                V.tensor_tensor(hl[:, n], a[:], hh[:, n].bitcast(F32), ALU.subtract).then_inc(m_lo, 1)
            dve.wait_ge(xres_in, 16)

            def add_sq(n, sq, acc, got, done):
                dve.wait_ge(got, n + 1)
                if n == 0:
                    V.tensor_copy(acc, sq).then_inc(done, 1)
                else:
                    dve.wait_ge(done, n)
                    V.tensor_tensor(acc, acc, sq, ALU.add).then_inc(done, 1)

            for n in range(KT):
                ps = result(dve, ("out", n))
                ins = V.tensor_tensor(x_res[:, n], ps[:], x_res[:, n], ALU.add)
                emptied(ins, ("out", n))
                add_sq(n, tmp[:, n % 2], mx[0][:], x_sq, x_ss)
                dve.wait_ge(h2hi, n + 1)
                V.scalar_tensor_tensor(out=h2l[:, n], in0=x_res[:, n], scalar=nrm[:, 1, n:n + 1], in1=h2h[:, n].bitcast(F32),
                                       op0=ALU.mult, op1=ALU.subtract).then_inc(h2lo, 1)
            dve.wait_ge(rs2, 1)
            nr = 0
            for s, (which, q) in enumerate(FF_ORDER):
                for n in range(8):
                    name = ("ff", s, n)
                    ps = result(dve, name)
                    if which == 1:
                        t = tmp[:, nr % 2]
                        if nr >= 2:
                            dve.wait_ge(r_lo, nr - 1)
                        V.tensor_scalar(t, ps[:], 0.0, None, ALU.max).then_inc(r_pos, 1)
                        dve.wait_ge(r_pos, nr + 1)
                        emptied(V.tensor_tensor(t, ps[:], t, ALU.mult), name)
                        stored(dve, name)
                        V.tensor_tensor(t, t, rstd_b[:], ALU.mult).then_inc(r_sc, 1)
                        dve.wait_ge(r_hi, nr + 1)
                        V.tensor_tensor(r_l[q % 2][:, n], t, r_h[q % 2][:, n].bitcast(F32), ALU.subtract).then_inc(r_lo, 1)
                        nr += 1
                    else:
                        ins = V.tensor_tensor(x_res[:, n], ps[:], x_res[:, n], ALU.add)
                        emptied(ins, name)
                        if q == QF - 1:
                            add_sq(n, fin_sq[:, n % 2], fin_ss[:], y_sq, y_ss)
            dve.wait_ge(rs3, 1)
            for n in range(KT):
                V.scalar_tensor_tensor(out=x_res[:, n], in0=x_res[:, n], scalar=nrm[:, 2, n:n + 1], in1=tmp[:, 0],
                                       op0=ALU.mult, op1=ALU.mult).then_inc(y_fin, 1)

        @block.tensor
        def _(pe_):
            M = nc.tensor.matmul

            def three(out, lh, ll, rh, rl, start, stop, **kw):
                M(out, ll, rh, start=start, stop=False, **kw)
                M(out, lh, rl, start=False, stop=False, **kw)
                return M(out, lh, rh, start=False, stop=stop, **kw)

            def panel(p, name, xh, xl, first=0, last=24):
                s = p % RING
                b = bank[USE[name][0]]
                for m in range(first, last):
                    k, a = divmod(m, 3)
                    if m == 0:
                        claim(pe_, name)
                        pe_.wait_ge(w_lo, p + 1)
                    lhs = (wlo if a == 0 else whi)[:, s, k, :]
                    ins = M(b[:], lhs, (xl if a == 1 else xh)[:, k, :], start=(m == 0), stop=(m == 23))
                    if m == 23:
                        filled(ins, name)

            def value_panels(p, names):
                pe_.wait_ge(w_lo, p + 2)
                s = p % RING
                for i, name in enumerate(names):
                    claim(pe_, name)
                    b = bank[USE[name][0]]
                    for a in range(2):
                        r = 2 * i + a
                        for k in range(KT):
                            lh, ll = hh[:, k, P * r:P * r + P], hl[:, k, P * r:P * r + P]
                            o = b[:, 2 * P * a:2 * P * a + 2 * P]
                            ins = three(o, lh, ll, whi[:, s:s + 2, k, :], wlo[:, s:s + 2, k, :], k == 0, k == KT - 1)
                    filled(ins, name)

            pe_.wait_ge(set_done, 4)
            pe_.wait_ge(cst_in, 16 * 5)
            for i in range(2):
                b = claim(pe_, f"vec{i}")
                filled(M(b[0:H, :], relx[:], oneh[:, T * i:T * i + T], start=True, stop=True), f"vec{i}")
            pe_.wait_ge(h_lo, KT)
            for i in range(2):
                panel(i, ("pan", i), hh, hl)
            b = claim(pe_, "rms")
            pe_.wait_ge(sqs_done, KT)
            filled(M(b[:], ones[:], sqs[:], start=True, stop=True), "rms")
            b = claim(pe_, "rcol")
            pe_.wait_ge(rst, 1)
            for r in range(RT):
                ins = nc.tensor.transpose(b[:, P * r:P * r + P], rstd_b[:, P * r:P * r + P], ident[:])
            filled(ins, "rcol")
            b = claim(pe_, "dt")
            pe_.wait_ge(dt_in, 16)
            for h in range(H):
                ins = nc.tensor.transpose(b[:, 56 * h:56 * h + 55], dts[:, h, :], ident[0:55, 0:55])
            filled(ins, "dt")
            value_panels(P_V, [("v", 0), ("v", 1)])
            b = claim(pe_, "gn")
            pe_.wait_ge(gn_split, 2)
            for r in range(RT):
                for k in range(KT):
                    ins = three(b[:, 32 * r:32 * r + 24], hh[:, k, P * r:P * r + P], hl[:, k, P * r:P * r + P],
                                gn_h[:, k, :], gn_l[:, k, :], k == 0, k == KT - 1)
            filled(ins, "gn")
            panel(4, ("pan", 4), hh, hl)
            panel(5, ("pan", 5), hh, hl)

            def hidden(i):
                b = claim(pe_, ("hid", i))
                pe_.wait_ge(bm_done, 2 + 2 * (i + 1))
                pe_.wait_ge(cmp_in, 16 * 7)
                for c in range(CI):
                    M(b[0:G * NC, 0:CM], bm[i][:, c, :], w1s[i][:, c, :], start=(c == 0), stop=False)
                filled(M(b[0:G * NC, 0:CM], ones[0:1, 0:G * NC], b1s[0:1, i, :], start=False, stop=True), ("hid", i))

            hidden(0)
            panel(6, ("pan", 6), hh, hl)
            hidden(1)
            panel(7, ("pan", 7), hh, hl)
            b = claim(pe_, "hidT")
            for i in range(2):
                stored(pe_, ("hid", i))
                for m in range(2):
                    ins = nc.tensor.transpose(b[:, 124 * i + 62 * m:124 * i + 62 * m + 62], hid[:, i, P * m:P * m + P], ident[0:62, 0:62])
            filled(ins, "hidT")
            panel(8, ("pan", 8), hh, hl)
            b = claim(pe_, "kcvc")
            stored(pe_, "hidT")
            for m in range(2):
                M(b[:, 0:64], w2k[:, m].rearrange("p a d -> p (a d)"), hidTk[:, m].rearrange("p g c -> p (g c)"),
                  start=(m == 0), stop=(m == 1))
            for g in range(G):
                for m in range(2):
                    ins = M(b[:, 64 + 64 * g:128 + 64 * g],
                            hidTv[:, m, g].rearrange("p j c -> p (j c)"), w2v[:, m, :],
                            start=(m == 0), stop=(m == 1))
            filled(ins, "kcvc")
            panel(9, ("pan", 9), hh, hl)

            def cmp_scores(r):
                pe_.wait_ge(kc_split, 2)
                pe_.wait_ge(t_lo, 6)
                for g in range(G):
                    b = claim(pe_, ("cs", r, g))
                    a = slice(64 * g, 64 * g + 64)
                    for j in range(HG):
                        ins = three(b[:, 32 * j:32 * j + 32], qn_h[a, j, P * r:P * r + P], qn_l[a, j, P * r:P * r + P],
                                    kc_h[a], kc_l[a], True, True)
                    filled(ins, ("cs", r, g))

            def cmp_transpose(r):
                b = claim(pe_, ("ct", r))
                pe_.wait_ge(c_pready, [1, 2, 4, 6][r])
                for g in range(G):
                    ins = nc.tensor.transpose(b[:, P * g:P * g + P], c_g[:, r % 2, HG * g:HG * g + HG, :].rearrange("p j c -> p (j c)"), ident[:])
                if r >= 2:
                    ins = nc.tensor.transpose(b[0:2 * NB, 2 * P:3 * P], c_k[:].rearrange("p g n -> p (g n)"), ident[:])
                filled(ins, ("ct", r))

            value_panels(P_SV, [("sv", 0), ("sv", 1)])
            cmp_scores(0)
            value_panels(P_SV + 2, [("sv", 2), ("sv", 3)])
            cmp_scores(1)
            for i in range(8):
                panel(P_SQK + i, ("pan", P_SQK + i), hh, hl)
                if i in (0, 2, 4, 6):
                    cmp_transpose(i // 2)
                if i in (1, 3):
                    cmp_scores(2 + i // 2)

            def gate_products(first, count):
                while count:
                    i, m = divmod(first, 24)
                    n = min(count, 24 - m)
                    panel(P_GM + i, ("gm", i), hh, hl, m, m + n)
                    first, count = first + n, count - n

            def logits(h):
                p, a = h // 2, slice(64 * (h % 2), 64 * (h % 2) + 64)
                b = 3 * (h % 2)
                for i in range(3):
                    claim(pe_, ("z", h, i))
                pe_.wait_ge(t_lo, 6 + 2 * p + 2)
                for k in (0, 1, 3, 2):
                    o = bank[b + KOFF[k] // T][:, KOFF[k] % T:KOFF[k] % T + KLEN[k]]
                    kk = slice(P * k, P * k + P)
                    three(o, sk_h[a, p, kk], sk_l[a, p, kk], sq_h[a, p, P * k:T], sq_l[a, p, P * k:T],
                          k != 3, False, skip_group_check=True)
                    ins = M(o[:, 0:P], ident_bf[:], diag_bf[:], start=False, stop=False, skip_group_check=True)
                    if k != 1:
                        filled(ins, ("z", h, KOFF[k] // T))

            def stick_sums(h):
                b = 3 * (h % 2)
                pe_.wait_ge(zlo, h + 1)
                for k in range(RT):
                    for j in range(k, RT):
                        c = KOFF[k] % T + P * (j - k)
                        o = bank[b + KOFF[k] // T][:, c:c + KLEN[j]]
                        w = negtri if j == k else negones
                        for part in (sp_l, sp_h):
                            ins = M(o, w[:], part[h % 2][:, KOFF[j]:KOFF[j] + KLEN[j]], start=False, stop=False, skip_group_check=True)
                ins.then_inc(c_acc, 1)

            def stick_pv(h):
                p, half = divmod(h, 2)
                for i in range(3):
                    stored(pe_, ("z", h, i))
                if half == 0:
                    claim(pe_, ("osb", p))
                o = bank[USE[("osb", p)][0]]
                for k in range(RT):
                    ins = M(o[64 * half:64 * half + 64, P * k:T], sv[:, k, DH * h:DH * h + DH],
                            ew[h % 2][:, KOFF[k]:KOFF[k] + KLEN[k]], start=(k == 0), stop=(k == RT - 1), skip_group_check=True)
                if half == 1:
                    filled(ins, ("osb", p))
                else:
                    ins.then_inc(pv_sb, 1)

            pe_.wait_ge(cast_done, 5)
            stored(pe_, ("sv", 2))
            stored(pe_, ("sv", 3))
            logits(0)
            for h in range(H):
                gate_products(CH_SB * h, CH_SB)
                if h + 1 < H:
                    logits(h + 1)
                if h:
                    stick_pv(h - 1)
                stick_sums(h)
            stick_pv(H - 1)

            def scores(u):
                p, br, g, r, run = unit(u)
                a, n = slice(64 * g, 64 * g + 64), P * (r + 1)
                b = bank[USE[("s", u)][0]]
                claim(pe_, ("s", u))
                masked = br == 1 and r >= 2
                ins = three(b[:, 0:n], qn_h[a, p, P * r:P * r + P], qn_l[a, p, P * r:P * r + P],
                            kn_h[a, br, 0:n], kn_l[a, br, 0:n], True, not masked)
                if masked:
                    stored(pe_, ("ct", r))
                    ins = M(b[:, 0:n], maskT[:, r - 2, :], blk_bf[:, g, 0:n], start=False, stop=True)
                filled(ins, ("s", u))

            def turn(u):
                p, br, g, r, run = unit(u)
                b = bank[USE[("t", u)][0]]
                claim(pe_, ("t", u))
                pe_.wait_ge(s_nrm, u + 1)
                for k in range(r + 1):
                    ins = nc.tensor.transpose(b[:, P * k:P * k + P], ns[u % 4][:, P * k:P * k + P], ident[:])
                filled(ins, ("t", u))

            def sparse_pv(run):
                p, bg = divmod(run, 2 * G)
                br, g = divmod(bg, G)
                o = bank[USE[("ons", p)][0]]
                if bg == 0:
                    claim(pe_, ("ons", p))
                    stored(pe_, ("ct", RT - 2))
                    stored(pe_, ("ct", RT - 1))
                    for gg in range(G):
                        a = slice(32 * p, 32 * p + 32)
                        M(o[64 * gg:64 * gg + 64, :], vc[a, gg, :], pct[a, gg, :], start=True, stop=False, skip_group_check=True)
                stored(pe_, ("t", RT * run + RT - 2))
                stored(pe_, ("t", RT * run + RT - 1))
                for k in range(RT):
                    ins = M(o[64 * g:64 * g + 64, P * k:T], nv[:, k, 1 - br, 64 * g:64 * g + 64], pt[run % 2][:, k, P * k:T],
                            start=False, stop=(k == RT - 1), skip_group_check=True)
                if bg == 2 * G - 1:
                    filled(ins, ("ons", p))
                else:
                    ins.then_inc(s_pv, 1)

            for i in range(UNITS + 5):
                if i < UNITS:
                    scores(i)
                    gate_products(24 * GM_SB + CH_NS * i, CH_NS)
                if 0 <= i - 2 < UNITS:
                    turn(i - 2)
                u = i - 4
                if 0 <= u < UNITS and u % 4 == 3:
                    sparse_pv(u // 4)
            gate_products(24 * GM_IN_ATT, 24 * (16 - GM_IN_ATT))

            stored(pe_, ("osb", PAIRS - 1))
            stored(pe_, ("ons", PAIRS - 1))
            for n in range(KT):
                p = P_UP + n
                pe_.wait_ge(w_lo, p + 1)
                s = p % RING
                for i, (oh, ol) in enumerate(((qn_h, qn_l), (sq_h, sq_l))):
                    name = (f"up{i}", n)
                    b = claim(pe_, name)
                    for k in range(PAIRS):
                        ins = three(b[:], whi[:, s, 4 * i + k, :], wlo[:, s, 4 * i + k, :], oh[:, k, :], ol[:, k, :], k == 0, k == PAIRS - 1)
                    filled(ins, name)
            pe_.wait_ge(m_lo, KT)
            for n in range(KT):
                panel(P_OUT + n, ("out", n), hh, hl)
            b = claim(pe_, "rms2")
            pe_.wait_ge(x_ss, KT)
            filled(M(b[:], ones[:], mx[0][:], start=True, stop=True), "rms2")
            pe_.wait_ge(h2lo, KT)
            for s, (which, q) in enumerate(FF_ORDER):
                if which == 2:
                    pe_.wait_ge(r_lo, 8 * (q + 1))
                for n in range(8):
                    a, c = (h2h, h2l) if which == 1 else (r_h[q % 2], r_l[q % 2])
                    panel(P_FF + 8 * s + n, ("ff", s, n), a, c)
            b = claim(pe_, "rms3")
            pe_.wait_ge(y_ss, KT)
            filled(M(b[:], ones[:], fin_ss[:], start=True, stop=True), "rms3")


def bucket(n):
    exact = BUCKETS // 2
    if n < exact:
        return n
    return min(BUCKETS - 1, exact + int(math.log(n / exact) / math.log(128 / exact) * (BUCKETS - exact)))


def constants():
    onehot = np.zeros((BUCKETS + 1, 2 * T), np.float32)
    for y in range(2 * T):
        d = y - (T - 1)
        if d < 0:
            onehot[BUCKETS, y] = 1.0
        else:
            onehot[bucket(d), y] = -1.0
    cst = np.zeros((P, 1433), np.float32)
    i, j = np.arange(P)[:, None], np.arange(P)[None, :]
    cst[:, 0:P] = np.where(i >= j, -1.0, 0.0)
    cst[:, P:2 * P] = np.where(i >= j, -BIG, 0.0)
    for g in range(G):
        for n in range(NB):
            cst[NB * g + n, 2 * P + T * g + 64 * n:2 * P + T * g + 64 * n + 64] = 1.0
    cst[:, 1280:1408] = np.eye(P)
    for r in range(2):
        own = (P * (r + 2) + np.arange(P)) // 64
        n = np.arange(NB)[None, :]
        add = np.where((n == own[:, None]) | (n == 0), FORCE, np.where(n <= own[:, None], 0.0, -FORCE))
        cst[:, 1408 + NB * r:1408 + NB * r + NB] = add
    cst[:, 1424] = np.arange(P) >= CL - 1
    cst[:, 1425:1433] = np.arange(NB)
    return onehot, cst


def kernel(**inputs):
    import concourse.bacc as bacc
    from concourse.bass_utils import run_bass_kernel_spmd

    a = {k: np.ascontiguousarray(v) for k, v in inputs.items()}
    w_in = a["w_in"][0]
    order = np.concatenate([np.arange(64) + 64 * h for j in range(PAIRS) for h in (j, j + HG)])
    kv = 512

    def cols(m):
        n = m.shape[1] // P
        return m.reshape(KT, P, n, P).transpose(2, 1, 0, 3).reshape(n, P, KT * P)

    def kvc(i):
        return w_in[:, kv + P * i:kv + P * i + P]

    sb = w_in[:, 512 + 768 + 24:512 + 768 + 24 + 1536]
    gates = w_in[:, 512 + 768 + 24 + 1536:]
    up = np.stack([a["w_up_nsa"][0][order], a["w_up_sb"][0]])
    up = up.reshape(2, PAIRS, P, KT, P).transpose(3, 2, 0, 1, 4).reshape(KT, P, KT * P)
    ff1 = cols(a["w_ff1"][0])
    ff2 = [cols(a["w_ff2"][0][D * q:D * q + D]) for q in range(QF)]
    parts = [cols(kvc(0)), cols(kvc(1)), cols(kvc(3)), cols(kvc(5)), cols(kvc(2)), cols(kvc(4)),
             cols(w_in[:, 0:512][:, order]), cols(sb[:, 1024:1536])]
    for p in range(PAIRS):
        parts += [cols(sb[:, P * p:P * p + P]), cols(sb[:, 512 + P * p:512 + P * p + P])]
    parts += [cols(gates), up, cols(a["w_out"][0])]
    for which, q in FF_ORDER:
        parts.append(ff1[8 * q:8 * q + 8] if which == 1 else ff2[q])
    panels = np.concatenate(parts)
    assert panels.shape == (NPANEL, P, KT * P), panels.shape
    w_gn = w_in[:, 1280:1304].reshape(KT, P, 24).transpose(1, 0, 2)
    norms = np.stack([a["norm_attn"][0], a["norm_mlp"][0], a["norm_final"]]).reshape(3, KT, P).transpose(2, 0, 1)
    two = ("cmp_k", "cmp_v")
    pe = np.stack([a[c + "_pe"][0].reshape(CI, P) for c in two]).transpose(2, 0, 1)
    w1 = np.stack([a[c + "_w1"][0].reshape(CI, P, CM).transpose(1, 0, 2) for c in two])
    b1 = np.stack([a[c + "_b1"][0] for c in two])[None]
    w2 = np.stack([a[c + "_w2"][0].reshape(2, P, DH).transpose(1, 0, 2) for c in two])
    xT = a["x"][0].T.reshape(KT, P, T).transpose(1, 0, 2)
    onehot, cst = constants()
    arrays = {"xT": xT, "panels": panels, "w_gn": w_gn, "norms": norms, "rel_bias": a["rel_bias"], "pe": pe,
              "w1": w1, "b1": b1, "w2": w2, "onehot": onehot, "cst": cst}
    arrays = {"in_" + k: np.ascontiguousarray(v) for k, v in arrays.items()}
    nc = bacc.Bacc("TRN2", target_bir_lowering=False, num_devices=1)
    args = [nc.dram_tensor(k, v.shape, mybir.dt.from_np(v.dtype), kind="ExternalInput").ap() for k, v in arrays.items()]
    args.append(nc.dram_tensor("out_0_dram", (P, KT, T), F32, kind="ExternalOutput").ap())
    block_kernel(nc, *args)
    r = run_bass_kernel_spmd(nc, [arrays], core_ids=[0])
    y = r.results[0]["out_0_dram"]
    return np.ascontiguousarray(y.transpose(1, 0, 2).reshape(D, T).T)[None]
```

```python
import math
from contextlib import ExitStack

import numpy as np

import concourse.bass as bass
from concourse import mybir

F32 = mybir.dt.float32
F32R = mybir.dt.float32r
BF16 = mybir.dt.bfloat16
U32 = mybir.dt.uint32
ALU = mybir.AluOpType
ACT = mybir.ActivationFunctionType
AX = mybir.AxisListType

P = 128
T = 512
D = 1024
KT = D // P
RT = T // P
DH = 64
H = 8
G = 2
HG = H // G
PAIRS = 4
CL, CS = 32, 16
NC = (T - CL) // CS + 1
CM = 256
CI = CL * DH // P
NB = T // 64
TOPK = 4
BUCKETS = 32
FT = 4 * D // P
QF = 4
EPS = 1e-6
BIG = 1e30
FORCE = 1e4

P_CK, P_CV, P_V, P_KS, P_KW, P_QN = 0, 1, 2, 4, 5, 6
P_SV, P_SQK, P_GM = 10, 14, 22
P_UP = P_GM + 16
P_OUT = P_UP + 8
P_FF = P_OUT + 8
FF_ORDER = [(1, 0), (1, 1), (2, 0), (1, 2), (2, 1), (1, 3), (2, 2), (2, 3)]
NPANEL = P_FF + 8 * len(FF_ORDER)
RING = 4

GM_IN_ATT = 12
GM_SB = 4
UNITS = PAIRS * 2 * G * RT
SB_BEFORE = [24] + [12] * 7
SB_BEHIND = [12] + [0] * 7
NS_PRODUCTS = [0, 0, 24] + [3, 2, 1, 4, 3, 2, 1, 4, 2, 2, 1, 4, 3, 2, 1, 4, 2, 2, 1, 4] * 3 + [0]


def bank_plan():
    order = [(("pan", 0), 0), (("pan", 1), 1), (("v", 0), 2), ("rms", 5), (("v", 1), 3), ("vec0", 6), ("vec1", 7),
             ("rcol", 4), ("gn", 7), (("pan", 4), 0), ("gnT", 3), (("pan", 5), 1), ("dt", 6),
             (("hid", 0), 5), (("pan", 6), 0), (("hid", 1), 6), (("pan", 7), 1),
             (("pan", 8), 0), ("kcvc", 7), (("pan", 9), 1)]
    sv = [(("sv", i), 2 + i % 2) for i in range(4)]
    cs = [(("cs", r), 4 + r % 2) for r in range(RT)]
    ct = [(("ct", r), 6 + r % 2) for r in range(RT)]
    order += [sv[0], sv[1], cs[0], sv[2], sv[3], cs[1]]
    for i in range(8):
        order.append((("pan", P_SQK + i), i % 2))
        if i in (0, 2, 4, 7):
            order.append(ct[i // 2])
        if i in (1, 3):
            order.append(cs[2 + i // 2])
    order += [(("z", h, i), 3 * (h % 2) + i) for h in range(H) for i in range(3)]
    order += [(("osb", p), 6) for p in range(PAIRS)]
    order += [(("gm", i), 6 if i > GM_SB and i % 2 == 0 else 7) for i in range(16)]
    order += [(("s", u), u % 3) for u in range(UNITS)]
    order += [(("t", u), 3 + u % 2) for u in range(UNITS)]
    order += [(("ons", p), 5) for p in range(PAIRS)]
    for n in range(KT):
        order += [(("up0", n), 2 * (n % 2)), (("up1", n), 2 * (n % 2) + 1)]
    order += [(("out", n), 4 + n % 2) for n in range(KT)]
    order += [("rms2", 6)]
    for s, (which, q) in enumerate(FF_ORDER):
        order += [(("ff", s, n), n % 4 if which == 1 else 4 + n % 2) for n in range(8)]
    order += [("rms3", 7)]
    seen, use = {}, {}
    for name, b in order:
        assert name not in use, name
        use[name] = (b, seen.get(b, 0))
        seen[b] = seen.get(b, 0) + 1
    return use


USE = bank_plan()


def panel_product(p):
    if P_V <= p < P_V + 2:
        return "v", 1
    if P_SV <= p < P_SV + 4:
        return "sv", (p - P_SV) // 2 * 2 + 1
    if p < P_GM:
        return "pan", p
    if p < P_UP:
        return "gm", p - P_GM
    if p < P_OUT:
        return "up1", p - P_UP
    if p < P_FF:
        return "out", p - P_OUT
    return "ff", (p - P_FF) // 8, (p - P_FF) % 8


def ff_use(stage, n, q, i):
    b, use = USE[("ff", stage, n)]
    bq, per_q = USE[("ff", stage + 2, n)]
    bi, per_i = USE[("ff", stage, n + RING)]
    assert b == bq == bi
    return [b, use + (per_q - use) * q + (per_i - use) * i]


def unit(u):
    run, r = divmod(u, RT)
    p, bg = divmod(run, 2 * G)
    return p, bg // G, bg % G, r, run


def block_kernel(nc, xT, panels, w_gn, norms, rel_bias, pe, w1, b1, w2, onehot, cst, outT):
    with ExitStack() as ctx:
        top = [nc.sbuf_base + (-nc.sbuf_base) % 64]
        fence = ctx.enter_context(nc.sbuf_tensor("arena", [P, (nc.sbuf_usable_end - top[0] - 256) // 4], F32))
        limit = nc.sbuf_usable_end

        def place(name, shape, dt=F32, at=None):
            size = int(np.prod(shape[1:])) * (2 if dt == BF16 else 4)
            size += (-size) % 64
            start = top[0] if at is None else at
            if at is None:
                top[0] += size
            assert start + size <= limit, (name, start + size - limit)
            return nc.alloc_sbuf_tensor_at(name, shape, dt, offset=start)

        def sem(name):
            return ctx.enter_context(nc.semaphore(name))

        wraw = [place(f"wraw{i}", [P, 8, P]) for i in range(RING)]
        whi = place("whi", [P, RING, 8, P], F32R)
        wlo = place("wlo", [P, RING, 8, P], F32R)
        rstd_b = place("rstd_b", [P, T])
        tmp = place("tmp", [P, 2, T])
        ones = place("ones", [P, P])
        nrm = place("nrm", [P, 3, KT])
        epsc = place("epsc", [P, 1])
        onec = place("onec", [P, 1])
        after_kept = top[0]
        hh = place("hh", [P, KT, T], F32R)
        hl = place("hl", [P, KT, T], F32R)
        at_q = top[0]
        qn_h = place("qn_h", [P, PAIRS, T], F32R)
        qn_l = place("qn_l", [P, PAIRS, T], F32R)
        kn_h = place("kn_h", [P, 2, T], F32R)
        kn_l = place("kn_l", [P, 2, T], F32R)
        at_sbq = top[0]
        sq_h = place("sq_h", [P, PAIRS, T], F32R)
        sq_l = place("sq_l", [P, PAIRS, T], F32R)
        at_sbk = top[0]
        sk_h = place("sk_h", [P, PAIRS, T], F32R)
        sk_l = place("sk_l", [P, PAIRS, T], F32R)
        at_sbv = top[0]
        sv = place("sv", [P, RT, H * DH])
        nv = place("nv", [P, RT, 2, P])
        at_g = top[0]
        hank = place("hank", [P, PAIRS, G, T])
        at_gm = top[0]
        gm = place("gm", [P, GM_IN_ATT, T])
        small = top[0]
        ident = place("ident", [P, P])
        tables = place("tables", [P, 2 * NB + 1 + NB])
        scoreadd = tables[:, 0:2 * NB].rearrange("p (r n) -> p r n", r=2)
        rowvalid = tables[:, 2 * NB:2 * NB + 1]
        iota8 = tables[:, 2 * NB + 1:]
        negtri = place("negtri", [P, P], F32R)
        negones = place("negones", [P, P], F32R)
        ident_bf = place("ident_bf", [P, P], BF16)
        diag_bf = place("diag_bf", [P, P], BF16)
        blk_bf = place("blk_bf", [2 * NB, G, T], BF16)
        rcol = place("rcol", [P, RT])
        gate = place("gate", [P, RT, H, 3])
        dmat = place("dmat", [P, H, 56])
        kc_h = place("kc_h", [P, 2 * 32], F32R)
        kc_l = place("kc_l", [P, 2 * 32], F32R)
        vc = place("vc", [P, G, DH])
        maskT = place("maskT", [2 * NB, 2, P], BF16)
        nmin = place("nmin", [P, 4])
        rsum = place("rsum", [P, 4])
        rec = place("rec", [P, 4])
        at_pct = top[0]
        pct = place("pct", [P, G, T])
        ckv = place("ckv", [P, 2, T], at=at_pct)
        xs = place("xs", [P, KT, T], at=at_gm)
        x2 = [place(f"x2{i}", [P, G, T], at=at_gm + 4096 * i) for i in range(2)]
        bm = [place(f"bm{i}", [P, CI, G * NC], at=at_gm + 8192 + 4096 * i) for i in range(2)]
        oneh = place("oneh", [BUCKETS + 1, 2 * T], at=at_gm + 16384)
        vec = place("vec", [H, 2 * T], at=at_gm + 20480)
        gsb = place("gsb", [3 * H, T], at=at_gm + 16384)
        hidTk = place("hidTk", [P, 2, G, 32], at=at_gm + 18432)
        hidTv = place("hidTv", [P, 2, G, 4, 32], at=at_gm + 18944)
        kc32 = place("kc32", [P, 2 * 32], at=at_gm + 20992)
        c_t = place("c_t", [P, H, NC], at=at_gm + 8192)
        c_p = place("c_p", [P, 2, H, 32], at=at_gm + 9216)
        c_g = place("c_g", [P, 2, H, 32], at=at_gm + 11264)
        c_m = place("c_m", [P, 4, H], at=at_gm + 13312)
        c_s = place("c_s", [P, G, 40], at=at_gm + 13440)
        c_i = place("c_i", [P, G, NB], at=at_gm + 13760)
        c_8 = place("c_8", [P, G, NB], at=at_gm + 13824)
        c_x = place("c_x", [P, G, NB], U32, at=at_gm + 13888)
        c_f = place("c_f", [P, G, NB], at=at_gm + 13952)
        c_e = place("c_e", [P, G, NB, TOPK], at=at_gm + 14016)
        c_k = place("c_k", [P, G, NB], at=at_gm + 14272)
        w1s = [place("w1k", [P, CI, CM], at=at_g), place("w1v", [P, CI, CM], at=at_sbk)]
        sqt = place("sqt", [P, 2, T], at=at_sbq)
        sqs = place("sqs", [P, T], at=at_sbq + 4096)
        dts = place("dts", [55, H, P], at=at_sbq + 6144)
        relx = place("relx", [BUCKETS + 1, H], at=at_sbq + 10240)
        pes = place("pes", [P, 2, CI], at=at_sbq + 10304)
        b1s = place("b1s", [P, 2, 2], at=at_sbq + 10496)
        w2k = place("w2k", [P, 2, 2, DH], at=at_sbq + 12544)
        w2v = place("w2v", [P, 2, DH], at=at_sbq + 13568)
        cstb = place("cstb", [P, 2 * P + 2 * T], at=at_sbv)
        gns = place("gns", [P, KT, 3 * H], at=at_sbv + 5632)
        gn_h = place("gn_h", [P, KT, 3 * H], F32R, at=at_sbv + 6400)
        gn_l = place("gn_l", [P, KT, 3 * H], F32R, at=at_sbv + 7168)
        KOFF = [0, T, 2 * T, T + 3 * P]
        KLEN = [T - P * k for k in range(RT)]
        SBW = 2 * T + 2 * P
        behind_gm = at_gm + 2048 * GM_SB
        ew = [place(f"ew{i}", [P, SBW], at=at_g + 5120 * i) for i in range(2)]
        sp_h = [place(f"sp_h{i}", [P, SBW], F32R, at=(at_g + 10240, behind_gm)[i]) for i in range(2)]
        sp_l = [place(f"sp_l{i}", [P, SBW], F32R, at=behind_gm + 5120 * (i + 1)) for i in range(2)]
        ns = [place(f"ns{i}", [P, T], at=at_sbk + 2048 * i) for i in range(4)]
        pt = [place(f"pt{i}", [P, RT, T], at=at_sbk + 8192 + 8192 * i) for i in range(2)]
        gm2 = place("gm2", [P, 16 - GM_IN_ATT, T], at=at_g)
        mx = [place(f"mx{i}", [P, T], at=at_sbk + 16384 + 2048 * i) for i in range(4)]
        x_res = place("x_res", [P, KT, T], at=at_sbk)
        h2h = place("h2h", [P, KT, T], F32R, at=at_q)
        h2l = place("h2l", [P, KT, T], F32R, at=at_q + 16384)
        r_h = place("r_h", [P, 2 * 8, T], F32R, at=at_sbv)
        r_l = place("r_l", [P, 2 * 8, T], F32R, at=at_sbv + 32768)
        fin_sq = place("fin_sq", [P, 2, T], at=after_kept)
        fin_ss = place("fin_ss", [P, T], at=after_kept + 4096)

        bank = [ctx.enter_context(nc.psum_tensor(f"bank{i}", [P, T], F32)) for i in range(8)]
        full = [sem(f"bank{i}_full") for i in range(8)]
        free = [sem(f"bank{i}_free") for i in range(8)]

        def where(name):
            return name if isinstance(name, list) else USE[name]

        def claim(eng, name):
            b, n = where(name)
            if not (isinstance(n, int) and n == 0):
                eng.wait_ge(free[b], n)
            return bank[b]

        def filled(ins, name):
            ins.then_inc(full[where(name)[0]], 1)

        def result(eng, name):
            b, n = where(name)
            eng.wait_ge(full[b], n + 1)
            return bank[b]

        def emptied(ins, name):
            ins.then_inc(free[where(name)[0]], 1)

        def stored(eng, name):
            b, n = where(name)
            eng.wait_ge(free[b], n + 1)

        x_in = [sem(f"x_in{i}") for i in range(KT)]
        small_in, cst_in, gn_in, cmp_in = sem("norms_in"), sem("constants_in"), sem("gate_weights_in"), sem("cmp_weights_in")
        vec_out, dt_in, x2_in = sem("bias_out"), sem("bias_rows_in"), [sem("cmp_k_tokens_in"), sem("cmp_v_tokens_in")]
        hank_in, xres_in, out_sem = [sem(f"bias_in{i}") for i in range(PAIRS)], sem("residual_in"), sem("out_written")
        w_in = [sem(f"panel_in{i}") for i in range(RING)]
        w_hi, w_lo = sem("panel_hi"), sem("panel_lo")
        set_done, cast_done = sem("memsets"), sem("const_casts")
        h_hi, h_lo, sq_done, sqs_done = sem("h_hi"), sem("h_lo"), sem("sq_done"), sem("sqsum_done")
        rst, gn_split, gate_st = sem("rstd_ready"), sem("gate_weights_split"), sem("branch_gate_steps")
        t_hi, t_lo = sem("tmp_hi"), sem("tmp_lo")
        bm_done, kc_cp, kc_split = sem("block_matrices"), sem("kc_copied"), sem("kc_split")
        c_min, c_sub, c_exp, c_pready, c_link = sem("cmp_min"), sem("cmp_less_min"), sem("cmp_exp"), sem("cmp_probs"), sem("cmp_links")
        zc, ze, zl, zs = sem("z_clamped"), sem("z_exp"), sem("z_log"), sem("softplus")
        zh, zlo, c_acc, pv_sb = sem("softplus_hi"), sem("softplus_lo"), sem("stick_sums"), sem("stick_pv_first_half")
        o_hi = sem("mixer_out_hi")
        s_exp, s_rec, s_nrm, s_pv = sem("scores_exp"), sem("sum_reciprocal"), sem("probs_ready"), sem("sparse_pv")
        sig_done, mxs, m_hi, m_lo = sem("gates"), sem("mixed"), sem("mixed_hi"), sem("mixed_lo")
        x_sq, x_ss, h2hi, h2lo, rs2 = sem("x_squared"), sem("x_sqsum"), sem("h2_hi"), sem("h2_lo"), sem("rstd2_ready")
        r_pos, r_sc, r_hi, r_lo = sem("relu"), sem("relu_squared"), sem("r_hi"), sem("r_lo")
        y_sq, y_ss, rs3, y_fin = sem("y_squared"), sem("y_sqsum"), sem("rstd3_ready"), sem("y_final")

        vf = nc.dram_tensor("bias_by_distance", [H, 2 * T], F32, kind="Internal").ap()

        def gate_tile(i):
            return gm[:, i, :] if i < GM_IN_ATT else gm2[:, i - GM_IN_ATT, :]

        SB_A = [(0, 0, T), (1, T, 2 * T), (2, 2 * T, SBW)]

        def stick_pv_done(eng, h):
            if h % 2:
                result(eng, ("osb", h // 2))
            else:
                eng.wait_ge(pv_sb, h // 2 + 1)

        def sparse_pv_done(eng, run):
            p, bg = divmod(run, 2 * G)
            if bg == 2 * G - 1:
                result(eng, ("ons", p))
            else:
                eng.wait_ge(s_pv, (2 * G - 1) * p + bg + 1)

        block = ctx.enter_context(nc.Block())

        @block.sync
        def _(sp):
            def panel(p, i=0):
                if p >= RING:
                    sp.wait_ge(w_lo, p - RING + 1 + RING * i)
                sp.dma_start(wraw[p % RING][:], panels[p + RING * i].rearrange("p (k m) -> p k m", k=8)).then_inc(w_in[p % RING], 16)

            def panel_loop(first, last):
                rounds = (last - first) // RING
                with sp.Fori(0, rounds) as i:
                    for j in range(RING):
                        panel(first + j, i)
                for p in range(first + RING * rounds, last):
                    panel(p)

            panel(0)
            for k in range(KT):
                sp.dma_start(xs[:, k, :], xT[:, k, :]).then_inc(x_in[k], 16)
                if k == 3:
                    panel(1)
            panel(2)
            panel(3)
            sp.dma_start(relx[0:BUCKETS, :], rel_bias).then_inc(cst_in, 16)
            sp.dma_start(oneh[:], onehot).then_inc(cst_in, 16)
            sp.dma_start(ident[:], cst[:, 2 * P + 2 * T:3 * P + 2 * T]).then_inc(cst_in, 16)
            sp.dma_start(gns[:], w_gn).then_inc(gn_in, 16)
            sp.dma_start(pes[:], pe).then_inc(cmp_in, 16)
            sp.dma_start(b1s[:], b1).then_inc(cmp_in, 16)
            sp.dma_start(w2k[:, :, 0, :], w2[0]).then_inc(cmp_in, 16)
            sp.dma_start(w2k[:, :, 1, :], w2[0]).then_inc(cmp_in, 16)
            sp.dma_start(w2v[:], w2[1]).then_inc(cmp_in, 16)
            panel(RING)
            panel(RING + 1)
            for i in range(2):
                sp.dma_start(w1s[i][:], w1[i]).then_inc(cmp_in, 16)
            sp.dma_start(cstb[:], cst[:, 0:2 * P + 2 * T]).then_inc(cst_in, 16)
            sp.dma_start(tables[:], cst[:, 3 * P + 2 * T:]).then_inc(cst_in, 16)
            panel_loop(RING + 2, P_GM + GM_SB + 5)
            for q in range(PAIRS):
                stick_pv_done(sp, H - 1 if q else H - 2)
                sp.dma_start(hank[:, q], bass.AP(vf.tensor, 3 * P + 2 * T * q, [[1, P], [HG * 2 * T, G], [1, T]])).then_inc(hank_in[q], 16)
            panel_loop(P_GM + GM_SB + 5, P_UP + 3)
            sparse_pv_done(sp, 4 * PAIRS - 1)
            sp.dma_start(x_res[:], xT).then_inc(xres_in, 16)
            panel_loop(P_UP + 3, NPANEL)
            for n in range(KT):
                sp.wait_ge(y_fin, n + 1)
                sp.dma_start(outT[:, n, :], x_res[:, n, :]).then_inc(out_sem, 16)
            sp.wait_ge(out_sem, 16 * KT)

        @block.gpsimd
        def _(pool):
            def low(p, i=0):
                s = p % RING
                pool.wait_ge(w_hi, p + 1 + RING * i)
                nc.gpsimd.tensor_tensor(wlo[:, s], wraw[s][:], whi[:, s].bitcast(F32), ALU.subtract).then_inc(w_lo, 1)

            with pool.Fori(0, NPANEL // RING) as i:
                for p in range(RING):
                    low(p, i)
            for p in range(NPANEL // RING * RING, NPANEL):
                low(p)

        @block.scalar
        def _(act):
            A = nc.scalar.activation

            def exp_and_ln():
                nc.scalar.preload_act_table_set("natural_log_exp_and_others")

            exp_and_ln()
            act.dma_start(nrm[:], norms).then_inc(small_in, 16)

            def split(p):
                s = p % RING
                act.wait_ge(w_in[s], 16 * (p // RING + 1))
                if p >= RING:
                    result(act, panel_product(p - RING))
                A(whi[:, s], wraw[s][:], ACT.Copy).then_inc(w_hi, 1)

            def split_next(stage, n, q, i):
                p = P_FF + 8 * stage + n + RING
                s = p % RING
                act.wait_ge(w_in[s], 16 * (p // RING + 1) + 16 * (4 * q + i))
                result(act, ff_use(stage, n, q, i))
                A(whi[:, s], wraw[s][:], ACT.Copy).then_inc(w_hi, 1)

            act.wait_ge(small_in, 16)
            split(0)
            for k in range(KT):
                act.wait_ge(x_in[k], 16)
                A(hh[:, k], xs[:, k], ACT.Copy, scale=nrm[:, 0, k:k + 1]).then_inc(h_hi, 1)
                if k == 5:
                    split(1)
            split(2)
            split(3)
            for k in range(KT):
                if k >= 2:
                    act.wait_ge(sqs_done, k - 1)
                A(sqt[:, k % 2], xs[:, k], ACT.Square).then_inc(sq_done, 1)
            ps = result(act, "rms")
            act.wait_ge(set_done, 4)
            emptied(A(rstd_b[:], ps[:], ACT.Ln, bias=epsc[:], scale=1.0 / D), "rms")
            stored(act, "rms")
            A(rstd_b[:], rstd_b[:], ACT.Exp, scale=-0.5).then_inc(rst, 1)
            act.wait_ge(gn_in, 16)
            A(gn_h[:], gns[:], ACT.Copy).then_inc(gn_split, 1)
            split(4)
            split(5)
            stored(act, "vec0")
            stored(act, "vec1")
            act.dma_start(vf, vec[:]).then_inc(vec_out, 16)
            act.wait_ge(vec_out, 16)
            act.dma_start(dts[:], bass.AP(vf.tensor, 0, [[16, 55], [2 * T, H], [1, P]])).then_inc(dt_in, 16)

            nt = [0]

            def round_tmp(p, dst):
                stored(act, ("pan", p))
                A(dst, tmp[:, nt[0] % 2], ACT.Copy).then_inc(t_hi, 1)
                nt[0] += 1

            def cmp_exp(r):
                act.wait_ge(c_sub, r + 1)
                A(c_p[:, r % 2, :, 0:NC], c_t[:], ACT.Exp, scale=-1.0).then_inc(c_exp, 1)

            for i in range(2):
                stored(act, ("pan", i))
                for g in range(G):
                    src = ckv[64 * g:64 * g + 64, i, :]
                    act.dma_start(x2[i][0:64, g, :], src).then_inc(x2_in[i], 16)
                    act.dma_start(x2[i][64:128, g, 0:T - 1], src[:, 1:T]).then_inc(x2_in[i], 16)
            ps = result(act, "gnT")
            emptied(A(gate[:].rearrange("p r h b -> p (r h b)"), ps[:, 0:RT * 3 * H], ACT.Exp, scale=-1.0), "gnT")
            split(6)
            split(7)
            split(8)
            round_tmp(P_KS, kn_h[:, 1])
            split(9)
            round_tmp(P_KW, kn_h[:, 0])
            for j in range(PAIRS):
                split(P_QN + j + RING)
                round_tmp(P_QN + j, qn_h[:, j])
                if j in (0, 1):
                    ps = result(act, ("hid", j))
                    act.wait_ge(bm_done, 2)
                    for m in range(2):
                        src = ps[:, 64 * m:64 * m + G * NC].rearrange("p (g c) -> p g c", g=G)
                        dst = hidTk[:, m, :, 0:NC]
                        if j == 1:
                            dst, src = hidTv[:, m, :, :, 0:NC], src.unsqueeze(2).to_broadcast([P, G, 4, NC])
                        ins = A(dst, src, ACT.Gelu_apprx_tanh, bias=b1s[:, j, m:m + 1])
                    emptied(ins, ("hid", j))
            exp_and_ln()
            act.wait_ge(kc_cp, 4)
            A(kc_h[:], kc32[:], ACT.Copy).then_inc(kc_split, 1)
            split(14)
            split(15)
            cmp_exp(0)
            split(16)
            split(17)
            cmp_exp(1)
            for i in range(8):
                p, qk = divmod(i, 2)
                split(P_SQK + i + RING)
                round_tmp(P_SQK + i, (sk_h if qk else sq_h)[:, p])
                if i in (1, 3):
                    cmp_exp(2 + i // 2)

            def stick_weights(h):
                act.wait_ge(c_acc, h + 1)
                act.wait_ge(zlo, h + 1)
                for i, lo, hi in SB_A:
                    emptied(A(ew[h % 2][:, lo:hi], bank[3 * (h % 2) + i][:, 0:hi - lo], ACT.Exp), ("z", h, i))

            def stick_out_high(p):
                A(sq_h[:, p], result(act, ("osb", p))[:], ACT.Copy).then_inc(o_hi, 1)

            for h in range(H):
                w = ew[h % 2]
                if h % 2 == 1 and h >= 3:
                    stick_out_high((h - 3) // 2)
                act.wait_ge(zc, 3 * h + 3)
                A(w[:], w[:], ACT.Exp).then_inc(ze, 1)
                act.wait_ge(ze, h + 1)
                A(w[:], w[:], ACT.Ln, bias=onec[:], scale=1.0).then_inc(zl, 1)
                if h:
                    stick_weights(h - 1)
                act.wait_ge(zs, 3 * h + 3)
                A(sp_h[h % 2][:], w[:], ACT.Copy).then_inc(zh, 1)
                if h % 2 == 1:
                    split(P_GM + h // 2 + RING)
            stick_weights(H - 1)
            stick_out_high(PAIRS - 1)

            for i in range(UNITS + 5):
                if i < UNITS:
                    n = P * (unit(i)[3] + 1)
                    stored(act, ("s", i))
                    if i >= 4:
                        act.wait_ge(s_rec, i - 3)
                    A(ns[i % 4][:, 0:n], ns[i % 4][:, 0:n], ACT.Exp, scale=-1.0, bias=nmin[:, i % 4:i % 4 + 1],
                      accum_out=rsum[:, i % 4:i % 4 + 1]).then_inc(s_exp, 1)
                if i == 0:
                    split(P_GM + GM_SB + RING)
                if i % 10 == 4 and i < UNITS:
                    split(P_GM + GM_SB + 1 + i // 10 + RING)
                u = i - 3
                if 0 <= u < UNITS:
                    r, run = unit(u)[3:]
                    ps = result(act, ("t", u))
                    if run >= 2 and r == 0:
                        sparse_pv_done(act, run - 2)
                    emptied(A(pt[run % 2][:, 0:r + 1, P * r:P * r + P],
                              ps[:, 0:P * (r + 1)].rearrange("p (k t) -> p k t", k=r + 1), ACT.Copy), ("t", u))
                if i >= 16 and i % 16 == 4:
                    p = i // 16 - 1
                    A(qn_h[:, p], result(act, ("ons", p))[:], ACT.Copy).then_inc(o_hi, 1)
            for i in range(16):
                j = i // 2 + 8 * (i % 2)
                if i == 0:
                    split(P_GM + GM_IN_ATT - 1 + RING)
                if i >= 8 and i % 2 == 0:
                    split(P_GM + GM_IN_ATT + (i - 8) // 2 + RING)
                stored(act, ("gm", j))
                A(gate_tile(j), gate_tile(j), ACT.Sigmoid).then_inc(sig_done, 1)
            exp_and_ln()
            for n in range(KT):
                split(P_UP + n + RING)
                act.wait_ge(mxs, n + 1)
                A(hh[:, n], mx[2 * (n % 2)][:], ACT.Copy).then_inc(m_hi, 1)
            for n in range(KT):
                split(P_OUT + n + RING)
                stored(act, ("out", n))
                if n >= 2:
                    act.wait_ge(x_ss, n - 1)
                A(tmp[:, n % 2], x_res[:, n], ACT.Square).then_inc(x_sq, 1)
                A(h2h[:, n], x_res[:, n], ACT.Copy, scale=nrm[:, 1, n:n + 1]).then_inc(h2hi, 1)
            ps = result(act, "rms2")
            emptied(A(rstd_b[:], ps[:], ACT.Ln, bias=epsc[:], scale=1.0 / D), "rms2")
            stored(act, "rms2")
            A(rstd_b[:], rstd_b[:], ACT.Exp, scale=-1.0).then_inc(rs2, 1)
            def hidden_high(n, nr, row):
                act.wait_ge(r_sc, nr + 1)
                A(r_h[:, row], tmp[:, n % 2], ACT.Copy).then_inc(r_hi, 1)

            for n in range(8):
                split(P_FF + n + RING)
                hidden_high(n, n, n)
            with act.Fori(0, QF - 1) as q:
                b, use = USE[("ff", 2, 7)]
                uses = USE[("ff", 4, 7)][1] - use
                act.wait_ge(full[b], use - uses + 1 + uses * q)
                with act.Fori(0, 2) as i:
                    for n in range(RING):
                        split_next(1, n, q, i)
                        hidden_high(n, 8 + n + 8 * q + RING * i, (q + 1) % 2 * 8 + n + RING * i)
                with act.Fori(0, 2) as i:
                    for n in range(RING):
                        split_next(2, n, q, i)
            for n in range(8):
                if n < RING:
                    split(P_FF + 8 * 7 + n + RING)
                stored(act, ("ff", 7, n))
                if n >= 2:
                    act.wait_ge(y_ss, n - 1)
                A(fin_sq[:, n % 2], x_res[:, n], ACT.Square).then_inc(y_sq, 1)
            ps = result(act, "rms3")
            act.wait_ge(r_lo, FT)
            emptied(A(tmp[:, 0], ps[:], ACT.Ln, bias=epsc[:], scale=1.0 / D), "rms3")
            stored(act, "rms3")
            A(tmp[:, 0], tmp[:, 0], ACT.Exp, scale=-0.5).then_inc(rs3, 1)

        @block.vector
        def _(dve):
            V = nc.vector
            for i, (t, v) in enumerate(((ones, 1.0), (epsc, EPS), (onec, 1.0))):
                V.memset(t[:], v).then_inc(set_done, 1)
            V.memset(relx[BUCKETS:BUCKETS + 1, :], BIG).then_inc(set_done, 1)
            dve.wait_ge(small_in, 16)
            for k in range(KT):
                dve.wait_ge(h_hi, k + 1)
                V.scalar_tensor_tensor(out=hl[:, k], in0=xs[:, k], scalar=nrm[:, 0, k:k + 1], in1=hh[:, k].bitcast(F32),
                                       op0=ALU.mult, op1=ALU.subtract).then_inc(h_lo, 1)
            for k in range(KT):
                dve.wait_ge(sq_done, k + 1)
                if k == 0:
                    V.tensor_copy(sqs[:], sqt[:, 0]).then_inc(sqs_done, 1)
                else:
                    dve.wait_ge(sqs_done, k)
                    V.tensor_tensor(sqs[:], sqs[:], sqt[:, k % 2], ALU.add).then_inc(sqs_done, 1)
            dve.wait_ge(gn_split, 1)
            V.tensor_tensor(gn_l[:], gns[:], gn_h[:].bitcast(F32), ALU.subtract).then_inc(gn_split, 1)
            for i in range(2):
                ps = result(dve, f"vec{i}")
                emptied(V.tensor_copy(vec[:, T * i:T * i + T], ps[0:H, :]), f"vec{i}")
            dve.wait_ge(rst, 1)

            for i in range(2):
                ps = result(dve, ("pan", i))
                emptied(V.tensor_tensor(ckv[:, i], ps[:], rstd_b[:], ALU.mult), ("pan", i))
            ps = result(dve, "rcol")
            ins = V.tensor_copy(rcol[:], ps[:].rearrange("p (r t) -> p r t", r=RT)[:, :, 0])
            emptied(ins, "rcol")
            stored(dve, "rcol")

            def values(name, i, dst, width):
                ps = result(dve, name)
                for a in range(2):
                    r = 2 * i + a
                    ins = V.tensor_scalar(dst[r], ps[:, width * a:width * a + width], rcol[:, r:r + 1], None, ALU.mult)
                emptied(ins, name)

            for i in range(2):
                values(("v", i), i, [nv[:, r].rearrange("p a b -> p (a b)") for r in range(RT)], 2 * P)
            ps = result(dve, "gn")
            ins = V.tensor_tensor(gsb[:], ps[0:3 * H, :], rstd_b[0:3 * H, :], ALU.mult)
            ins.then_inc(gate_st, 1)
            dve.wait_ge(gate_st, 1)
            emptied(V.tensor_scalar(gsb[:], gsb[:], -80.0, None, ALU.max), "gn")
            stored(dve, "gnT")
            V.tensor_scalar(gate[:], gate[:], 1.0, None, ALU.add).then_inc(gate_st, 1)
            dve.wait_ge(gate_st, 2)
            V.reciprocal(gate[:], gate[:]).then_inc(gate_st, 1)
            dve.wait_ge(cst_in, 16 * 5)
            V.tensor_copy(negtri[:], cstb[:, 0:P]).then_inc(cast_done, 1)
            V.tensor_scalar(negones[:], ident[:], 0.0, -1.0, ALU.mult, ALU.add).then_inc(cast_done, 1)
            V.tensor_copy(diag_bf[:], cstb[:, P:2 * P]).then_inc(cast_done, 1)
            V.tensor_copy(ident_bf[:], ident[:]).then_inc(cast_done, 1)
            V.tensor_copy(blk_bf[:], cstb[0:2 * NB, 2 * P:2 * P + 2 * T].rearrange("p (g t) -> p g t", g=G)).then_inc(cast_done, 1)
            dve.wait_ge(cmp_in, 16 * 7)
            V.memset(hidTk[:], 0.0).then_inc(bm_done, 1)
            V.memset(hidTv[:], 0.0).then_inc(bm_done, 1)
            for i in range(2):
                dve.wait_ge(x2_in[i], 16 * 4)
                for g in range(G):
                    src = x2[i][:, g, :]
                    row = src.ap[0]
                    view = bass.AP(src.tensor, src.offset, [list(row), [2, CI], [CS, NC]])
                    V.tensor_tensor(bm[i][:, :, NC * g:NC * g + NC], view,
                                    pes[:, i, :].unsqueeze(2).to_broadcast([P, CI, NC]), ALU.add).then_inc(bm_done, 1)

            ps = result(dve, "dt")
            emptied(V.tensor_copy(dmat[:, :, 0:55], ps[:, 0:H * 56].rearrange("p (h m) -> p h m", h=H)[:, :, 0:55]), "dt")
            nt = [0]

            def evac(name, scale, lo, hi):
                i = nt[0]
                nt[0] += 1
                ps = result(dve, name)
                if i >= 2:
                    dve.wait_ge(t_lo, i - 1)
                ins = V.scalar_tensor_tensor(out=tmp[:, i % 2], in0=ps[:], scalar=scale, in1=rstd_b[:],
                                             op0=ALU.mult, op1=ALU.mult)
                emptied(ins, name)
                dve.wait_ge(t_hi, i + 1)
                V.tensor_tensor(lo, tmp[:, i % 2], hi.bitcast(F32), ALU.subtract).then_inc(t_lo, 1)

            evac(("pan", P_KS), 1.0, kn_l[:, 1], kn_h[:, 1])
            evac(("pan", P_KW), 1.0, kn_l[:, 0], kn_h[:, 0])
            evac(("pan", 6), -DH ** -0.5, qn_l[:, 0], qn_h[:, 0])
            evac(("pan", 7), -DH ** -0.5, qn_l[:, 1], qn_h[:, 1])
            evac(("pan", 8), -DH ** -0.5, qn_l[:, 2], qn_h[:, 2])
            ps = result(dve, "kcvc")
            for g in range(G):
                a = slice(64 * g, 64 * g + 64)
                V.tensor_copy(kc32[a, 32 * g:32 * g + 32], ps[a, 32 * g:32 * g + 32]).then_inc(kc_cp, 1)
                V.memset(kc32[a, 32 - 32 * g:64 - 32 * g], 0.0).then_inc(kc_cp, 1)
            emptied(V.tensor_copy(vc[:], ps[:, 64:192].rearrange("p (g d) -> p g d", g=G)), "kcvc")
            evac(("pan", 9), -DH ** -0.5, qn_l[:, 3], qn_h[:, 3])
            dve.wait_ge(kc_split, 1)
            V.tensor_tensor(kc_l[:], kc32[:], kc_h[:].bitcast(F32), ALU.subtract).then_inc(kc_split, 1)

            def cmp_scores(r):
                dview = dmat[:, :, 30 + 8 * r - NC + 1:30 + 8 * r + 1][:, :, ::-1]
                if r:
                    dve.wait_ge(c_exp, r)
                ps = result(dve, ("cs", r))[:, 0:H * 32].rearrange("p (j g c) -> p g j c", j=HG, g=G)
                emptied(V.tensor_tensor(c_t[:].rearrange("p (g j) c -> p g j c", g=G), ps[:, :, :, 0:NC],
                                        dview.rearrange("p (g j) c -> p g j c", g=G), ALU.add), ("cs", r))
                stored(dve, ("cs", r))
                V.tensor_reduce(c_m[:, 0, :], c_t[:], AX.X, ALU.min).then_inc(c_min, 1)
                dve.wait_ge(c_min, r + 1)
                V.tensor_tensor(c_t[:], c_t[:], c_m[:, 0, :].unsqueeze(2).to_broadcast([P, H, NC]), ALU.subtract).then_inc(c_sub, 1)

            sel = [0]

            def step(ins):
                sel[0] += 1
                ins.then_inc(c_link, 1)
                dve.wait_ge(c_link, sel[0])

            def cmp_probs(r):
                dve.wait_ge(c_exp, r + 1)
                pr, pg = c_p[:, r % 2], c_g[:, r % 2]
                step(V.tensor_reduce(c_m[:, 1, :], pr[:, :, 0:NC], AX.X, ALU.add))
                step(V.reciprocal(c_m[:, 2, :], c_m[:, 1, :]))
                if r == 0:
                    step(V.tensor_scalar(c_m[:, 2, :], c_m[:, 2, :], rowvalid, None, ALU.mult))
                step(V.tensor_tensor(pr[:, :, 0:NC], pr[:, :, 0:NC], c_m[:, 2, :].unsqueeze(2).to_broadcast([P, H, NC]), ALU.mult))
                if r >= 2:
                    ct_read(r - 2)
                V.tensor_tensor(pg[:, :, 0:NC], pr[:, :, 0:NC], gate[:, r, :, 0].unsqueeze(2).to_broadcast([P, H, NC]), ALU.mult).then_inc(c_pready, 1)
                if r < 2:
                    return
                step(V.tensor_reduce(c_s[:, :, 1:1 + NC], pr.rearrange("p (g j) c -> p g c j", g=G)[:, :, 0:NC, :], AX.X, ALU.add))
                row = c_s[:].ap[0]
                win = bass.AP(c_s[:].tensor, c_s[:].offset, [list(row), [40, G], [4, NB], [1, 5]])
                step(V.tensor_reduce(c_i[:], win, AX.X, ALU.add))
                step(V.tensor_tensor(c_i[:], c_i[:], scoreadd[:, r - 2, :].unsqueeze(1).to_broadcast([P, G, NB]), ALU.add))
                for g in range(G):
                    step(V.max(c_8[:, g, :], c_i[:, g, :]))
                for g in range(G):
                    step(V.max_index(c_x[:, g, :], c_8[:, g, :], c_i[:, g, :]))
                step(V.tensor_copy(c_f[:], c_x[:]))
                for g in range(G):
                    step(V.tensor_tensor(c_e[:, g], iota8.unsqueeze(2).to_broadcast([P, NB, TOPK]),
                                         c_f[:, g, 0:TOPK].unsqueeze(1).to_broadcast([P, NB, TOPK]), ALU.is_equal))
                step(V.tensor_reduce(c_k[:], c_e[:], AX.X, ALU.max))
                V.tensor_scalar(c_k[:], c_k[:], -BIG, BIG, ALU.mult, ALU.add).then_inc(c_pready, 1)

            def ct_read(r):
                ps = result(dve, ("ct", r))
                ins = V.tensor_copy(pct[:, :, P * r:P * r + P], ps[:, 0:2 * P].rearrange("p (g t) -> p g t", g=G))
                if r >= 2:
                    ins = V.tensor_copy(maskT[:, r - 2, :], ps[0:2 * NB, 2 * P:3 * P])
                emptied(ins, ("ct", r))

            for t in (c_p, c_g, c_s):
                step(V.memset(t[:], 0.0))
            svd = [sv[:, r] for r in range(RT)]

            def sb_values(i):
                values(("sv", i), i % 2, [sv[:, r, 2 * P * (i // 2):2 * P * (i // 2) + 2 * P] for r in range(RT)], 2 * P)

            sb_values(0)
            sb_values(1)
            cmp_scores(0)
            sb_values(2)
            sb_values(3)
            cmp_probs(0)
            cmp_scores(1)
            for i in range(8):
                p, qk = divmod(i, 2)
                d_h, d_l = (sk_h, sk_l) if qk else (sq_h, sq_l)
                evac(("pan", P_SQK + i), 1.0 if qk else DH ** -0.5, d_l[:, p], d_h[:, p])
                if i == 1:
                    cmp_probs(1)
                    cmp_scores(2)
                if i == 3:
                    cmp_probs(2)
                    cmp_scores(3)
                if i == 5:
                    cmp_probs(3)
            for r in (2, 3):
                ct_read(r)

            def gate_logit(i):
                if i == GM_SB:
                    stick_pv_done(dve, H - 1)
                emptied(V.tensor_tensor(gate_tile(i), result(dve, ("gm", i))[:], rstd_b[:], ALU.mult), ("gm", i))

            def o_low(name, hi, lo, n):
                ps = result(dve, name)
                dve.wait_ge(o_hi, n + 1)
                emptied(V.tensor_tensor(lo, ps[:], hi.bitcast(F32), ALU.subtract), name)

            for h in range(H):
                w, b = ew[h % 2], 3 * (h % 2)
                if h >= 2:
                    stick_pv_done(dve, h - 2)
                for i, lo, hi in SB_A:
                    result(dve, ("z", h, i))
                    V.tensor_scalar(w[:, lo:hi], bank[b + i][:, 0:hi - lo], 40.0, None, ALU.min).then_inc(zc, 1)
                if h % 2 == 1 and h >= 3:
                    o_low(("osb", (h - 3) // 2), sq_h[:, (h - 3) // 2], sq_l[:, (h - 3) // 2], (h - 3) // 2)
                if h % 2 == 0 and h:
                    gate_logit(h // 2)
                dve.wait_ge(zl, h + 1)
                for i, lo, hi in SB_A:
                    V.tensor_tensor(w[:, lo:hi], bank[b + i][:, 0:hi - lo], w[:, lo:hi], ALU.max).then_inc(zs, 1)
                if h == 0:
                    gate_logit(0)
                dve.wait_ge(zh, h + 1)
                V.tensor_tensor(sp_l[h % 2][:], w[:], sp_h[h % 2][:].bitcast(F32), ALU.subtract).then_inc(zlo, 1)
            gate_logit(GM_SB)
            o_low(("osb", PAIRS - 1), sq_h[:, PAIRS - 1], sq_l[:, PAIRS - 1], PAIRS - 1)

            for i in range(UNITS + 5):
                if i < UNITS:
                    p, br, g, r, run = unit(i)
                    n = P * (r + 1)
                    ps = result(dve, ("s", i))
                    if i % (UNITS // PAIRS) == 0:
                        dve.wait_ge(hank_in[p], 16)
                    if i >= 4:
                        result(dve, ("t", i - 4))
                    emptied(V.tensor_tensor_reduce(ns[i % 4][:, 0:n], ps[:, 0:n], hank[:, p, g, 0:n][:, ::-1], 1.0, 3.0e38,
                                                   ALU.add, ALU.min, nmin[:, i % 4:i % 4 + 1]), ("s", i))
                u = i - 1
                if 0 <= u < UNITS:
                    p, br, g, r, run = unit(u)
                    n = P * (r + 1)
                    dve.wait_ge(s_exp, u + 1)
                    V.reciprocal(rec[:, u % 4:u % 4 + 1], rsum[:, u % 4:u % 4 + 1]).then_inc(s_rec, 1)
                    dve.wait_ge(s_rec, u + 1)
                    V.tensor_scalar(ns[u % 4][:, 0:n], ns[u % 4][:, 0:n], rec[:, u % 4:u % 4 + 1],
                                    gate[:, r, g * HG + p, 2 - br:3 - br], ALU.mult, ALU.mult).then_inc(s_nrm, 1)
                if i % 10 == 3:
                    gate_logit(GM_SB + 1 + i // 10)
                if i >= 16 and i % 16 == 4:
                    p = i // 16 - 1
                    o_low(("ons", p), qn_h[:, p], qn_l[:, p], PAIRS + p)
            for i in range(GM_IN_ATT, 16):
                gate_logit(i)
            for n in range(KT):
                a, b = mx[2 * (n % 2)], mx[2 * (n % 2) + 1]
                dve.wait_ge(sig_done, 2 * n + 2)
                if n >= 2:
                    dve.wait_ge(m_lo, n - 1)
                for i, t in ((0, a), (1, b)):
                    ps = result(dve, (f"up{i}", n))
                    ins = V.tensor_tensor(t[:], ps[:], gate_tile(n + 8 * i), ALU.mult)
                    emptied(ins, (f"up{i}", n))
                stored(dve, ("up0", n))
                stored(dve, ("up1", n))
                V.tensor_tensor(a[:], a[:], b[:], ALU.add).then_inc(mxs, 1)
                dve.wait_ge(m_hi, n + 1)
                V.tensor_tensor(hl[:, n], a[:], hh[:, n].bitcast(F32), ALU.subtract).then_inc(m_lo, 1)
            dve.wait_ge(xres_in, 16)

            def add_sq(n, sq, acc, got, done):
                dve.wait_ge(got, n + 1)
                if n == 0:
                    V.tensor_copy(acc, sq).then_inc(done, 1)
                else:
                    dve.wait_ge(done, n)
                    V.tensor_tensor(acc, acc, sq, ALU.add).then_inc(done, 1)

            for n in range(KT):
                ps = result(dve, ("out", n))
                ins = V.tensor_tensor(x_res[:, n], ps[:], x_res[:, n], ALU.add)
                emptied(ins, ("out", n))
                add_sq(n, tmp[:, n % 2], mx[0][:], x_sq, x_ss)
                dve.wait_ge(h2hi, n + 1)
                V.scalar_tensor_tensor(out=h2l[:, n], in0=x_res[:, n], scalar=nrm[:, 1, n:n + 1], in1=h2h[:, n].bitcast(F32),
                                       op0=ALU.mult, op1=ALU.subtract).then_inc(h2lo, 1)
            dve.wait_ge(rs2, 1)
            def hidden_tile(name, n, nr, row, peeled=False):
                t = tmp[:, n % 2]
                ps = result(dve, name)
                if not (peeled and n < 2):
                    dve.wait_ge(r_lo, nr - 1)
                V.tensor_scalar(t, ps[:], 0.0, None, ALU.max).then_inc(r_pos, 1)
                dve.wait_ge(r_pos, nr + 1)
                emptied(V.tensor_tensor(t, ps[:], t, ALU.mult), name)
                stored(dve, name)
                V.tensor_tensor(t, t, rstd_b[:], ALU.mult).then_inc(r_sc, 1)
                dve.wait_ge(r_hi, nr + 1)
                V.tensor_tensor(r_l[:, row], t, r_h[:, row].bitcast(F32), ALU.subtract).then_inc(r_lo, 1)

            def add_product(name, n):
                ps = result(dve, name)
                emptied(V.tensor_tensor(x_res[:, n], ps[:], x_res[:, n], ALU.add), name)

            for n in range(8):
                hidden_tile(("ff", 0, n), n, n, n, peeled=True)
            with dve.Fori(0, QF - 1) as q:
                with dve.Fori(0, 2) as i:
                    for n in range(RING):
                        hidden_tile(ff_use(1, n, q, i), n, 8 + n + 8 * q + RING * i, (q + 1) % 2 * 8 + n + RING * i)
                with dve.Fori(0, 2) as i:
                    for n in range(RING):
                        add_product(ff_use(2, n, q, i), n + RING * i)
            for n in range(8):
                add_product(("ff", 7, n), n)
                add_sq(n, fin_sq[:, n % 2], fin_ss[:], y_sq, y_ss)
            dve.wait_ge(rs3, 1)
            for n in range(KT):
                V.scalar_tensor_tensor(out=x_res[:, n], in0=x_res[:, n], scalar=nrm[:, 2, n:n + 1], in1=tmp[:, 0],
                                       op0=ALU.mult, op1=ALU.mult).then_inc(y_fin, 1)

        @block.tensor
        def _(pe_):
            M = nc.tensor.matmul

            def three(out, lh, ll, rh, rl, start, stop, **kw):
                M(out, ll, rh, start=start, stop=False, **kw)
                M(out, lh, rl, start=False, stop=False, **kw)
                return M(out, lh, rh, start=False, stop=stop, **kw)

            def panel(p, name, xh, xl, first=0, last=24, ready=None, more=0, row=0):
                s = p % RING
                b = bank[where(name)[0]]
                for m in range(first, last):
                    k, a = divmod(m, 3)
                    if m == 0:
                        claim(pe_, name)
                        pe_.wait_ge(w_lo, p + 1 + more)
                    if ready and a == 0:
                        pe_.wait_ge(ready, k + 1)
                    lhs = (wlo if a == 0 else whi)[:, s, k, :]
                    ins = M(b[:], lhs, (xl if a == 1 else xh)[:, row + k, :], start=(m == 0), stop=(m == 23))
                    if m == 23:
                        filled(ins, name)

            def value_panels(p, names):
                pe_.wait_ge(w_lo, p + 2)
                s = p % RING
                for i, name in enumerate(names):
                    if name is None:
                        continue
                    claim(pe_, name)
                    b = bank[USE[name][0]]
                    for a in range(2):
                        r = 2 * i + a
                        for k in range(KT):
                            lh, ll = hh[:, k, P * r:P * r + P], hl[:, k, P * r:P * r + P]
                            o = b[:, 2 * P * a:2 * P * a + 2 * P]
                            ins = three(o, lh, ll, whi[:, s:s + 2, k, :], wlo[:, s:s + 2, k, :], k == 0, k == KT - 1)
                    filled(ins, name)

            panel(0, ("pan", 0), hh, hl, ready=h_lo)
            panel(1, ("pan", 1), hh, hl)
            value_panels(P_V, [("v", 0)])
            b = claim(pe_, "rms")
            pe_.wait_ge(set_done, 4)
            pe_.wait_ge(sqs_done, KT)
            filled(M(b[:], ones[:], sqs[:], start=True, stop=True), "rms")
            value_panels(P_V, [None, ("v", 1)])
            pe_.wait_ge(cst_in, 16 * 5)
            for i in range(2):
                b = claim(pe_, f"vec{i}")
                filled(M(b[0:H, :], relx[:], oneh[:, T * i:T * i + T], start=True, stop=True), f"vec{i}")
            b = claim(pe_, "rcol")
            pe_.wait_ge(rst, 1)
            for r in range(RT):
                ins = nc.tensor.transpose(b[:, P * r:P * r + P], rstd_b[:, P * r:P * r + P], ident[:])
            filled(ins, "rcol")
            b = claim(pe_, "gn")
            pe_.wait_ge(gn_split, 2)
            for k in range(KT):
                ins = three(b[0:3 * H, :], gn_h[:, k, :], gn_l[:, k, :], hh[:, k, :], hl[:, k, :], k == 0, k == KT - 1)
            filled(ins, "gn")
            panel(4, ("pan", 4), hh, hl)
            b = claim(pe_, "gnT")
            stored(pe_, "gn")
            for r in range(RT):
                ins = nc.tensor.transpose(b[:, 3 * H * r:3 * H * r + 3 * H], gsb[:, P * r:P * r + P], ident[0:3 * H, 0:3 * H])
            filled(ins, "gnT")
            panel(5, ("pan", 5), hh, hl)
            b = claim(pe_, "dt")
            pe_.wait_ge(dt_in, 16)
            for h in range(H):
                ins = nc.tensor.transpose(b[:, 56 * h:56 * h + 55], dts[:, h, :], ident[0:55, 0:55])
            filled(ins, "dt")

            def hidden(i):
                b = claim(pe_, ("hid", i))
                pe_.wait_ge(bm_done, 2 + 2 * (i + 1))
                pe_.wait_ge(cmp_in, 16 * 7)
                for m in range(2):
                    for c in range(CI):
                        ins = M(b[:, 64 * m:64 * m + G * NC], w1s[i][:, c, P * m:P * m + P], bm[i][:, c, :], start=(c == 0), stop=(c == CI - 1))
                filled(ins, ("hid", i))

            hidden(0)
            panel(6, ("pan", 6), hh, hl)
            hidden(1)
            panel(7, ("pan", 7), hh, hl)
            panel(8, ("pan", 8), hh, hl)
            b = claim(pe_, "kcvc")
            for i in range(2):
                stored(pe_, ("hid", i))
            for m in range(2):
                M(b[:, 0:64], w2k[:, m].rearrange("p a d -> p (a d)"), hidTk[:, m].rearrange("p g c -> p (g c)"),
                  start=(m == 0), stop=(m == 1))
            for g in range(G):
                for m in range(2):
                    ins = M(b[:, 64 + 64 * g:128 + 64 * g],
                            hidTv[:, m, g].rearrange("p j c -> p (j c)"), w2v[:, m, :],
                            start=(m == 0), stop=(m == 1))
            filled(ins, "kcvc")
            panel(9, ("pan", 9), hh, hl)

            def cmp_scores(r):
                pe_.wait_ge(kc_split, 2)
                pe_.wait_ge(t_lo, 6)
                b = claim(pe_, ("cs", r))
                for j in range(HG):
                    ins = three(b[:, 64 * j:64 * j + 64], qn_h[:, j, P * r:P * r + P], qn_l[:, j, P * r:P * r + P],
                                kc_h[:], kc_l[:], True, True)
                filled(ins, ("cs", r))

            def cmp_transpose(r):
                b = claim(pe_, ("ct", r))
                pe_.wait_ge(c_pready, [1, 2, 4, 6][r])
                for g in range(G):
                    ins = nc.tensor.transpose(b[:, P * g:P * g + P], c_g[:, r % 2, HG * g:HG * g + HG, :].rearrange("p j c -> p (j c)"), ident[:])
                if r >= 2:
                    ins = nc.tensor.transpose(b[0:2 * NB, 2 * P:3 * P], c_k[:].rearrange("p g n -> p (g n)"), ident[:])
                filled(ins, ("ct", r))

            value_panels(P_SV, [("sv", 0), ("sv", 1)])
            cmp_scores(0)
            value_panels(P_SV + 2, [("sv", 2), ("sv", 3)])
            cmp_scores(1)
            for i in range(8):
                panel(P_SQK + i, ("pan", P_SQK + i), hh, hl)
                if i in (0, 2, 4, 7):
                    cmp_transpose(i // 2)
                if i in (1, 3):
                    cmp_scores(2 + i // 2)

            def gate_products(first, count):
                while count:
                    i, m = divmod(first, 24)
                    n = min(count, 24 - m)
                    panel(P_GM + i, ("gm", i), hh, hl, m, m + n)
                    first, count = first + n, count - n

            def logits(h):
                p, a = h // 2, slice(64 * (h % 2), 64 * (h % 2) + 64)
                b = 3 * (h % 2)
                for i in range(3):
                    claim(pe_, ("z", h, i))
                pe_.wait_ge(t_lo, 6 + 2 * p + 2)
                for k in (0, 1, 3, 2):
                    o = bank[b + KOFF[k] // T][:, KOFF[k] % T:KOFF[k] % T + KLEN[k]]
                    kk = slice(P * k, P * k + P)
                    three(o, sk_h[a, p, kk], sk_l[a, p, kk], sq_h[a, p, P * k:T], sq_l[a, p, P * k:T],
                          k != 3, False, skip_group_check=True)
                    ins = M(o[:, 0:P], ident_bf[:], diag_bf[:], start=False, stop=False, skip_group_check=True)
                    if k != 1:
                        filled(ins, ("z", h, KOFF[k] // T))

            def stick_sums(h):
                b = 3 * (h % 2)
                pe_.wait_ge(zlo, h + 1)
                for k in range(RT):
                    for j in range(k, RT):
                        c = KOFF[k] % T + P * (j - k)
                        o = bank[b + KOFF[k] // T][:, c:c + KLEN[j]]
                        w = negtri if j == k else negones
                        for part in (sp_l, sp_h):
                            ins = M(o, w[:], part[h % 2][:, KOFF[j]:KOFF[j] + KLEN[j]], start=False, stop=False, skip_group_check=True)
                ins.then_inc(c_acc, 1)

            def stick_pv(h):
                p, half = divmod(h, 2)
                for i in range(3):
                    stored(pe_, ("z", h, i))
                if half == 0:
                    claim(pe_, ("osb", p))
                o = bank[USE[("osb", p)][0]]
                for k in range(RT):
                    ins = M(o[64 * half:64 * half + 64, P * k:T], sv[:, k, DH * h:DH * h + DH],
                            ew[h % 2][:, KOFF[k]:KOFF[k] + KLEN[k]], start=(k == 0), stop=(k == RT - 1), skip_group_check=True)
                if half == 1:
                    filled(ins, ("osb", p))
                else:
                    ins.then_inc(pv_sb, 1)

            pe_.wait_ge(cast_done, 5)
            stored(pe_, ("sv", 2))
            stored(pe_, ("sv", 3))
            logits(0)
            gate_done = 0
            for h in range(H):
                gate_products(gate_done, SB_BEFORE[h])
                gate_done += SB_BEFORE[h]
                if h + 1 < H:
                    logits(h + 1)
                if h:
                    stick_pv(h - 1)
                gate_products(gate_done, SB_BEHIND[h])
                gate_done += SB_BEHIND[h]
                stick_sums(h)
            def scores(u):
                p, br, g, r, run = unit(u)
                a, n = slice(64 * g, 64 * g + 64), P * (r + 1)
                b = bank[USE[("s", u)][0]]
                claim(pe_, ("s", u))
                masked = br == 1 and r >= 2
                ins = three(b[:, 0:n], qn_h[a, p, P * r:P * r + P], qn_l[a, p, P * r:P * r + P],
                            kn_h[a, br, 0:n], kn_l[a, br, 0:n], True, not masked)
                if masked:
                    stored(pe_, ("ct", r))
                    ins = M(b[:, 0:n], maskT[:, r - 2, :], blk_bf[:, g, 0:n], start=False, stop=True)
                filled(ins, ("s", u))

            scores(0)
            scores(1)
            stick_pv(H - 1)

            def turn(u):
                p, br, g, r, run = unit(u)
                b = bank[USE[("t", u)][0]]
                claim(pe_, ("t", u))
                pe_.wait_ge(s_nrm, u + 1)
                for k in range(r + 1):
                    ins = nc.tensor.transpose(b[:, P * k:P * k + P], ns[u % 4][:, P * k:P * k + P], ident[:])
                filled(ins, ("t", u))

            def sparse_pv(run):
                p, bg = divmod(run, 2 * G)
                br, g = divmod(bg, G)
                o = bank[USE[("ons", p)][0]]
                if bg == 0:
                    claim(pe_, ("ons", p))
                    stored(pe_, ("ct", RT - 2))
                    stored(pe_, ("ct", RT - 1))
                    for gg in range(G):
                        a = slice(32 * p, 32 * p + 32)
                        M(o[64 * gg:64 * gg + 64, :], vc[a, gg, :], pct[a, gg, :], start=True, stop=False, skip_group_check=True)
                stored(pe_, ("t", RT * run + RT - 2))
                stored(pe_, ("t", RT * run + RT - 1))
                for k in range(RT):
                    ins = M(o[64 * g:64 * g + 64, P * k:T], nv[:, k, 1 - br, 64 * g:64 * g + 64], pt[run % 2][:, k, P * k:T],
                            start=False, stop=(k == RT - 1), skip_group_check=True)
                if bg == 2 * G - 1:
                    filled(ins, ("ons", p))
                else:
                    ins.then_inc(s_pv, 1)

            for i in range(UNITS + 5):
                if i < UNITS:
                    if i > 1:
                        scores(i)
                    gate_products(gate_done, NS_PRODUCTS[i])
                    gate_done += NS_PRODUCTS[i]
                if 0 <= i - 2 < UNITS:
                    turn(i - 2)
                u = i - 4
                if 0 <= u < UNITS and u % 4 == 3:
                    sparse_pv(u // 4)
            gate_products(24 * GM_IN_ATT, 24 * (16 - GM_IN_ATT))

            stored(pe_, ("osb", PAIRS - 1))
            stored(pe_, ("ons", PAIRS - 1))
            for n in range(KT):
                p = P_UP + n
                pe_.wait_ge(w_lo, p + 1)
                s = p % RING
                for i, (oh, ol) in enumerate(((qn_h, qn_l), (sq_h, sq_l))):
                    name = (f"up{i}", n)
                    b = claim(pe_, name)
                    for k in range(PAIRS):
                        ins = three(b[:], whi[:, s, 4 * i + k, :], wlo[:, s, 4 * i + k, :], oh[:, k, :], ol[:, k, :], k == 0, k == PAIRS - 1)
                    filled(ins, name)
            for n in range(KT):
                panel(P_OUT + n, ("out", n), hh, hl, ready=None if n else m_lo)
            panel(P_FF, ("ff", 0, 0), h2h, h2l, ready=h2lo)
            b = claim(pe_, "rms2")
            pe_.wait_ge(x_ss, KT)
            filled(M(b[:], ones[:], mx[0][:], start=True, stop=True), "rms2")
            for n in range(1, 8):
                panel(P_FF + n, ("ff", 0, n), h2h, h2l)
            with pe_.Fori(0, QF - 1) as q:
                with pe_.Fori(0, 2) as i:
                    for n in range(RING):
                        panel(P_FF + 8 + n, ff_use(1, n, q, i), h2h, h2l, more=16 * q + RING * i)
                with pe_.Fori(0, 2) as i:
                    for n in range(RING):
                        if n == 0:
                            pe_.wait_ge(r_lo, 8 * q + 8)
                        panel(P_FF + 16 + n, ff_use(2, n, q, i), r_h, r_l, more=16 * q + RING * i, row=q % 2 * 8)
            pe_.wait_ge(r_lo, 8 * QF)
            for n in range(8):
                panel(P_FF + 56 + n, ("ff", 7, n), r_h, r_l, row=(QF - 1) % 2 * 8)
            b = claim(pe_, "rms3")
            pe_.wait_ge(y_ss, KT)
            filled(M(b[:], ones[:], fin_ss[:], start=True, stop=True), "rms3")


def bucket(n):
    exact = BUCKETS // 2
    if n < exact:
        return n
    return min(BUCKETS - 1, exact + int(math.log(n / exact) / math.log(128 / exact) * (BUCKETS - exact)))


def constants():
    onehot = np.zeros((BUCKETS + 1, 2 * T), np.float32)
    for y in range(2 * T):
        d = y - (T - 1)
        if d < 0:
            onehot[BUCKETS, y] = 1.0
        else:
            onehot[bucket(d), y] = -1.0
    cst = np.zeros((P, 1433), np.float32)
    i, j = np.arange(P)[:, None], np.arange(P)[None, :]
    cst[:, 0:P] = np.where(i >= j, -1.0, 0.0)
    cst[:, P:2 * P] = np.where(i >= j, -BIG, 0.0)
    for g in range(G):
        for n in range(NB):
            cst[NB * g + n, 2 * P + T * g + 64 * n:2 * P + T * g + 64 * n + 64] = 1.0
    cst[:, 1280:1408] = np.eye(P)
    for r in range(2):
        own = (P * (r + 2) + np.arange(P)) // 64
        n = np.arange(NB)[None, :]
        add = np.where((n == own[:, None]) | (n == 0), FORCE, np.where(n <= own[:, None], 0.0, -FORCE))
        cst[:, 1408 + NB * r:1408 + NB * r + NB] = add
    cst[:, 1424] = np.arange(P) >= CL - 1
    cst[:, 1425:1433] = np.arange(NB)
    return onehot, cst


def kernel(**inputs):
    import concourse.bacc as bacc
    from concourse.bass_utils import run_bass_kernel_spmd

    a = {k: np.ascontiguousarray(v) for k, v in inputs.items()}
    w_in = a["w_in"][0]
    order = np.concatenate([np.arange(64) + 64 * h for j in range(PAIRS) for h in (j, j + HG)])
    kv = 512

    def cols(m):
        n = m.shape[1] // P
        return m.reshape(KT, P, n, P).transpose(2, 1, 0, 3).reshape(n, P, KT * P)

    def kvc(i):
        return w_in[:, kv + P * i:kv + P * i + P]

    sb = w_in[:, 512 + 768 + 24:512 + 768 + 24 + 1536]
    gates = w_in[:, 512 + 768 + 24 + 1536:]
    up = np.stack([a["w_up_nsa"][0][order], a["w_up_sb"][0]])
    up = up.reshape(2, PAIRS, P, KT, P).transpose(3, 2, 0, 1, 4).reshape(KT, P, KT * P)
    ff1 = cols(a["w_ff1"][0])
    ff2 = [cols(a["w_ff2"][0][D * q:D * q + D]) for q in range(QF)]
    parts = [cols(kvc(0)), cols(kvc(1)), cols(kvc(3)), cols(kvc(5)), cols(kvc(2)), cols(kvc(4)),
             cols(w_in[:, 0:512][:, order]), cols(sb[:, 1024:1536])]
    for p in range(PAIRS):
        parts += [cols(sb[:, P * p:P * p + P]), cols(sb[:, 512 + P * p:512 + P * p + P])]
    parts += [cols(gates), up, cols(a["w_out"][0])]
    for which, q in FF_ORDER:
        parts.append(ff1[8 * q:8 * q + 8] if which == 1 else ff2[q])
    panels = np.concatenate(parts)
    assert panels.shape == (NPANEL, P, KT * P), panels.shape
    w_gn = w_in[:, 1280:1304].reshape(KT, P, 24).transpose(1, 0, 2)
    norms = np.stack([a["norm_attn"][0], a["norm_mlp"][0], a["norm_final"]]).reshape(3, KT, P).transpose(2, 0, 1)
    two = ("cmp_k", "cmp_v")
    pe = np.stack([a[c + "_pe"][0].reshape(CI, P) for c in two]).transpose(2, 0, 1)
    w1 = np.stack([a[c + "_w1"][0].reshape(CI, P, CM).transpose(1, 0, 2) for c in two])
    b1 = np.stack([a[c + "_b1"][0].reshape(2, P).T for c in two]).transpose(1, 0, 2)
    w2 = np.stack([a[c + "_w2"][0].reshape(2, P, DH).transpose(1, 0, 2) for c in two])
    xT = a["x"][0].T.reshape(KT, P, T).transpose(1, 0, 2)
    onehot, cst = constants()
    arrays = {"xT": xT, "panels": panels, "w_gn": w_gn, "norms": norms, "rel_bias": a["rel_bias"], "pe": pe,
              "w1": w1, "b1": b1, "w2": w2, "onehot": onehot, "cst": cst}
    arrays = {"in_" + k: np.ascontiguousarray(v) for k, v in arrays.items()}
    nc = bacc.Bacc("TRN2", target_bir_lowering=False, num_devices=1)
    args = [nc.dram_tensor(k, v.shape, mybir.dt.from_np(v.dtype), kind="ExternalInput").ap() for k, v in arrays.items()]
    args.append(nc.dram_tensor("out_0_dram", (P, KT, T), F32, kind="ExternalOutput").ap())
    block_kernel(nc, *args)
    r = run_bass_kernel_spmd(nc, [arrays], core_ids=[0])
    y = r.results[0]["out_0_dram"]
    return np.ascontiguousarray(y.transpose(1, 0, 2).reshape(D, T).T)[None]
```

```python
import math
from contextlib import ExitStack

import numpy as np

import concourse.bass as bass
from concourse import mybir

F32 = mybir.dt.float32
F32R = mybir.dt.float32r
BF16 = mybir.dt.bfloat16
U32 = mybir.dt.uint32
ALU = mybir.AluOpType
ACT = mybir.ActivationFunctionType
AX = mybir.AxisListType

P = 128
T = 512
D = 1024
KT = D // P
RT = T // P
DH = 64
H = 8
G = 2
HG = H // G
PAIRS = 4
CL, CS = 32, 16
NC = (T - CL) // CS + 1
CM = 256
CI = CL * DH // P
NB = T // 64
TOPK = 4
BUCKETS = 32
FT = 4 * D // P
QF = 4
EPS = 1e-6
ALL = slice(0, P)
GROUP = [slice(0, DH), slice(DH, P)]
HALF = [slice(0, T // 2), slice(T // 2, T)]
BIG = 1e30
FORCE = 1e4

P_CK, P_CV, P_V, P_KS, P_KW, P_QN = 0, 1, 2, 4, 5, 6
P_SV, P_SQK, P_GM = 10, 14, 22
P_UP = P_GM + 16
P_OUT = P_UP + 8
P_FF = P_OUT + 8
FF_ORDER = [(1, 0), (1, 1), (2, 0), (1, 2), (2, 1), (1, 3), (2, 2), (2, 3)]
NPANEL = P_FF + 8 * len(FF_ORDER)
RING = 4

GM_IN_ATT = 12
GM_SB = 4
UNITS = PAIRS * 2 * G * RT
SB_BEFORE = [24, 8] + [12] * 6
SB_BEHIND = [12, 4] + [0] * 6
NS_PRODUCTS = [0, 0, 24] + [3, 1, 3, 3, 3, 1, 3, 3, 3, 1, 2, 3, 3, 1, 3, 3, 3, 1, 2, 3] * 3 + [0]
CMP_TRANSPOSE = [0, 2, 5, 7]


def bank_plan():
    order = [(("pan", 0), 0), (("pan", 1), 1), (("v", 0), 2), ("rms", 5), (("v", 1), 3), ("vec0", 6), ("vec1", 7),
             ("rcol", 4), ("gn", 7), (("pan", 4), 0), ("gnT", 3), (("pan", 5), 1), ("dt", 6),
             (("hid", 0), 5), (("pan", 6), 0), (("hid", 1), 6), (("pan", 7), 1),
             (("pan", 8), 0), ("kcvc", 7), (("pan", 9), 1)]
    sv = [(("sv", i), 2 + i % 2) for i in range(4)]
    cs = [(("cs", r), 4 + r % 2) for r in range(RT)]
    ct = [(("ct", r), 7 - r % 2) for r in range(RT)]
    order += [sv[0], sv[1], cs[0], sv[2], sv[3], cs[1]]
    for i in range(8):
        order.append((("pan", P_SQK + i), i % 2 + (4 if i >= 6 else 0)))
        if i in CMP_TRANSPOSE:
            order.append(ct[CMP_TRANSPOSE.index(i)])
        if i in (1, 3):
            order.append(cs[2 + i // 2])
    order += [(("z", h, i), 3 * (h % 2) + i) for h in range(H) for i in range(3)]
    order += [(("osb", p), 6) for p in range(PAIRS)]
    order += [(("gm", i), 6 if i > GM_SB and i % 2 == 0 else 7) for i in range(16)]
    order += [(("s", u), u % 3) for u in range(UNITS)]
    order += [(("t", u), 3 + u % 2) for u in range(UNITS)]
    order += [(("ons", p), 5) for p in range(PAIRS)]
    for n in range(KT):
        order += [(("up0", n), 2 * (n % 2)), (("up1", n), 2 * (n % 2) + 1)]
    order += [(("out", n), 4 + n % 2) for n in range(KT)]
    order += [("rms2", 6)]
    for s, (which, q) in enumerate(FF_ORDER):
        order += [(("ff", s, n), n % 4 if which == 1 else 4 + n % 2) for n in range(8 if s < 7 else 4)]
    order += [(("end", t, n), 4 * t + n) for t in range(2) for n in range(4)]
    order += [(("rms3", t), t) for t in range(2)]
    seen, use = {}, {}
    for name, b in order:
        assert name not in use, name
        use[name] = (b, seen.get(b, 0))
        seen[b] = seen.get(b, 0) + 1
    return use


USE = bank_plan()


def panel_product(p):
    if P_V <= p < P_V + 2:
        return "v", 1
    if P_SV <= p < P_SV + 4:
        return "sv", (p - P_SV) // 2 * 2 + 1
    if p < P_GM:
        return "pan", p
    if p < P_UP:
        return "gm", p - P_GM
    if p < P_OUT:
        return "up1", p - P_UP
    if p < P_FF:
        return "out", p - P_OUT
    return "ff", (p - P_FF) // 8, (p - P_FF) % 8


def later_use(name, i):
    b, use = USE[name]
    bi, per_i = USE[name[:-1] + (name[-1] + RING,)]
    assert b == bi
    return [b, use + (per_i - use) * i]


def ff_use(stage, n, q, i):
    b, use = USE[("ff", stage, n)]
    bq, per_q = USE[("ff", stage + 2, n)]
    bi, per_i = USE[("ff", stage, n + RING)]
    assert b == bq == bi
    return [b, use + (per_q - use) * q + (per_i - use) * i]


def unit(u):
    run, r = divmod(u, RT)
    p, bg = divmod(run, 2 * G)
    return p, bg // G, bg % G, r, run


def block_kernel(nc, xT, panels, w_gn, norms, rel_bias, pe, w1, b1, w2, onehot, cst, outT):
    with ExitStack() as ctx:
        top = [nc.sbuf_base + (-nc.sbuf_base) % 64]
        fence = ctx.enter_context(nc.sbuf_tensor("arena", [P, (nc.sbuf_usable_end - top[0] - 256) // 4], F32))
        limit = nc.sbuf_usable_end

        def place(name, shape, dt=F32, at=None):
            size = int(np.prod(shape[1:])) * (2 if dt == BF16 else 4)
            size += (-size) % 64
            start = top[0] if at is None else at
            if at is None:
                top[0] += size
            assert start + size <= limit, (name, start + size - limit)
            return nc.alloc_sbuf_tensor_at(name, shape, dt, offset=start)

        def sem(name):
            return ctx.enter_context(nc.semaphore(name))

        wraw = [place(f"wraw{i}", [P, 8, P]) for i in range(RING)]
        whi = place("whi", [P, RING, 8, P], F32R)
        wlo = place("wlo", [P, RING, 8, P], F32R)
        rstd_b = place("rstd_b", [P, T])
        tmp_at = top[0]
        tmp = place("tmp", [P, 2, T])
        ones = place("ones", [P, P])
        nrm = place("nrm", [P, 3, KT])
        epsc = place("epsc", [P, 1])
        onec = place("onec", [P, 1])
        after_kept = top[0]
        hh = place("hh", [P, KT, T], F32R)
        hl = place("hl", [P, KT, T], F32R)
        at_q = top[0]
        qn = [place(f"qn{g}", [P, PAIRS, T], F32R) for g in range(G)]
        kn_h = place("kn_h", [P, 2, T], F32R)
        kn_l = place("kn_l", [P, 2, T], F32R)
        at_sbq = top[0]
        sq_h = place("sq_h", [P, PAIRS, T], F32R)
        sq_l = place("sq_l", [P, PAIRS, T], F32R)
        at_sbk = top[0]
        sk = [place(f"sk{i}", [P, PAIRS, T], F32R) for i in range(2)]
        at_sbv = top[0]
        sv = place("sv", [P, RT, H * DH])
        nv = place("nv", [P, RT, 2, P])
        at_g = top[0]
        hank = place("hank", [P, PAIRS, G, T])
        at_gm = top[0]
        gm = place("gm", [P, GM_IN_ATT, T])
        small = top[0]
        ident = place("ident", [P, P])
        tables = place("tables", [P, 2 * NB + 1 + NB])
        scoreadd = tables[:, 0:2 * NB].rearrange("p (r n) -> p r n", r=2)
        rowvalid = tables[:, 2 * NB:2 * NB + 1]
        iota8 = tables[:, 2 * NB + 1:]
        negtri = place("negtri", [P, P], F32R)
        negones = place("negones", [P, P], F32R)
        ident_bf = place("ident_bf", [P, P], BF16)
        diag_bf = place("diag_bf", [P, P], BF16)
        blk_bf = place("blk_bf", [2 * NB, G, T], BF16)
        rcol = place("rcol", [P, RT])
        gate = place("gate", [P, RT, H, 3])
        sq_odd = [place("sq_odd0", [P, T], F32R), None]
        kc = place("kc", [P, G, 2, 32], F32R)
        vc = place("vc", [P, G, DH])
        maskT = place("maskT", [2 * NB, 2, P], BF16)
        nmin = place("nmin", [P, 4])
        rsum = place("rsum", [P, 4])
        rec = place("rec", [P, 4])
        at_pct = top[0]
        pct = place("pct", [P, G, T])
        ckv = place("ckv", [P, 2, T], at=at_pct)
        xs = place("xs", [P, KT, T], at=at_gm)
        x2 = [place(f"x2{i}", [P, G, T], at=at_gm + 4096 * i) for i in range(2)]
        bm = [place(f"bm{i}", [P, CI, G * NC], at=at_gm + 8192 + 4096 * i) for i in range(2)]
        oneh = place("oneh", [BUCKETS + 1, 2 * T], at=at_gm + 16384)
        vec = place("vec", [H, 2 * T], at=at_gm + 20480)
        gsb = place("gsb", [3 * H, T], at=at_gm + 16384)
        hidTk = place("hidTk", [P, 2, G, 32], at=at_gm + 18432)
        hidTv = place("hidTv", [P, 2, G, 4, 32], at=at_gm + 18944)
        kc32 = place("kc32", [P, G, 32], at=at_gm + 20992)
        dmat = place("dmat", [P, H, 56], at=at_gm + 22528)
        c_t = place("c_t", [P, H, NC], at=at_gm + 8192)
        c_p = place("c_p", [P, 2, H, 32], at=at_gm + 9216)
        c_g = place("c_g", [P, 2, H, 32], at=at_gm + 11264)
        c_m = place("c_m", [P, 4, H], at=at_gm + 13312)
        c_s = place("c_s", [P, G, 40], at=at_gm + 13440)
        c_i = place("c_i", [P, G, NB], at=at_gm + 13760)
        c_8 = place("c_8", [P, G, NB], at=at_gm + 13824)
        c_x = place("c_x", [P, G, NB], U32, at=at_gm + 13888)
        c_f = place("c_f", [P, G, NB], at=at_gm + 13952)
        c_e = place("c_e", [P, G, NB, TOPK], at=at_gm + 14016)
        c_k = place("c_k", [P, G, NB], at=at_gm + 14272)
        w1s = [place("w1k", [P, CI, CM], at=at_g), place("w1v", [P, CI, CM], at=at_sbk)]
        sqt = place("sqt", [P, 2, T], at=at_sbq)
        sqs = place("sqs", [P, T], at=at_sbq + 4096)
        dts = place("dts", [55, H, P], at=at_sbq + 6144)
        relx = place("relx", [BUCKETS + 1, H], at=at_sbq + 10240)
        pes = place("pes", [P, 2, CI], at=at_sbq + 10304)
        b1s = place("b1s", [P, 2, 2], at=at_sbq + 10496)
        w2k = place("w2k", [P, 2, 2, DH], at=at_sbq + 12544)
        w2v = place("w2v", [P, 2, DH], at=at_sbq + 13568)
        cstb = place("cstb", [P, 2 * P + 2 * T], at=at_sbv)
        gns = place("gns", [P, KT, 3 * H], at=at_sbv + 5632)
        gn_h = place("gn_h", [P, KT, 3 * H], F32R, at=at_sbv + 6400)
        gn_l = place("gn_l", [P, KT, 3 * H], F32R, at=at_sbv + 7168)
        kd1 = place("kd1", [P, 2, T], F32R, at=tmp_at)
        sq_odd[1] = place("sq_odd1", [P, T], F32R, at=tmp_at)
        KOFF = [0, T, 2 * T, T + 3 * P]
        KLEN = [T - P * k for k in range(RT)]
        SBW = 2 * T + 2 * P
        behind_gm = at_gm + 2048 * GM_SB
        ew = [place(f"ew{i}", [P, SBW], at=at_g + 5120 * i) for i in range(2)]
        sp_h = [place(f"sp_h{i}", [P, SBW], F32R, at=(at_g + 10240, behind_gm)[i]) for i in range(2)]
        sp_l = [place(f"sp_l{i}", [P, SBW], F32R, at=behind_gm + 5120 * (i + 1)) for i in range(2)]
        ns = [place(f"ns{i}", [P, T], at=at_sbk + 2048 * i) for i in range(4)]
        pt = [place(f"pt{i}", [P, RT, T], at=at_sbk + 8192 + 8192 * i) for i in range(2)]
        gm2 = place("gm2", [P, 16 - GM_IN_ATT, T], at=at_g)
        mx = [place(f"mx{i}", [P, T], at=at_sbk + 16384 + 2048 * i) for i in range(4)]
        x_res = place("x_res", [P, KT, T], at=at_sbk)
        h2h = place("h2h", [P, KT, T], F32R, at=at_q)
        h2l = place("h2l", [P, KT, T], F32R, at=at_q + 16384)
        r_h = place("r_h", [P, 2 * 8, T], F32R, at=at_sbv)
        r_l = place("r_l", [P, 2 * 8, T], F32R, at=at_sbv + 32768)
        fin_sq = place("fin_sq", [P, 2, T], at=after_kept)
        fin_ss = place("fin_ss", [P, T], at=after_kept + 4096)

        bank = [ctx.enter_context(nc.psum_tensor(f"bank{i}", [P, T], F32)) for i in range(8)]
        full = [sem(f"bank{i}_full") for i in range(8)]
        free = [sem(f"bank{i}_free") for i in range(8)]

        def where(name):
            return name if isinstance(name, list) else USE[name]

        def claim(eng, name):
            b, n = where(name)
            if not (isinstance(n, int) and n == 0):
                eng.wait_ge(free[b], n)
            return bank[b]

        def filled(ins, name):
            ins.then_inc(full[where(name)[0]], 1)

        def result(eng, name):
            b, n = where(name)
            eng.wait_ge(full[b], n + 1)
            return bank[b]

        def emptied(ins, name):
            ins.then_inc(free[where(name)[0]], 1)

        def stored(eng, name):
            b, n = where(name)
            eng.wait_ge(free[b], n + 1)

        x_in = [sem(f"x_in{i}") for i in range(KT)]
        small_in, table_in, cst_in, gn_in, cmp_in = sem("norms_in"), sem("bias_table_in"), sem("constants_in"), sem("gate_weights_in"), sem("cmp_weights_in")
        vec_out, dt_in, x2_in = sem("bias_out"), sem("bias_rows_in"), [sem("cmp_k_tokens_in"), sem("cmp_v_tokens_in")]
        hank_in, xres_in, out_sem = [sem(f"bias_in{i}") for i in range(PAIRS)], sem("residual_in"), sem("out_written")
        w_in = [sem(f"panel_in{i}") for i in range(RING)]
        w_hi, w_lo = sem("panel_hi"), sem("panel_lo")
        first_in, first_hi, first_lo = sem("first_half_panel_in"), sem("first_half_panel_hi"), sem("first_half_panel_lo")
        set_done, cast_done = sem("memsets"), sem("const_casts")
        h_hi, h_lo, sq_done, sqs_done = sem("h_hi"), sem("h_lo"), sem("sq_done"), sem("sqsum_done")
        rst, gn_split, gate_st = sem("rstd_ready"), sem("gate_weights_split"), sem("branch_gate_steps")
        t_hi, t_lo = sem("tmp_hi"), sem("tmp_lo")
        bm_done, kc_cp, kc_split = sem("block_matrices"), sem("kc_copied"), sem("kc_split")
        c_bias, c_min, c_sub, c_exp, c_pready, c_link = sem("cmp_bias"), sem("cmp_min"), sem("cmp_less_min"), sem("cmp_exp"), sem("cmp_probs"), sem("cmp_links")
        q_twice, k_twice = sem("stick_queries_twice"), sem("keys_twice")
        zc, ze, zl, zs = sem("z_clamped"), sem("z_exp"), sem("z_log"), sem("softplus")
        zh, zlo, c_acc, pv_sb = sem("softplus_hi"), sem("softplus_lo"), sem("stick_sums"), sem("stick_pv_first_half")
        o_hi = sem("mixer_out_hi")
        s_exp, s_rec, s_nrm, s_pv = sem("scores_exp"), sem("sum_reciprocal"), sem("probs_ready"), sem("sparse_pv")
        sig_done, mxs, m_hi, m_lo = sem("gates"), sem("mixed"), sem("mixed_hi"), sem("mixed_lo")
        x_sq, x_ss, h2hi, h2lo, rs2 = sem("x_squared"), sem("x_sqsum"), sem("h2_hi"), sem("h2_lo"), sem("rstd2_ready")
        r_pos, r_sc, r_hi, r_lo = sem("relu"), sem("relu_squared"), sem("r_hi"), sem("r_lo")
        y_sq, y_ss, rs3, y_fin = sem("y_squared"), sem("y_sqsum"), sem("rstd3_ready"), sem("y_final")

        vf = nc.dram_tensor("bias_by_distance", [H, 2 * T], F32, kind="Internal").ap()

        def gate_tile(i):
            return gm[:, i, :] if i < GM_IN_ATT else gm2[:, i - GM_IN_ATT, :]

        SB_A = [(0, 0, T), (1, T, 2 * T), (2, 2 * T, SBW)]

        def stick_pv_done(eng, h):
            if h % 2:
                result(eng, ("osb", h // 2))
            else:
                eng.wait_ge(pv_sb, h // 2 + 1)

        def sparse_pv_done(eng, run):
            p, bg = divmod(run, 2 * G)
            if bg == 2 * G - 1:
                result(eng, ("ons", p))
            else:
                eng.wait_ge(s_pv, (2 * G - 1) * p + bg + 1)

        block = ctx.enter_context(nc.Block())

        @block.sync
        def _(sp):
            def panel(p, i=0):
                if p >= RING:
                    sp.wait_ge(w_lo, p - RING + 1 + RING * i)
                sp.dma_start(wraw[p % RING][:], panels[p + RING * i].rearrange("p (k m) -> p k m", k=8)).then_inc(w_in[p % RING], 16)

            def panel_loop(first, last):
                rounds = (last - first) // RING
                with sp.Fori(0, rounds) as i:
                    for j in range(RING):
                        panel(first + j, i)
                for p in range(first + RING * rounds, last):
                    panel(p)

            for k in range(KT):
                if k < 2:
                    sp.dma_start(wraw[0][:, 4 * k:4 * k + 4], panels[0].rearrange("p (k m) -> p k m", k=8)[:, 4 * k:4 * k + 4]).then_inc([first_in, w_in[0]][k], 16)
                sp.dma_start(xs[:, k, :], xT[:, k, :]).then_inc(x_in[k], 16)
                if k == 3:
                    panel(1)
            panel(2)
            panel(3)
            sp.dma_start(relx[0:BUCKETS, :], rel_bias).then_inc(table_in, 16)
            sp.dma_start(oneh[:], onehot).then_inc(table_in, 16)
            sp.dma_start(ident[:], cst[:, 2 * P + 2 * T:3 * P + 2 * T]).then_inc(table_in, 16)
            sp.dma_start(gns[:], w_gn).then_inc(gn_in, 16)
            sp.dma_start(pes[:], pe).then_inc(cmp_in, 16)
            sp.dma_start(b1s[:], b1).then_inc(cmp_in, 16)
            sp.dma_start(w2k[:, :, 0, :], w2[0]).then_inc(cmp_in, 16)
            sp.dma_start(w2k[:, :, 1, :], w2[0]).then_inc(cmp_in, 16)
            sp.dma_start(w2v[:], w2[1]).then_inc(cmp_in, 16)
            panel(RING)
            panel(RING + 1)
            for i in range(2):
                sp.dma_start(w1s[i][:], w1[i]).then_inc(cmp_in, 16)
            sp.dma_start(cstb[:], cst[:, 0:2 * P + 2 * T]).then_inc(cst_in, 16)
            sp.dma_start(tables[:], cst[:, 3 * P + 2 * T:]).then_inc(cst_in, 16)
            panel_loop(RING + 2, P_GM + GM_SB + 5)
            for q in range(PAIRS):
                stick_pv_done(sp, H - 1 if q else H - 2)
                sp.dma_start(hank[:, q], bass.AP(vf.tensor, 3 * P + 2 * T * q, [[1, P], [HG * 2 * T, G], [1, T]])).then_inc(hank_in[q], 16)
            panel_loop(P_GM + GM_SB + 5, P_UP + 3)
            sparse_pv_done(sp, 4 * PAIRS - 1)
            sp.dma_start(x_res[:], xT).then_inc(xres_in, 16)
            panel_loop(P_UP + 3, NPANEL)
            for t in range(2):
                for n in range(KT):
                    sp.wait_ge(y_fin, KT * t + n + 1)
                    sp.dma_start(outT[:, n, HALF[t]], x_res[:, n, HALF[t]]).then_inc(out_sem, 16)
            sp.wait_ge(out_sem, 16 * 2 * KT)

        @block.gpsimd
        def _(pool):
            def low(p, i=0):
                s = p % RING
                pool.wait_ge(w_hi, p + 1 + RING * i)
                nc.gpsimd.tensor_tensor(wlo[:, s], wraw[s][:], whi[:, s].bitcast(F32), ALU.subtract).then_inc(w_lo, 1)

            for got, done, half in ((first_hi, first_lo, slice(0, 4)), (w_hi, w_lo, slice(4, 8))):
                pool.wait_ge(got, 1)
                nc.gpsimd.tensor_tensor(wlo[:, 0, half], wraw[0][:, half], whi[:, 0, half].bitcast(F32), ALU.subtract).then_inc(done, 1)
            rounds = (NPANEL - 1) // RING
            with pool.Fori(0, rounds) as i:
                for p in range(1, RING + 1):
                    low(p, i)
            for p in range(RING * rounds + 1, NPANEL):
                low(p)

        @block.scalar
        def _(act):
            A = nc.scalar.activation

            def exp_and_ln():
                nc.scalar.preload_act_table_set("natural_log_exp_and_others")

            exp_and_ln()
            act.dma_start(nrm[:], norms).then_inc(small_in, 16)

            def split(p):
                s = p % RING
                act.wait_ge(w_in[s], 16 * (p // RING + 1))
                if p >= RING:
                    result(act, panel_product(p - RING))
                A(whi[:, s], wraw[s][:], ACT.Copy).then_inc(w_hi, 1)

            def split_half(p, half):
                s = p % RING
                if half == 0:
                    act.wait_ge(w_in[s], 16 * (p // RING + 1))
                    result(act, panel_product(p - RING))
                ins = A(whi[:, s, 4 * half:4 * half + 4], wraw[s][:, 4 * half:4 * half + 4], ACT.Copy)
                if half == 1:
                    ins.then_inc(w_hi, 1)

            def split_next(stage, n, q, i):
                p = P_FF + 8 * stage + n + RING
                s = p % RING
                act.wait_ge(w_in[s], 16 * (p // RING + 1) + 16 * (4 * q + i))
                result(act, ff_use(stage, n, q, i))
                A(whi[:, s], wraw[s][:], ACT.Copy).then_inc(w_hi, 1)

            for k in range(KT):
                if k < 2:
                    act.wait_ge([first_in, w_in[0]][k], 16)
                    A(whi[:, 0, 4 * k:4 * k + 4], wraw[0][:, 4 * k:4 * k + 4], ACT.Copy).then_inc([first_hi, w_hi][k], 1)
                if k == 0:
                    act.wait_ge(small_in, 16)
                act.wait_ge(x_in[k], 16)
                A(hh[:, k], xs[:, k], ACT.Copy, scale=nrm[:, 0, k:k + 1]).then_inc(h_hi, 1)
                if k == 5:
                    split(1)
            split(2)
            split(3)
            for k in range(KT):
                if k >= 2:
                    act.wait_ge(sqs_done, k - 1)
                A(sqt[:, k % 2], xs[:, k], ACT.Square).then_inc(sq_done, 1)
            ps = result(act, "rms")
            act.wait_ge(set_done, 4)
            emptied(A(rstd_b[:], ps[:], ACT.Ln, bias=epsc[:], scale=1.0 / D), "rms")
            stored(act, "rms")
            A(rstd_b[:], rstd_b[:], ACT.Exp, scale=-0.5).then_inc(rst, 1)
            act.wait_ge(gn_in, 16)
            A(gn_h[:], gns[:], ACT.Copy).then_inc(gn_split, 1)
            split(4)
            split(5)
            stored(act, "vec0")
            stored(act, "vec1")
            act.dma_start(vf, vec[:]).then_inc(vec_out, 16)
            act.wait_ge(vec_out, 16)
            act.dma_start(dts[:], bass.AP(vf.tensor, 0, [[16, 55], [2 * T, H], [1, P]])).then_inc(dt_in, 16)

            nt = [0]

            def round_tmp(p, *parts):
                stored(act, ("pan", p))
                for a, dst in parts:
                    ins = A(dst, tmp[a, nt[0] % 2], ACT.Copy)
                ins.then_inc(t_hi, 1)
                nt[0] += 1

            def cmp_exp(r):
                act.wait_ge(c_sub, r + 1)
                A(c_p[:, r % 2, :, 0:NC], c_t[:], ACT.Exp, scale=-1.0).then_inc(c_exp, 1)

            for i in range(2):
                stored(act, ("pan", i))
                for g in range(G):
                    src = ckv[64 * g:64 * g + 64, i, :]
                    act.dma_start(x2[i][0:64, g, :], src).then_inc(x2_in[i], 16)
                    act.dma_start(x2[i][64:128, g, 0:T - 1], src[:, 1:T]).then_inc(x2_in[i], 16)
            ps = result(act, "gnT")
            emptied(A(gate[:].rearrange("p r h b -> p (r h b)"), ps[:, 0:RT * 3 * H], ACT.Exp, scale=-1.0), "gnT")
            split(6)
            split(7)
            split(8)
            round_tmp(P_KS, (ALL, kn_h[:, 1]))
            split(9)
            round_tmp(P_KW, (ALL, kn_h[:, 0]))
            for j in range(PAIRS):
                split(P_QN + j + RING)
                round_tmp(P_QN + j, *((GROUP[g], qn[g][GROUP[g], j]) for g in range(G)))
                if j in (0, 1):
                    ps = result(act, ("hid", j))
                    act.wait_ge(bm_done, 2)
                    for m in range(2):
                        src = ps[:, 64 * m:64 * m + G * NC].rearrange("p (g c) -> p g c", g=G)
                        dst = hidTk[:, m, :, 0:NC]
                        if j == 1:
                            dst, src = hidTv[:, m, :, :, 0:NC], src.unsqueeze(2).to_broadcast([P, G, 4, NC])
                        ins = A(dst, src, ACT.Gelu_apprx_tanh, bias=b1s[:, j, m:m + 1])
                    emptied(ins, ("hid", j))
            exp_and_ln()
            act.wait_ge(kc_cp, 1)
            A(kc[:, :, 0], kc32[:], ACT.Copy).then_inc(kc_split, 1)
            split(14)
            split(15)
            cmp_exp(0)
            split(16)
            split(17)
            cmp_exp(1)
            def queries_twice(p):
                for o in range(2):
                    A(sq_odd[p % 2][GROUP[o]], sq_h[GROUP[1], p], ACT.Copy).then_inc(q_twice, 1)
                act.wait_ge(q_twice, 3 * p + 2)
                A(sq_h[GROUP[1], p], sq_h[GROUP[0], p], ACT.Copy).then_inc(q_twice, 1)


            for i in range(8):
                p, qk = divmod(i, 2)
                split(P_SQK + i + RING)
                if qk:
                    round_tmp(P_SQK + i, *((GROUP[o], sk[o][GROUP[o], p]) for o in range(2)))
                else:
                    round_tmp(P_SQK + i, (ALL, sq_h[:, p]))
                if i == 3:
                    act.wait_ge(t_lo, 6 + 1)
                    queries_twice(0)
                if i in (1, 3):
                    cmp_exp(2 + i // 2)

            def stick_weights(h):
                act.wait_ge(c_acc, h + 1)
                act.wait_ge(zlo, 3 * h + 3)
                for i, lo, hi in SB_A:
                    emptied(A(ew[h % 2][:, lo:hi], bank[3 * (h % 2) + i][:, 0:hi - lo], ACT.Exp), ("z", h, i))

            def stick_out_high(p):
                A(sq_h[:, p], result(act, ("osb", p))[:], ACT.Copy).then_inc(o_hi, 1)

            for h in range(H):
                w = ew[h % 2]
                if h % 2 == 1 and h >= 3:
                    stick_out_high((h - 3) // 2)
                for i, lo, hi in SB_A:
                    act.wait_ge(zc, 3 * h + i + 1)
                    A(w[:, lo:hi], w[:, lo:hi], ACT.Exp).then_inc(ze, 1)
                for i, lo, hi in SB_A:
                    act.wait_ge(ze, 3 * h + i + 1)
                    A(w[:, lo:hi], w[:, lo:hi], ACT.Ln, bias=onec[:], scale=1.0).then_inc(zl, 1)
                if h:
                    stick_weights(h - 1)
                for i, lo, hi in SB_A:
                    act.wait_ge(zs, 3 * h + i + 1)
                    A(sp_h[h % 2][:, lo:hi], w[:, lo:hi], ACT.Copy).then_inc(zh, 1)
                if h % 2 == 0 and h // 2 + 1 < PAIRS:
                    act.wait_ge(t_lo, 6 + 8)
                    queries_twice(h // 2 + 1)
                if h == H - 1:
                    for g in range(G):
                        A(kd1[GROUP[g]], kn_h[GROUP[1]], ACT.Copy).then_inc(k_twice, 1)
                    act.wait_ge(k_twice, 2)
                    A(kn_h[GROUP[1]], kn_h[GROUP[0]], ACT.Copy).then_inc(k_twice, 1)
                if h % 2 == 1:
                    split(P_GM + h // 2 + RING)
            stick_weights(H - 1)
            stick_out_high(PAIRS - 1)

            for i in range(UNITS + 5):
                if i < UNITS:
                    n = P * (unit(i)[3] + 1)
                    stored(act, ("s", i))
                    if i >= 4:
                        act.wait_ge(s_rec, i - 3)
                    A(ns[i % 4][:, 0:n], ns[i % 4][:, 0:n], ACT.Exp, scale=-1.0, bias=nmin[:, i % 4:i % 4 + 1],
                      accum_out=rsum[:, i % 4:i % 4 + 1]).then_inc(s_exp, 1)
                if i == 0:
                    split(P_GM + GM_SB + RING)
                if i % 10 in (5, 7) and i < UNITS:
                    split_half(P_GM + GM_SB + 1 + i // 10 + RING, i % 10 // 7)
                u = i - 3
                if 0 <= u < UNITS:
                    r, run = unit(u)[3:]
                    ps = result(act, ("t", u))
                    if run >= 2 and r == 0:
                        sparse_pv_done(act, run - 2)
                    emptied(A(pt[run % 2][:, 0:r + 1, P * r:P * r + P],
                              ps[:, 0:P * (r + 1)].rearrange("p (k t) -> p k t", k=r + 1), ACT.Copy), ("t", u))
                if i >= 16 and i % 16 == 4:
                    p = i // 16 - 1
                    A(qn[0][:, p], result(act, ("ons", p))[:], ACT.Copy).then_inc(o_hi, 1)
            for i in range(16):
                j = i // 2 + 8 * (i % 2)
                if i == 0:
                    split(P_GM + GM_IN_ATT - 1 + RING)
                if i >= 8 and i % 2 == 0:
                    split(P_GM + GM_IN_ATT + (i - 8) // 2 + RING)
                stored(act, ("gm", j))
                A(gate_tile(j), gate_tile(j), ACT.Sigmoid).then_inc(sig_done, 1)
            exp_and_ln()
            for n in range(KT):
                split(P_UP + n + RING)
                act.wait_ge(mxs, n + 1)
                A(hh[:, n], mx[2 * (n % 2)][:], ACT.Copy).then_inc(m_hi, 1)
            for n in range(KT):
                split(P_OUT + n + RING)
                stored(act, ("out", n))
                if n >= 2:
                    act.wait_ge(x_ss, n - 1)
                A(tmp[:, n % 2], x_res[:, n], ACT.Square).then_inc(x_sq, 1)
                A(h2h[:, n], x_res[:, n], ACT.Copy, scale=nrm[:, 1, n:n + 1]).then_inc(h2hi, 1)
            ps = result(act, "rms2")
            emptied(A(rstd_b[:], ps[:], ACT.Ln, bias=epsc[:], scale=1.0 / D), "rms2")
            stored(act, "rms2")
            A(rstd_b[:], rstd_b[:], ACT.Exp, scale=-1.0).then_inc(rs2, 1)
            def hidden_high(n, nr, row):
                act.wait_ge(r_sc, nr + 1)
                A(r_h[:, row], tmp[:, n % 2], ACT.Copy).then_inc(r_hi, 1)

            for n in range(8):
                split(P_FF + n + RING)
                hidden_high(n, n, n)
            with act.Fori(0, QF - 1) as q:
                b, use = USE[("ff", 2, 7)]
                uses = USE[("ff", 4, 7)][1] - use
                act.wait_ge(full[b], use - uses + 1 + uses * q)
                with act.Fori(0, 2) as i:
                    for n in range(RING):
                        split_next(1, n, q, i)
                        hidden_high(n, 8 + n + 8 * q + RING * i, (q + 1) % 2 * 8 + n + RING * i)
                with act.Fori(0, 2) as i:
                    for n in range(RING):
                        split_next(2, n, q, i)
            for n in range(4):
                split(P_FF + 8 * 7 + n + RING)
                stored(act, ("ff", 7, n))
                if n >= 2:
                    act.wait_ge(y_ss, n - 1)
                A(fin_sq[:, n % 2], x_res[:, n], ACT.Square).then_inc(y_sq, 1)
            for t in range(2):
                c = HALF[t]
                for n in range(4):
                    stored(act, ("end", t, n))
                    act.wait_ge(y_ss, 4 * t + n + 3)
                    A(fin_sq[:, n % 2, c], x_res[:, 4 + n, c], ACT.Square).then_inc(y_sq, 1)
                ps = result(act, ("rms3", t))
                if t == 0:
                    act.wait_ge(r_lo, FT)
                emptied(A(tmp[:, 0, c], ps[:, c], ACT.Ln, bias=epsc[:], scale=1.0 / D), ("rms3", t))
                stored(act, ("rms3", t))
                A(tmp[:, 0, c], tmp[:, 0, c], ACT.Exp, scale=-0.5).then_inc(rs3, 1)

        @block.vector
        def _(dve):
            V = nc.vector
            for i, (t, v) in enumerate(((ones, 1.0), (epsc, EPS), (onec, 1.0))):
                V.memset(t[:], v).then_inc(set_done, 1)
            V.memset(relx[BUCKETS:BUCKETS + 1, :], BIG).then_inc(set_done, 1)
            dve.wait_ge(small_in, 16)
            for k in range(KT):
                dve.wait_ge(h_hi, k + 1)
                V.scalar_tensor_tensor(out=hl[:, k], in0=xs[:, k], scalar=nrm[:, 0, k:k + 1], in1=hh[:, k].bitcast(F32),
                                       op0=ALU.mult, op1=ALU.subtract).then_inc(h_lo, 1)
            for k in range(KT):
                dve.wait_ge(sq_done, k + 1)
                if k == 0:
                    V.tensor_copy(sqs[:], sqt[:, 0]).then_inc(sqs_done, 1)
                else:
                    dve.wait_ge(sqs_done, k)
                    V.tensor_tensor(sqs[:], sqs[:], sqt[:, k % 2], ALU.add).then_inc(sqs_done, 1)
            dve.wait_ge(gn_split, 1)
            V.tensor_tensor(gn_l[:], gns[:], gn_h[:].bitcast(F32), ALU.subtract).then_inc(gn_split, 1)
            for i in range(2):
                ps = result(dve, f"vec{i}")
                emptied(V.tensor_copy(vec[:, T * i:T * i + T], ps[0:H, :]), f"vec{i}")
            dve.wait_ge(rst, 1)

            for i in range(2):
                ps = result(dve, ("pan", i))
                emptied(V.tensor_tensor(ckv[:, i], ps[:], rstd_b[:], ALU.mult), ("pan", i))
            ps = result(dve, "rcol")
            ins = V.tensor_copy(rcol[:], ps[:].rearrange("p (r t) -> p r t", r=RT)[:, :, 0])
            emptied(ins, "rcol")
            stored(dve, "rcol")

            def values(name, i, dst, width):
                ps = result(dve, name)
                for a in range(2):
                    r = 2 * i + a
                    ins = V.tensor_scalar(dst[r], ps[:, width * a:width * a + width], rcol[:, r:r + 1], None, ALU.mult)
                emptied(ins, name)

            for i in range(2):
                values(("v", i), i, [nv[:, r].rearrange("p a b -> p (a b)") for r in range(RT)], 2 * P)
            ps = result(dve, "gn")
            ins = V.tensor_tensor(gsb[:], ps[0:3 * H, :], rstd_b[0:3 * H, :], ALU.mult)
            ins.then_inc(gate_st, 1)
            dve.wait_ge(gate_st, 1)
            emptied(V.tensor_scalar(gsb[:], gsb[:], -80.0, None, ALU.max), "gn")
            stored(dve, "gnT")
            V.tensor_scalar(gate[:], gate[:], 1.0, None, ALU.add).then_inc(gate_st, 1)
            dve.wait_ge(gate_st, 2)
            V.reciprocal(gate[:], gate[:]).then_inc(gate_st, 1)
            dve.wait_ge(table_in, 16 * 3)
            dve.wait_ge(cst_in, 16 * 2)
            V.tensor_copy(negtri[:], cstb[:, 0:P]).then_inc(cast_done, 1)
            V.tensor_scalar(negones[:], ident[:], 0.0, -1.0, ALU.mult, ALU.add).then_inc(cast_done, 1)
            V.tensor_copy(diag_bf[:], cstb[:, P:2 * P]).then_inc(cast_done, 1)
            V.tensor_copy(ident_bf[:], ident[:]).then_inc(cast_done, 1)
            V.tensor_copy(blk_bf[:], cstb[0:2 * NB, 2 * P:2 * P + 2 * T].rearrange("p (g t) -> p g t", g=G)).then_inc(cast_done, 1)
            dve.wait_ge(cmp_in, 16 * 7)
            V.memset(hidTk[:], 0.0).then_inc(bm_done, 1)
            V.memset(hidTv[:], 0.0).then_inc(bm_done, 1)
            for i in range(2):
                dve.wait_ge(x2_in[i], 16 * 4)
                for g in range(G):
                    src = x2[i][:, g, :]
                    row = src.ap[0]
                    view = bass.AP(src.tensor, src.offset, [list(row), [2, CI], [CS, NC]])
                    V.tensor_tensor(bm[i][:, :, NC * g:NC * g + NC], view,
                                    pes[:, i, :].unsqueeze(2).to_broadcast([P, CI, NC]), ALU.add).then_inc(bm_done, 1)

            ps = result(dve, "dt")
            emptied(V.tensor_copy(dmat[:, :, 0:55], ps[:, 0:H * 56].rearrange("p (h m) -> p h m", h=H)[:, :, 0:55]), "dt")
            nt = [0]

            def evac(name, scale, *parts):
                i = nt[0]
                nt[0] += 1
                ps = result(dve, name)
                if i >= 2:
                    dve.wait_ge(t_lo, i - 1)
                ins = V.scalar_tensor_tensor(out=tmp[:, i % 2], in0=ps[:], scalar=scale, in1=rstd_b[:],
                                             op0=ALU.mult, op1=ALU.mult)
                emptied(ins, name)
                dve.wait_ge(t_hi, i + 1)
                for a, lo, hi in parts:
                    ins = V.tensor_tensor(lo, tmp[a, i % 2], hi.bitcast(F32), ALU.subtract)
                ins.then_inc(t_lo, 1)

            def evac_queries(j):
                evac(("pan", P_QN + j), -DH ** -0.5, *((GROUP[g], qn[g][GROUP[1 - g], j], qn[g][GROUP[g], j]) for g in range(G)))

            evac(("pan", P_KS), 1.0, (ALL, kn_l[:, 1], kn_h[:, 1]))
            evac(("pan", P_KW), 1.0, (ALL, kn_l[:, 0], kn_h[:, 0]))
            evac_queries(0)
            evac_queries(1)
            evac_queries(2)
            ps = result(dve, "kcvc")
            V.tensor_copy(kc32[:], ps[:, 0:2 * 32].rearrange("p (g c) -> p g c", g=G)).then_inc(kc_cp, 1)
            emptied(V.tensor_copy(vc[:], ps[:, 64:192].rearrange("p (g d) -> p g d", g=G)), "kcvc")
            evac_queries(3)
            dve.wait_ge(kc_split, 1)
            V.tensor_tensor(kc[:, :, 1], kc32[:], kc[:, :, 0].bitcast(F32), ALU.subtract).then_inc(kc_split, 1)

            def cmp_scores(r):
                dview = dmat[:, :, 30 + 8 * r - NC + 1:30 + 8 * r + 1][:, :, ::-1]
                if r:
                    dve.wait_ge(c_exp, r)
                ps = result(dve, ("cs", r))[:].rearrange("p (h a c) -> p h a c", h=H, a=2)
                V.tensor_tensor(c_t[:], ps[:, :, 0, 0:NC], dview, ALU.add).then_inc(c_bias, 1)
                dve.wait_ge(c_bias, r + 1)
                emptied(V.tensor_tensor(c_t[:], ps[:, :, 1, 0:NC], c_t[:], ALU.add), ("cs", r))
                stored(dve, ("cs", r))
                V.tensor_reduce(c_m[:, 0, :], c_t[:], AX.X, ALU.min).then_inc(c_min, 1)
                dve.wait_ge(c_min, r + 1)
                V.tensor_tensor(c_t[:], c_t[:], c_m[:, 0, :].unsqueeze(2).to_broadcast([P, H, NC]), ALU.subtract).then_inc(c_sub, 1)

            sel = [0]

            def step(ins):
                sel[0] += 1
                ins.then_inc(c_link, 1)
                dve.wait_ge(c_link, sel[0])

            def cmp_probs(r):
                dve.wait_ge(c_exp, r + 1)
                pr, pg = c_p[:, r % 2], c_g[:, r % 2]
                step(V.tensor_reduce(c_m[:, 1, :], pr[:, :, 0:NC], AX.X, ALU.add))
                step(V.reciprocal(c_m[:, 2, :], c_m[:, 1, :]))
                if r == 0:
                    step(V.tensor_scalar(c_m[:, 2, :], c_m[:, 2, :], rowvalid, None, ALU.mult))
                step(V.tensor_tensor(pr[:, :, 0:NC], pr[:, :, 0:NC], c_m[:, 2, :].unsqueeze(2).to_broadcast([P, H, NC]), ALU.mult))
                if r >= 2:
                    ct_read(r - 2)
                V.tensor_tensor(pg[:, :, 0:NC], pr[:, :, 0:NC], gate[:, r, :, 0].unsqueeze(2).to_broadcast([P, H, NC]), ALU.mult).then_inc(c_pready, 1)
                if r < 2:
                    return
                step(V.tensor_reduce(c_s[:, :, 1:1 + NC], pr.rearrange("p (g j) c -> p g c j", g=G)[:, :, 0:NC, :], AX.X, ALU.add))
                row = c_s[:].ap[0]
                win = bass.AP(c_s[:].tensor, c_s[:].offset, [list(row), [40, G], [4, NB], [1, 5]])
                step(V.tensor_reduce(c_i[:], win, AX.X, ALU.add))
                step(V.tensor_tensor(c_i[:], c_i[:], scoreadd[:, r - 2, :].unsqueeze(1).to_broadcast([P, G, NB]), ALU.add))
                for g in range(G):
                    step(V.max(c_8[:, g, :], c_i[:, g, :]))
                for g in range(G):
                    step(V.max_index(c_x[:, g, :], c_8[:, g, :], c_i[:, g, :]))
                step(V.tensor_copy(c_f[:], c_x[:]))
                for g in range(G):
                    step(V.tensor_tensor(c_e[:, g], iota8.unsqueeze(2).to_broadcast([P, NB, TOPK]),
                                         c_f[:, g, 0:TOPK].unsqueeze(1).to_broadcast([P, NB, TOPK]), ALU.is_equal))
                step(V.tensor_reduce(c_k[:], c_e[:], AX.X, ALU.max))
                V.tensor_scalar(c_k[:], c_k[:], -BIG, BIG, ALU.mult, ALU.add).then_inc(c_pready, 1)

            def ct_read(r):
                ps = result(dve, ("ct", r))
                ins = V.tensor_copy(pct[:, :, P * r:P * r + P], ps[:, 0:2 * P].rearrange("p (g t) -> p g t", g=G))
                if r >= 2:
                    ins = V.tensor_copy(maskT[:, r - 2, :], ps[0:2 * NB, 2 * P:3 * P])
                emptied(ins, ("ct", r))

            for t in (c_p, c_g, c_s):
                step(V.memset(t[:], 0.0))
            svd = [sv[:, r] for r in range(RT)]

            def sb_values(i):
                values(("sv", i), i % 2, [sv[:, r, 2 * P * (i // 2):2 * P * (i // 2) + 2 * P] for r in range(RT)], 2 * P)

            sb_values(0)
            sb_values(1)
            cmp_scores(0)
            sb_values(2)
            sb_values(3)
            cmp_probs(0)
            cmp_scores(1)
            for i in range(8):
                p, qk = divmod(i, 2)
                if qk:
                    evac(("pan", P_SQK + i), 1.0, *((GROUP[o], sk[o][GROUP[1 - o], p], sk[o][GROUP[o], p]) for o in range(2)))
                else:
                    evac(("pan", P_SQK + i), DH ** -0.5, (ALL, sq_l[:, p], sq_h[:, p]))
                if i == 1:
                    cmp_probs(1)
                    cmp_scores(2)
                if i == 3:
                    cmp_probs(2)
                    cmp_scores(3)
                if i == 5:
                    ct_read(2)
                    cmp_probs(3)
            ct_read(3)

            def gate_logit(i):
                if i == GM_SB:
                    stick_pv_done(dve, H - 1)
                emptied(V.tensor_tensor(gate_tile(i), result(dve, ("gm", i))[:], rstd_b[:], ALU.mult), ("gm", i))

            def o_low(name, hi, lo, n):
                ps = result(dve, name)
                dve.wait_ge(o_hi, n + 1)
                emptied(V.tensor_tensor(lo, ps[:], hi.bitcast(F32), ALU.subtract), name)

            for h in range(H):
                w, b = ew[h % 2], 3 * (h % 2)
                if h >= 2:
                    stick_pv_done(dve, h - 2)
                for i, lo, hi in SB_A:
                    result(dve, ("z", h, i))
                    V.tensor_scalar(w[:, lo:hi], bank[b + i][:, 0:hi - lo], 40.0, None, ALU.min).then_inc(zc, 1)
                if h % 2 == 1 and h >= 3:
                    o_low(("osb", (h - 3) // 2), sq_h[:, (h - 3) // 2], sq_l[:, (h - 3) // 2], (h - 3) // 2)
                if h % 2 == 0 and h:
                    gate_logit(h // 2)
                for i, lo, hi in SB_A:
                    dve.wait_ge(zl, 3 * h + i + 1)
                    V.tensor_tensor(w[:, lo:hi], bank[b + i][:, 0:hi - lo], w[:, lo:hi], ALU.max).then_inc(zs, 1)
                if h == 0:
                    gate_logit(0)
                for i, lo, hi in SB_A:
                    dve.wait_ge(zh, 3 * h + i + 1)
                    V.tensor_tensor(sp_l[h % 2][:, lo:hi], w[:, lo:hi], sp_h[h % 2][:, lo:hi].bitcast(F32), ALU.subtract).then_inc(zlo, 1)
            gate_logit(GM_SB)
            o_low(("osb", PAIRS - 1), sq_h[:, PAIRS - 1], sq_l[:, PAIRS - 1], PAIRS - 1)

            for i in range(UNITS + 5):
                if i < UNITS:
                    p, br, g, r, run = unit(i)
                    n = P * (r + 1)
                    ps = result(dve, ("s", i))
                    if i % (UNITS // PAIRS) == 0:
                        dve.wait_ge(hank_in[p], 16)
                    if i >= 4:
                        result(dve, ("t", i - 4))
                    emptied(V.tensor_tensor_reduce(ns[i % 4][:, 0:n], ps[:, 0:n], hank[:, p, g, 0:n][:, ::-1], 1.0, 3.0e38,
                                                   ALU.add, ALU.min, nmin[:, i % 4:i % 4 + 1]), ("s", i))
                u = i - 1
                if 0 <= u < UNITS:
                    p, br, g, r, run = unit(u)
                    n = P * (r + 1)
                    dve.wait_ge(s_exp, u + 1)
                    V.reciprocal(rec[:, u % 4:u % 4 + 1], rsum[:, u % 4:u % 4 + 1]).then_inc(s_rec, 1)
                    dve.wait_ge(s_rec, u + 1)
                    V.tensor_scalar(ns[u % 4][:, 0:n], ns[u % 4][:, 0:n], rec[:, u % 4:u % 4 + 1],
                                    gate[:, r, g * HG + p, 2 - br:3 - br], ALU.mult, ALU.mult).then_inc(s_nrm, 1)
                if i % 10 == 3:
                    gate_logit(GM_SB + 1 + i // 10)
                if i >= 16 and i % 16 == 4:
                    p = i // 16 - 1
                    o_low(("ons", p), qn[0][:, p], qn[1][:, p], PAIRS + p)
            for i in range(GM_IN_ATT, 16):
                gate_logit(i)
            for n in range(KT):
                a, b = mx[2 * (n % 2)], mx[2 * (n % 2) + 1]
                dve.wait_ge(sig_done, 2 * n + 2)
                if n >= 2:
                    dve.wait_ge(m_lo, n - 1)
                for i, t in ((0, a), (1, b)):
                    ps = result(dve, (f"up{i}", n))
                    ins = V.tensor_tensor(t[:], ps[:], gate_tile(n + 8 * i), ALU.mult)
                    emptied(ins, (f"up{i}", n))
                stored(dve, ("up0", n))
                stored(dve, ("up1", n))
                V.tensor_tensor(a[:], a[:], b[:], ALU.add).then_inc(mxs, 1)
                dve.wait_ge(m_hi, n + 1)
                V.tensor_tensor(hl[:, n], a[:], hh[:, n].bitcast(F32), ALU.subtract).then_inc(m_lo, 1)
            dve.wait_ge(xres_in, 16)

            def add_sq(n, sq, acc, got, done):
                dve.wait_ge(got, n + 1)
                if n == 0:
                    V.tensor_copy(acc, sq).then_inc(done, 1)
                else:
                    dve.wait_ge(done, n)
                    V.tensor_tensor(acc, acc, sq, ALU.add).then_inc(done, 1)

            for n in range(KT):
                ps = result(dve, ("out", n))
                ins = V.tensor_tensor(x_res[:, n], ps[:], x_res[:, n], ALU.add)
                emptied(ins, ("out", n))
                add_sq(n, tmp[:, n % 2], mx[0][:], x_sq, x_ss)
                dve.wait_ge(h2hi, n + 1)
                V.scalar_tensor_tensor(out=h2l[:, n], in0=x_res[:, n], scalar=nrm[:, 1, n:n + 1], in1=h2h[:, n].bitcast(F32),
                                       op0=ALU.mult, op1=ALU.subtract).then_inc(h2lo, 1)
            dve.wait_ge(rs2, 1)
            def hidden_tile(name, n, nr, row, peeled=False):
                t = tmp[:, n % 2]
                ps = result(dve, name)
                if not (peeled and n < 2):
                    dve.wait_ge(r_lo, nr - 1)
                V.tensor_scalar(t, ps[:], 0.0, None, ALU.max).then_inc(r_pos, 1)
                dve.wait_ge(r_pos, nr + 1)
                emptied(V.tensor_tensor(t, ps[:], t, ALU.mult), name)
                stored(dve, name)
                V.tensor_tensor(t, t, rstd_b[:], ALU.mult).then_inc(r_sc, 1)
                dve.wait_ge(r_hi, nr + 1)
                V.tensor_tensor(r_l[:, row], t, r_h[:, row].bitcast(F32), ALU.subtract).then_inc(r_lo, 1)

            def add_product(name, n):
                ps = result(dve, name)
                emptied(V.tensor_tensor(x_res[:, n], ps[:], x_res[:, n], ALU.add), name)

            for n in range(8):
                hidden_tile(("ff", 0, n), n, n, n, peeled=True)
            with dve.Fori(0, QF - 1) as q:
                with dve.Fori(0, 2) as i:
                    for n in range(RING):
                        hidden_tile(ff_use(1, n, q, i), n, 8 + n + 8 * q + RING * i, (q + 1) % 2 * 8 + n + RING * i)
                with dve.Fori(0, 2) as i:
                    for n in range(RING):
                        add_product(ff_use(2, n, q, i), n + RING * i)
            for n in range(4):
                add_product(("ff", 7, n), n)
                add_sq(n, fin_sq[:, n % 2], fin_ss[:], y_sq, y_ss)
            def final_norm(t):
                c = HALF[t]
                dve.wait_ge(rs3, t + 1)
                for n in range(KT):
                    V.scalar_tensor_tensor(out=x_res[:, n, c], in0=x_res[:, n, c], scalar=nrm[:, 2, n:n + 1], in1=tmp[:, 0, c],
                                           op0=ALU.mult, op1=ALU.mult).then_inc(y_fin, 1)

            for t in range(2):
                c = HALF[t]
                for n in range(4):
                    ps = result(dve, ("end", t, n))
                    emptied(V.tensor_tensor(x_res[:, 4 + n, c], ps[:, c], x_res[:, 4 + n, c], ALU.add), ("end", t, n))
                    add_sq(4 + 4 * t + n, fin_sq[:, n % 2, c], fin_ss[:, c], y_sq, y_ss)
                    if t == 1 and n == 0:
                        final_norm(0)
            final_norm(1)

        @block.tensor
        def _(pe_):
            M = nc.tensor.matmul

            def three(out, lh, ll, rh, rl, start, stop, **kw):
                M(out, ll, rh, start=start, stop=False, **kw)
                M(out, lh, rl, start=False, stop=False, **kw)
                return M(out, lh, rh, start=False, stop=stop, **kw)

            def panel(p, name, xh, xl, first=0, last=24, ready=None, more=0, row=0, cols=slice(0, T)):
                s = p % RING
                b = bank[where(name)[0]]
                for m in range(first, last):
                    k, a = divmod(m, 3)
                    if m == 0:
                        claim(pe_, name)
                    if m == 0 and p == 0:
                        pe_.wait_ge(first_lo, 1)
                    if m == (12 if p == 0 else 0):
                        pe_.wait_ge(w_lo, p + 1 + more)
                    if ready and a == 0:
                        pe_.wait_ge(ready, k + 1)
                    lhs = (wlo if a == 0 else whi)[:, s, k, :]
                    ins = M(b[:, cols], lhs, (xl if a == 1 else xh)[:, row + k, cols], start=(m == 0), stop=(m == 23))
                    if m == 23:
                        filled(ins, name)

            def value_panels(p, names):
                pe_.wait_ge(w_lo, p + 2)
                s = p % RING
                for i, name in enumerate(names):
                    if name is None:
                        continue
                    claim(pe_, name)
                    b = bank[USE[name][0]]
                    for a in range(2):
                        r = 2 * i + a
                        for k in range(KT):
                            lh, ll = hh[:, k, P * r:P * r + P], hl[:, k, P * r:P * r + P]
                            o = b[:, 2 * P * a:2 * P * a + 2 * P]
                            ins = three(o, lh, ll, whi[:, s:s + 2, k, :], wlo[:, s:s + 2, k, :], k == 0, k == KT - 1)
                    filled(ins, name)

            panel(0, ("pan", 0), hh, hl, ready=h_lo)
            panel(1, ("pan", 1), hh, hl)
            value_panels(P_V, [("v", 0)])
            b = claim(pe_, "rms")
            pe_.wait_ge(set_done, 4)
            pe_.wait_ge(sqs_done, KT)
            filled(M(b[:], ones[:], sqs[:], start=True, stop=True), "rms")
            value_panels(P_V, [None, ("v", 1)])
            pe_.wait_ge(table_in, 16 * 3)
            for i in range(2):
                b = claim(pe_, f"vec{i}")
                filled(M(b[0:H, :], relx[:], oneh[:, T * i:T * i + T], start=True, stop=True), f"vec{i}")
            b = claim(pe_, "rcol")
            pe_.wait_ge(rst, 1)
            for r in range(RT):
                ins = nc.tensor.transpose(b[:, P * r:P * r + P], rstd_b[:, P * r:P * r + P], ident[:])
            filled(ins, "rcol")
            b = claim(pe_, "gn")
            pe_.wait_ge(gn_split, 2)
            for k in range(KT):
                ins = three(b[0:3 * H, :], gn_h[:, k, :], gn_l[:, k, :], hh[:, k, :], hl[:, k, :], k == 0, k == KT - 1)
            filled(ins, "gn")
            panel(4, ("pan", 4), hh, hl)
            b = claim(pe_, "gnT")
            stored(pe_, "gn")
            for r in range(RT):
                ins = nc.tensor.transpose(b[:, 3 * H * r:3 * H * r + 3 * H], gsb[:, P * r:P * r + P], ident[0:3 * H, 0:3 * H])
            filled(ins, "gnT")
            panel(5, ("pan", 5), hh, hl)
            b = claim(pe_, "dt")
            pe_.wait_ge(dt_in, 16)
            for h in range(H):
                ins = nc.tensor.transpose(b[:, 56 * h:56 * h + 55], dts[:, h, :], ident[0:55, 0:55])
            filled(ins, "dt")

            def hidden(i):
                b = claim(pe_, ("hid", i))
                pe_.wait_ge(bm_done, 2 + 2 * (i + 1))
                pe_.wait_ge(cmp_in, 16 * 7)
                for m in range(2):
                    for c in range(CI):
                        ins = M(b[:, 64 * m:64 * m + G * NC], w1s[i][:, c, P * m:P * m + P], bm[i][:, c, :], start=(c == 0), stop=(c == CI - 1))
                filled(ins, ("hid", i))

            hidden(0)
            panel(6, ("pan", 6), hh, hl)
            hidden(1)
            panel(7, ("pan", 7), hh, hl)
            panel(8, ("pan", 8), hh, hl)
            b = claim(pe_, "kcvc")
            for i in range(2):
                stored(pe_, ("hid", i))
            for m in range(2):
                M(b[:, 0:64], w2k[:, m].rearrange("p a d -> p (a d)"), hidTk[:, m].rearrange("p g c -> p (g c)"),
                  start=(m == 0), stop=(m == 1))
            for g in range(G):
                for m in range(2):
                    ins = M(b[:, 64 + 64 * g:128 + 64 * g],
                            hidTv[:, m, g].rearrange("p j c -> p (j c)"), w2v[:, m, :],
                            start=(m == 0), stop=(m == 1))
            filled(ins, "kcvc")
            panel(9, ("pan", 9), hh, hl)

            def cmp_scores(r):
                pe_.wait_ge(kc_split, 2)
                pe_.wait_ge(t_lo, 6)
                b = claim(pe_, ("cs", r))
                for h in range(H):
                    g, j = divmod(h, HG)
                    ins = M(b[:, 64 * h:64 * h + 64], qn[g][:, j, P * r:P * r + P], kc[:, g].rearrange("p a c -> p (a c)"),
                            start=True, stop=True)
                filled(ins, ("cs", r))

            def cmp_transpose(r):
                b = claim(pe_, ("ct", r))
                pe_.wait_ge(c_pready, [1, 2, 4, 6][r])
                for g in range(G):
                    ins = nc.tensor.transpose(b[:, P * g:P * g + P], c_g[:, r % 2, HG * g:HG * g + HG, :].rearrange("p j c -> p (j c)"), ident[:])
                if r >= 2:
                    ins = nc.tensor.transpose(b[0:2 * NB, 2 * P:3 * P], c_k[:].rearrange("p g n -> p (g n)"), ident[:])
                filled(ins, ("ct", r))

            value_panels(P_SV, [("sv", 0), ("sv", 1)])
            cmp_scores(0)
            value_panels(P_SV + 2, [("sv", 2), ("sv", 3)])
            cmp_scores(1)
            for i in range(8):
                panel(P_SQK + i, ("pan", P_SQK + i), hh, hl)
                if i in CMP_TRANSPOSE:
                    cmp_transpose(CMP_TRANSPOSE.index(i))
                if i in (1, 3):
                    cmp_scores(2 + i // 2)

            def gate_products(first, count):
                while count:
                    i, m = divmod(first, 24)
                    n = min(count, 24 - m)
                    panel(P_GM + i, ("gm", i), hh, hl, m, m + n)
                    first, count = first + n, count - n

            def logits(h):
                p, odd = divmod(h, 2)
                a, keys = GROUP[odd], sk[odd]
                queries = sq_odd[p % 2][:] if odd else sq_h[:, p]
                b = 3 * odd
                for i in range(3):
                    claim(pe_, ("z", h, i))
                pe_.wait_ge(t_lo, 6 + 2 * p + 2)
                pe_.wait_ge(q_twice, 3 * p + 3)
                for k in (0, 1, 3, 2):
                    o = bank[b + KOFF[k] // T][:, KOFF[k] % T:KOFF[k] % T + KLEN[k]]
                    kk = slice(P * k, P * k + P)
                    M(o, keys[:, p, kk], queries[:, P * k:T], start=(k != 3), stop=False, skip_group_check=True)
                    M(o, keys[a, p, kk], sq_l[a, p, P * k:T], start=False, stop=False, skip_group_check=True)
                    ins = M(o[:, 0:P], ident_bf[:], diag_bf[:], start=False, stop=False, skip_group_check=True)
                    if k != 1:
                        filled(ins, ("z", h, KOFF[k] // T))

            def stick_sums(h):
                b = 3 * (h % 2)
                pe_.wait_ge(zlo, 3 * h + 3)
                for k in range(RT):
                    for j in range(k, RT):
                        c = KOFF[k] % T + P * (j - k)
                        o = bank[b + KOFF[k] // T][:, c:c + KLEN[j]]
                        w = negtri if j == k else negones
                        for part in (sp_l, sp_h):
                            ins = M(o, w[:], part[h % 2][:, KOFF[j]:KOFF[j] + KLEN[j]], start=False, stop=False, skip_group_check=True)
                ins.then_inc(c_acc, 1)

            def stick_pv(h):
                p, half = divmod(h, 2)
                for i in range(3):
                    stored(pe_, ("z", h, i))
                if half == 0:
                    claim(pe_, ("osb", p))
                o = bank[USE[("osb", p)][0]]
                for k in range(RT):
                    ins = M(o[64 * half:64 * half + 64, P * k:T], sv[:, k, DH * h:DH * h + DH],
                            ew[h % 2][:, KOFF[k]:KOFF[k] + KLEN[k]], start=(k == 0), stop=(k == RT - 1), skip_group_check=True)
                if half == 1:
                    filled(ins, ("osb", p))
                else:
                    ins.then_inc(pv_sb, 1)

            pe_.wait_ge(cast_done, 5)
            stored(pe_, ("sv", 2))
            stored(pe_, ("sv", 3))
            logits(0)
            gate_done = 0
            for h in range(H):
                gate_products(gate_done, SB_BEFORE[h])
                gate_done += SB_BEFORE[h]
                if h + 1 < H:
                    logits(h + 1)
                if h:
                    stick_pv(h - 1)
                gate_products(gate_done, SB_BEHIND[h])
                gate_done += SB_BEHIND[h]
                stick_sums(h)
            def scores(u):
                p, br, g, r, run = unit(u)
                a, n = slice(64 * g, 64 * g + 64), P * (r + 1)
                b = bank[USE[("s", u)][0]]
                claim(pe_, ("s", u))
                masked = br == 1 and r >= 2
                M(b[:, 0:n], qn[g][:, p, P * r:P * r + P], (kn_h, kd1)[g][:, br, 0:n], start=True, stop=False)
                ins = M(b[:, 0:n], qn[g][a, p, P * r:P * r + P], kn_l[a, br, 0:n], start=False, stop=not masked)
                if masked:
                    stored(pe_, ("ct", r))
                    ins = M(b[:, 0:n], maskT[:, r - 2, :], blk_bf[:, g, 0:n], start=False, stop=True)
                filled(ins, ("s", u))

            pe_.wait_ge(k_twice, 3)
            scores(0)
            scores(1)
            stick_pv(H - 1)

            def turn(u):
                p, br, g, r, run = unit(u)
                b = bank[USE[("t", u)][0]]
                claim(pe_, ("t", u))
                pe_.wait_ge(s_nrm, u + 1)
                for k in range(r + 1):
                    ins = nc.tensor.transpose(b[:, P * k:P * k + P], ns[u % 4][:, P * k:P * k + P], ident[:])
                filled(ins, ("t", u))

            def sparse_pv(run):
                p, bg = divmod(run, 2 * G)
                br, g = divmod(bg, G)
                o = bank[USE[("ons", p)][0]]
                if bg == 0:
                    claim(pe_, ("ons", p))
                    stored(pe_, ("ct", RT - 2))
                    stored(pe_, ("ct", RT - 1))
                    for gg in range(G):
                        a = slice(32 * p, 32 * p + 32)
                        M(o[64 * gg:64 * gg + 64, :], vc[a, gg, :], pct[a, gg, :], start=True, stop=False, skip_group_check=True)
                stored(pe_, ("t", RT * run + RT - 2))
                stored(pe_, ("t", RT * run + RT - 1))
                for k in range(RT):
                    ins = M(o[64 * g:64 * g + 64, P * k:T], nv[:, k, 1 - br, 64 * g:64 * g + 64], pt[run % 2][:, k, P * k:T],
                            start=False, stop=(k == RT - 1), skip_group_check=True)
                if bg == 2 * G - 1:
                    filled(ins, ("ons", p))
                else:
                    ins.then_inc(s_pv, 1)

            for i in range(UNITS + 5):
                if i < UNITS:
                    if i > 1:
                        scores(i)
                    gate_products(gate_done, NS_PRODUCTS[i])
                    gate_done += NS_PRODUCTS[i]
                if 0 <= i - 2 < UNITS:
                    turn(i - 2)
                u = i - 4
                if 0 <= u < UNITS and u % 4 == 3:
                    sparse_pv(u // 4)
            gate_products(24 * GM_IN_ATT, 24 * (16 - GM_IN_ATT))

            stored(pe_, ("osb", PAIRS - 1))
            stored(pe_, ("ons", PAIRS - 1))
            with pe_.Fori(0, KT // RING) as i:
                for n in range(RING):
                    p = P_UP + n
                    s = p % RING
                    for m, (oh, ol) in enumerate((qn, (sq_h, sq_l))):
                        name = later_use((f"up{m}", n), i)
                        b = claim(pe_, name)
                        if m == 0:
                            pe_.wait_ge(w_lo, p + 1 + RING * i)
                        for k in range(PAIRS):
                            ins = three(b[:], whi[:, s, 4 * m + k, :], wlo[:, s, 4 * m + k, :], oh[:, k, :], ol[:, k, :], k == 0, k == PAIRS - 1)
                        filled(ins, name)
            for n in range(KT):
                panel(P_OUT + n, ("out", n), hh, hl, ready=None if n else m_lo)
            panel(P_FF, ("ff", 0, 0), h2h, h2l, ready=h2lo)
            b = claim(pe_, "rms2")
            pe_.wait_ge(x_ss, KT)
            filled(M(b[:], ones[:], mx[0][:], start=True, stop=True), "rms2")
            for n in range(1, 8):
                panel(P_FF + n, ("ff", 0, n), h2h, h2l)
            with pe_.Fori(0, QF - 1) as q:
                with pe_.Fori(0, 2) as i:
                    for n in range(RING):
                        panel(P_FF + 8 + n, ff_use(1, n, q, i), h2h, h2l, more=16 * q + RING * i)
                with pe_.Fori(0, 2) as i:
                    for n in range(RING):
                        if n == 0:
                            pe_.wait_ge(r_lo, 8 * q + 8)
                        panel(P_FF + 16 + n, ff_use(2, n, q, i), r_h, r_l, more=16 * q + RING * i, row=q % 2 * 8)
            pe_.wait_ge(r_lo, 8 * QF)
            for n in range(4):
                panel(P_FF + 56 + n, ("ff", 7, n), r_h, r_l, row=(QF - 1) % 2 * 8)

            def total(t):
                b = claim(pe_, ("rms3", t))
                pe_.wait_ge(y_ss, 8 + 4 * t)
                filled(M(b[:, HALF[t]], ones[:], fin_ss[:, HALF[t]], start=True, stop=True), ("rms3", t))

            for t in range(2):
                for n in range(4):
                    panel(NPANEL - 4 + n, ("end", t, n), r_h, r_l, row=(QF - 1) % 2 * 8, cols=HALF[t])
                    if t == 1 and n == 0:
                        total(0)
            total(1)


def bucket(n):
    exact = BUCKETS // 2
    if n < exact:
        return n
    return min(BUCKETS - 1, exact + int(math.log(n / exact) / math.log(128 / exact) * (BUCKETS - exact)))


def constants():
    onehot = np.zeros((BUCKETS + 1, 2 * T), np.float32)
    for y in range(2 * T):
        d = y - (T - 1)
        if d < 0:
            onehot[BUCKETS, y] = 1.0
        else:
            onehot[bucket(d), y] = -1.0
    cst = np.zeros((P, 1433), np.float32)
    i, j = np.arange(P)[:, None], np.arange(P)[None, :]
    cst[:, 0:P] = np.where(i >= j, -1.0, 0.0)
    cst[:, P:2 * P] = np.where(i >= j, -BIG, 0.0)
    for g in range(G):
        for n in range(NB):
            cst[NB * g + n, 2 * P + T * g + 64 * n:2 * P + T * g + 64 * n + 64] = 1.0
    cst[:, 1280:1408] = np.eye(P)
    for r in range(2):
        own = (P * (r + 2) + np.arange(P)) // 64
        n = np.arange(NB)[None, :]
        add = np.where((n == own[:, None]) | (n == 0), FORCE, np.where(n <= own[:, None], 0.0, -FORCE))
        cst[:, 1408 + NB * r:1408 + NB * r + NB] = add
    cst[:, 1424] = np.arange(P) >= CL - 1
    cst[:, 1425:1433] = np.arange(NB)
    return onehot, cst


def kernel(**inputs):
    import concourse.bacc as bacc
    from concourse.bass_utils import run_bass_kernel_spmd

    a = {k: np.ascontiguousarray(v) for k, v in inputs.items()}
    w_in = a["w_in"][0]
    order = np.concatenate([np.arange(64) + 64 * h for j in range(PAIRS) for h in (j, j + HG)])
    kv = 512

    def cols(m):
        n = m.shape[1] // P
        return m.reshape(KT, P, n, P).transpose(2, 1, 0, 3).reshape(n, P, KT * P)

    def kvc(i):
        return w_in[:, kv + P * i:kv + P * i + P]

    sb = w_in[:, 512 + 768 + 24:512 + 768 + 24 + 1536]
    gates = w_in[:, 512 + 768 + 24 + 1536:]
    up = np.stack([a["w_up_nsa"][0][order], a["w_up_sb"][0]])
    up = up.reshape(2, PAIRS, P, KT, P).transpose(3, 2, 0, 1, 4).reshape(KT, P, KT * P)
    ff1 = cols(a["w_ff1"][0])
    ff2 = [cols(a["w_ff2"][0][D * q:D * q + D]) for q in range(QF)]
    parts = [cols(kvc(0)), cols(kvc(1)), cols(kvc(3)), cols(kvc(5)), cols(kvc(2)), cols(kvc(4)),
             cols(w_in[:, 0:512][:, order]), cols(sb[:, 1024:1536])]
    for p in range(PAIRS):
        parts += [cols(sb[:, P * p:P * p + P]), cols(sb[:, 512 + P * p:512 + P * p + P])]
    parts += [cols(gates), up, cols(a["w_out"][0])]
    for which, q in FF_ORDER:
        parts.append(ff1[8 * q:8 * q + 8] if which == 1 else ff2[q])
    panels = np.concatenate(parts)
    assert panels.shape == (NPANEL, P, KT * P), panels.shape
    w_gn = w_in[:, 1280:1304].reshape(KT, P, 24).transpose(1, 0, 2)
    norms = np.stack([a["norm_attn"][0], a["norm_mlp"][0], a["norm_final"]]).reshape(3, KT, P).transpose(2, 0, 1)
    two = ("cmp_k", "cmp_v")
    pe = np.stack([a[c + "_pe"][0].reshape(CI, P) for c in two]).transpose(2, 0, 1)
    w1 = np.stack([a[c + "_w1"][0].reshape(CI, P, CM).transpose(1, 0, 2) for c in two])
    b1 = np.stack([a[c + "_b1"][0].reshape(2, P).T for c in two]).transpose(1, 0, 2)
    w2 = np.stack([a[c + "_w2"][0].reshape(2, P, DH).transpose(1, 0, 2) for c in two])
    xT = a["x"][0].T.reshape(KT, P, T).transpose(1, 0, 2)
    onehot, cst = constants()
    arrays = {"xT": xT, "panels": panels, "w_gn": w_gn, "norms": norms, "rel_bias": a["rel_bias"], "pe": pe,
              "w1": w1, "b1": b1, "w2": w2, "onehot": onehot, "cst": cst}
    arrays = {"in_" + k: np.ascontiguousarray(v) for k, v in arrays.items()}
    nc = bacc.Bacc("TRN2", target_bir_lowering=False, num_devices=1)
    args = [nc.dram_tensor(k, v.shape, mybir.dt.from_np(v.dtype), kind="ExternalInput").ap() for k, v in arrays.items()]
    args.append(nc.dram_tensor("out_0_dram", (P, KT, T), F32, kind="ExternalOutput").ap())
    block_kernel(nc, *args)
    r = run_bass_kernel_spmd(nc, [arrays], core_ids=[0])
    y = r.results[0]["out_0_dram"]
    return np.ascontiguousarray(y.transpose(1, 0, 2).reshape(D, T).T)[None]
```
